# Optimizing a Trainium2 kernel written in Bass

```python
import math
import jax, jax.numpy as jnp
from jax import lax
import numpy as np
import jax
import jax.numpy as jnp

D_MODEL = 1024
BATCH = 1
SEQ = 256
DEPTH = 2

BRANCH_WIDTH = 512
N_BRANCHES = 3
SWA_Q_HEADS = 8
SWA_KV_HEADS = 2
SWA_GROUP = SWA_Q_HEADS // SWA_KV_HEADS
SWA_HEAD_DIM = BRANCH_WIDTH // SWA_Q_HEADS
WINDOW = 128
N_BUCKETS = 32
MAX_DISTANCE = 128
CONV_CHANNELS = BRANCH_WIDTH
CONV_WIDTH = 31
MLA_HEADS = 8
MLA_Q_RANK = 256
MLA_KV_RANK = 128
MLA_NOPE_DIM = 64
MLA_ROPE_DIM = 32
MLA_V_DIM = BRANCH_WIDTH // MLA_HEADS
ROPE_THETA = 10000.0
Q_BLOCK = 128
D_FF = 4 * D_MODEL
EPS = 1e-6
NEG_INF = -1e30

IN_SPLIT_SIZES = (
    SWA_Q_HEADS * SWA_HEAD_DIM,
    SWA_KV_HEADS * SWA_HEAD_DIM,
    SWA_KV_HEADS * SWA_HEAD_DIM,
    2 * CONV_CHANNELS,
    MLA_Q_RANK,
    MLA_KV_RANK,
    MLA_ROPE_DIM,
    N_BRANCHES * D_MODEL,
)
IN_COLS = sum(IN_SPLIT_SIZES)
IN_SPLIT_POINTS = tuple(sum(IN_SPLIT_SIZES[: i + 1]) for i in range(len(IN_SPLIT_SIZES) - 1))


def rms_norm(x, g):
    xf = x.astype(jnp.float32)
    y = xf * lax.rsqrt(jnp.mean(xf * xf, axis=-1, keepdims=True) + EPS)
    return (y * g.astype(jnp.float32)).astype(x.dtype)

def layer_norm(x, g, b):
    xf = x.astype(jnp.float32)
    mu = jnp.mean(xf, axis=-1, keepdims=True)
    var = jnp.mean(jnp.square(xf - mu), axis=-1, keepdims=True)
    y = (xf - mu) * lax.rsqrt(var + EPS) * g.astype(jnp.float32) + b.astype(jnp.float32)
    return y.astype(x.dtype)

def t5_bucket(rel):
    n = jnp.maximum(rel, 0)
    max_exact = N_BUCKETS // 2
    nf = jnp.maximum(n, max_exact).astype(jnp.float32)
    large = max_exact + (jnp.log(nf / max_exact) / math.log(MAX_DISTANCE / max_exact)
                         * (N_BUCKETS - max_exact)).astype(jnp.int32)
    return jnp.where(n < max_exact, n, jnp.minimum(large, N_BUCKETS - 1))

def band_frames(t):
    b, s = t.shape[:2]
    blocks = t.reshape((b, s // WINDOW, WINDOW) + t.shape[2:])
    prev = jnp.concatenate([jnp.zeros_like(blocks[:, :1]), blocks[:, :-1]], axis=1)
    return jnp.concatenate([prev, blocks], axis=2)

def swa_bias_and_mask(positions, rel_bias):
    b, s = positions.shape
    nb = s // WINDOW
    pq = positions.reshape(b, nb, WINDOW)
    pk = band_frames(positions)
    bucket = t5_bucket(pq[..., :, None] - pk[..., None, :])
    bias = rel_bias[bucket].astype(jnp.float32).reshape(b, nb, WINDOW, 2 * WINDOW, SWA_KV_HEADS, SWA_GROUP)
    qi = WINDOW + jnp.arange(WINDOW)[:, None]
    ki = jnp.arange(2 * WINDOW)[None, :]
    in_band = (ki <= qi) & (qi - ki < WINDOW)
    has_prev = (jnp.arange(nb) > 0)[:, None, None] | (ki >= WINDOW)[None]
    mask = in_band[None] & has_prev
    return bias, mask[None, :, :, :, None, None]

def swa_attention(q, k, v, sinks, bias, mask):
    b, s = q.shape[:2]
    nb = s // WINDOW
    qb = q.reshape(b, nb, WINDOW, SWA_KV_HEADS, SWA_GROUP, SWA_HEAD_DIM)
    kk = band_frames(k.reshape(b, s, SWA_KV_HEADS, SWA_HEAD_DIM))
    vv = band_frames(v.reshape(b, s, SWA_KV_HEADS, SWA_HEAD_DIM))
    scores = jnp.einsum('bnqhgd,bnkhd->bnqkhg', qb, kk).astype(jnp.float32) * (SWA_HEAD_DIM ** -0.5) + bias
    scores = jnp.where(mask, scores, NEG_INF)
    sink = sinks.astype(jnp.float32).reshape(SWA_KV_HEADS, SWA_GROUP)
    m = jnp.maximum(scores.max(axis=3, keepdims=True), sink)
    p = jnp.exp(scores - m)
    p = p / (p.sum(axis=3, keepdims=True) + jnp.exp(sink - m))
    out = jnp.einsum('bnqkhg,bnkhd->bnqhgd', p.astype(vv.dtype), vv)
    return out.reshape(b, s, SWA_Q_HEADS * SWA_HEAD_DIM)

def conformer_conv(u_glu, w_dw, b_dw, g_ln, b_ln):
    a, gate = jnp.split(u_glu, 2, axis=-1)
    u = a * jax.nn.sigmoid(gate)
    u = lax.conv_general_dilated(u, w_dw, window_strides=(1,), padding=[(CONV_WIDTH - 1, 0)],
                                 dimension_numbers=('NWC', 'WIO', 'NWC'),
                                 feature_group_count=CONV_CHANNELS) + b_dw
    return jax.nn.silu(layer_norm(u, g_ln, b_ln))

def rope(x, positions):
    d = x.shape[-1]
    half = d // 2
    freqs = jnp.exp(-math.log(ROPE_THETA) * jnp.arange(half, dtype=jnp.float32) / half)
    ang = positions.astype(jnp.float32)[..., None] * freqs
    cos = jnp.cos(ang)[:, :, None, :]
    sin = jnp.sin(ang)[:, :, None, :]
    x1 = x[..., :half].astype(jnp.float32)
    x2 = x[..., half:].astype(jnp.float32)
    return jnp.concatenate([x1 * cos - x2 * sin, x2 * cos + x1 * sin], axis=-1).astype(x.dtype)

def mla_attention(cq, ckv, kpe_raw, positions, g_qn, w_uq, g_kvn, w_ukv):
    b, s = cq.shape[:2]
    q = (rms_norm(cq, g_qn) @ w_uq).reshape(b, s, MLA_HEADS, MLA_NOPE_DIM + MLA_ROPE_DIM)
    q_nope = q[..., :MLA_NOPE_DIM]
    q_pe = rope(q[..., MLA_NOPE_DIM:], positions)
    kv = (rms_norm(ckv, g_kvn) @ w_ukv).reshape(b, s, MLA_HEADS, MLA_NOPE_DIM + MLA_V_DIM)
    k_nope = kv[..., :MLA_NOPE_DIM]
    v = kv[..., MLA_NOPE_DIM:]
    k_pe = rope(kpe_raw[:, :, None, :], positions)[:, :, 0]
    scale = (MLA_NOPE_DIM + MLA_ROPE_DIM) ** -0.5
    nb = s // Q_BLOCK
    key_idx = jnp.arange(s)

    def to_blocks(t):
        return jnp.moveaxis(t.reshape((b, nb, Q_BLOCK) + t.shape[2:]), 1, 0)

    def attend_block(args):
        qn, qp, blk = args
        sc = (jnp.einsum('bqhd,bkhd->bhqk', qn, k_nope)
              + jnp.einsum('bqhd,bkd->bhqk', qp, k_pe)).astype(jnp.float32) * scale
        q_idx = blk * Q_BLOCK + jnp.arange(Q_BLOCK)
        sc = jnp.where(key_idx[None, :] <= q_idx[:, None], sc, NEG_INF)
        p = jax.nn.softmax(sc, axis=-1)
        return jnp.einsum('bhqk,bkhd->bqhd', p.astype(v.dtype), v)

    out = lax.map(attend_block, (to_blocks(q_nope), to_blocks(q_pe), jnp.arange(nb)))
    return jnp.moveaxis(out, 0, 1).reshape(b, s, MLA_HEADS * MLA_V_DIM)

def first_inputs(seed: int = 0) -> dict:
    key = jax.random.key(seed)
    ks = jax.random.split(key, 20)
    f32 = jnp.float32

    def nrm(k, shape, scale):
        return jax.random.normal(k, shape, f32) * scale

    def gain(k, shape):
        return 1.0 + 0.05 * jax.random.normal(k, shape, f32)

    return {
        "x": nrm(ks[0], (BATCH, SEQ, D_MODEL), 1.0),
        "positions": jnp.broadcast_to(jnp.arange(SEQ, dtype=jnp.int32), (BATCH, SEQ)),
        "rel_bias": nrm(ks[1], (N_BUCKETS, SWA_Q_HEADS), 0.5),
        "g_final": gain(ks[2], (D_MODEL,)),
        "g_mix": gain(ks[3], (DEPTH, D_MODEL)),
        "w_in": nrm(ks[4], (DEPTH, D_MODEL, IN_COLS), D_MODEL ** -0.5),
        "swa_sinks": nrm(ks[5], (DEPTH, SWA_Q_HEADS), 0.5),
        "g_q_norm": gain(ks[6], (DEPTH, MLA_Q_RANK)),
        "w_q_up": nrm(ks[7], (DEPTH, MLA_Q_RANK, MLA_HEADS * (MLA_NOPE_DIM + MLA_ROPE_DIM)), MLA_Q_RANK ** -0.5),
        "g_kv_norm": gain(ks[8], (DEPTH, MLA_KV_RANK)),
        "w_kv_up": nrm(ks[9], (DEPTH, MLA_KV_RANK, MLA_HEADS * (MLA_NOPE_DIM + MLA_V_DIM)), MLA_KV_RANK ** -0.5),
        "w_dw": nrm(ks[10], (DEPTH, CONV_WIDTH, 1, CONV_CHANNELS), CONV_WIDTH ** -0.5),
        "b_dw": nrm(ks[11], (DEPTH, CONV_CHANNELS), 0.02),
        "g_conv_ln": gain(ks[12], (DEPTH, CONV_CHANNELS)),
        "b_conv_ln": nrm(ks[13], (DEPTH, CONV_CHANNELS), 0.02),
        "w_branch": nrm(ks[14], (DEPTH, N_BRANCHES, BRANCH_WIDTH, D_MODEL), BRANCH_WIDTH ** -0.5),
        "w_out": nrm(ks[15], (DEPTH, D_MODEL, D_MODEL), D_MODEL ** -0.5),
        "g_mlp": gain(ks[16], (DEPTH, D_MODEL)),
        "w_up": nrm(ks[17], (DEPTH, D_MODEL, D_FF), D_MODEL ** -0.5),
        "w_down": nrm(ks[18], (DEPTH, D_FF, D_MODEL), D_FF ** -0.5),
    }

def first_block(x, positions, rel_bias, g_final, g_mix, w_in, swa_sinks, g_q_norm, w_q_up,
              g_kv_norm, w_kv_up, w_dw, b_dw, g_conv_ln, b_conv_ln, w_branch, w_out,
              g_mlp, w_up, w_down):
    b, s, _ = x.shape
    swa_bias, swa_mask = swa_bias_and_mask(positions, rel_bias)
    for l in range(DEPTH):
        h = rms_norm(x, g_mix[l])
        q_a, k_a, v_a, u_b, cq_c, ckv_c, kpe_c, gate_logits = jnp.split(h @ w_in[l], IN_SPLIT_POINTS, axis=-1)
        y_a = swa_attention(q_a, k_a, v_a, swa_sinks[l], swa_bias, swa_mask)
        y_b = conformer_conv(u_b, w_dw[l], b_dw[l], g_conv_ln[l], b_conv_ln[l])
        y_c = mla_attention(cq_c, ckv_c, kpe_c, positions, g_q_norm[l], w_q_up[l],
                            g_kv_norm[l], w_kv_up[l])
        branches = jnp.einsum('bsnc,ncd->bsnd', jnp.stack([y_a, y_b, y_c], axis=2), w_branch[l])
        gates = jax.nn.sigmoid(gate_logits.reshape(b, s, N_BRANCHES, D_MODEL))
        x = x + jnp.einsum('bsnd,bsnd->bsd', gates, branches) @ w_out[l]
        h = rms_norm(x, g_mlp[l])
        x = x + jnp.square(jax.nn.relu(h @ w_up[l])) @ w_down[l]
    return rms_norm(x, g_final)


GRID_W = 64
CTX_LEN = 256

RET_HEADS = 4
RET_DK = 128
RET_DV = 128
RET_CHUNK = 128
NA_HEADS = 8
NA_DH = 64
NA_WIN_R = 8
NA_WIN_C = 16
NA_QB = NA_WIN_C
NA_KBW = 2 * NA_WIN_C
POOL_SIZES = (2, 4, 8, 16)
POOL_GROUP = D_MODEL // len(POOL_SIZES)
MOE_GROUPS = 4
MOE_PER_GROUP = 8
MOE_EXPERTS = MOE_GROUPS * MOE_PER_GROUP
MOE_HIDDEN = D_MODEL // 2
MOE_TOPK = 2

ROPE_BASE = 10000.0
LN_EPS = 1e-5
N_MOD = 6
DEEPNORM_ALPHA = (2 * DEPTH) ** 0.25
DEEPNORM_BETA = (8 * DEPTH) ** -0.25

RET_QKW = RET_HEADS * RET_DK
RET_VW = RET_HEADS * RET_DV
NA_W = NA_HEADS * NA_DH
MIX_W = RET_VW + NA_W
OFF_RK = 0
OFF_RV = OFF_RK + RET_QKW
OFF_NK = OFF_RV + RET_VW
OFF_NV = OFF_NK + NA_W
KV_COLS = OFF_NV + NA_W
OFF_RQ = KV_COLS
OFF_RG = OFF_RQ + RET_QKW
OFF_NQ = OFF_RG + RET_VW
IN_COLS_2 = OFF_NQ + NA_W


def _layer_norm(x, g, b):
    xf = x.astype(jnp.float32)
    mu = jnp.mean(xf, -1, keepdims=True)
    var = jnp.mean(jnp.square(xf - mu), -1, keepdims=True)
    return ((xf - mu) * lax.rsqrt(var + LN_EPS)).astype(x.dtype) * g + b

def _post_norm(h, y, g, b):
    return _layer_norm(DEEPNORM_ALPHA * h + y, g, b)

def _modulation(cvec, w_mod, b_mod):
    m = jax.nn.silu(cvec) @ w_mod + b_mod
    return [p[..., None, :] for p in jnp.split(m, N_MOD, axis=-1)]

def _modulate(h, shift, scale):
    return h * (1 + scale) + shift

def _split_heads(t, n_heads):
    b, n, _ = t.shape
    return jnp.transpose(t.reshape(b, n, n_heads, -1), (0, 2, 1, 3))

def _merge_heads(t):
    b, h, n, d = t.shape
    return jnp.transpose(t, (0, 2, 1, 3)).reshape(b, n, h * d)

def _axial_rope(n_tokens, head_dim):
    t = jnp.arange(n_tokens)
    rows = (t // GRID_W).astype(jnp.float32)
    cols = (t % GRID_W).astype(jnp.float32)
    n_freq = head_dim // 4
    inv_freq = ROPE_BASE ** (-jnp.arange(n_freq, dtype=jnp.float32) / n_freq)
    ang = jnp.concatenate([rows[:, None] * inv_freq, cols[:, None] * inv_freq], axis=-1)
    return jnp.cos(ang), jnp.sin(ang)

def _apply_rope(x, cos, sin):
    half = x.shape[-1] // 2
    x1, x2 = x[..., :half], x[..., half:]
    cos = cos.astype(x.dtype)
    sin = sin.astype(x.dtype)
    return jnp.concatenate([x1 * cos - x2 * sin, x1 * sin + x2 * cos], axis=-1)

def _retention_chunked(q, k, v, log_gamma, s0):
    b, h, n, _ = q.shape
    dv = v.shape[-1]
    nc = n // RET_CHUNK
    idx = jnp.arange(RET_CHUNK, dtype=jnp.float32)
    lg = log_gamma[:, None]
    diff = idx[:, None] - idx[None, :]
    intra = jnp.where(diff >= 0, jnp.exp(lg[..., None] * jnp.maximum(diff, 0.0)), 0.0)
    q_dec = jnp.exp(lg * (idx + 1.0))[..., None]
    k_dec = jnp.exp(lg * (RET_CHUNK - 1.0 - idx))[..., None]
    chunk_dec = jnp.exp(log_gamma * RET_CHUNK)[:, None, None]

    def to_chunks(t):
        return jnp.moveaxis(t.astype(jnp.float32).reshape(b, h, nc, RET_CHUNK, t.shape[-1]), 2, 0)

    def step(state, blk):
        qi, ki, vi = blk
        att = jnp.einsum('bhid,bhjd->bhij', qi, ki) * intra
        o = (jnp.einsum('bhij,bhje->bhie', att, vi)
             + jnp.einsum('bhid,bhde->bhie', qi, state) * q_dec)
        state = state * chunk_dec + jnp.einsum('bhjd,bhje->bhde', ki * k_dec, vi)
        return state, o

    state, o = lax.scan(step, s0, (to_chunks(q), to_chunks(k), to_chunks(v)))
    return jnp.moveaxis(o, 0, 2).reshape(b, h, n, dv), state

def _bidir_retention(q, k, v, log_gamma2, s0_fwd, s0_bwd):
    o_f, s_f = _retention_chunked(q, k, v, log_gamma2[0], s0_fwd)
    flip = lambda t: jnp.flip(t, axis=2)
    o_b, s_b = _retention_chunked(flip(q), flip(k), flip(v), log_gamma2[1], s0_bwd)
    return o_f + flip(o_b), s_f, s_b

def _retention_final_states(k, v, log_gamma2):
    n = k.shape[2]
    pos = jnp.arange(n, dtype=jnp.float32)
    w_f = jnp.exp(log_gamma2[0][:, None] * (n - 1.0 - pos))
    w_b = jnp.exp(log_gamma2[1][:, None] * pos)
    kf = k.astype(jnp.float32)
    vf = v.astype(jnp.float32)
    s_f = jnp.einsum('bhld,hl,bhle->bhde', kf, w_f, vf)
    s_b = jnp.einsum('bhld,hl,bhle->bhde', kf, w_b, vf)
    return s_f, s_b

def _head_group_norm(o):
    mu = jnp.mean(o, -1, keepdims=True)
    var = jnp.mean(jnp.square(o - mu), -1, keepdims=True)
    return (o - mu) * lax.rsqrt(var + LN_EPS)

def _neighbourhood_attention(q, k, v, k_ctx, v_ctx, rpb):
    b, h, n, d = q.shape
    rows = n // GRID_W
    wr = min(NA_WIN_R, rows)
    ncb = GRID_W // NA_QB
    qcol = np.arange(ncb)[:, None] * NA_QB + np.arange(NA_QB)[None, :]
    kstart = np.clip(np.arange(ncb) * NA_QB - NA_WIN_C // 2, 0, GRID_W - NA_KBW)
    kcol = kstart[:, None] + np.arange(NA_KBW)[None, :]
    wstart = np.clip(qcol - NA_WIN_C // 2, 0, GRID_W - NA_WIN_C)[..., None]
    col_ok = (kcol[:, None, :] >= wstart) & (kcol[:, None, :] < wstart + NA_WIN_C)
    col_bias_idx = np.clip(kcol[:, None, :] - qcol[..., None] + NA_WIN_C - 1, 0, 2 * NA_WIN_C - 2)
    qg = (q * NA_DH ** -0.5).reshape(b, h, rows, GRID_W, d)
    kg = k.reshape(b, h, rows, GRID_W, d)
    vg = v.reshape(b, h, rows, GRID_W, d)
    n_win = wr * NA_KBW

    def row_block(r):
        r0 = jnp.clip(r - wr // 2, 0, rows - wr)
        k_blk = lax.dynamic_slice_in_dim(kg, r0, wr, axis=2)[:, :, :, kcol]
        v_blk = lax.dynamic_slice_in_dim(vg, r0, wr, axis=2)[:, :, :, kcol]
        q_r = lax.dynamic_index_in_dim(qg, r, axis=2, keepdims=False).reshape(b, h, ncb, NA_QB, d)
        row_bias_idx = r0 + jnp.arange(wr) - r + NA_WIN_R - 1
        bias = rpb[:, row_bias_idx[:, None, None, None], col_bias_idx[None]]
        s_win = jnp.einsum('bhcqd,bhrckd->bhcqrk', q_r, k_blk).astype(jnp.float32)
        s_win = s_win + jnp.transpose(bias, (0, 2, 3, 1, 4)).astype(jnp.float32)
        s_win = jnp.where(col_ok[:, :, None, :], s_win, -jnp.inf)
        s_ctx = jnp.einsum('bhcqd,bhld->bhcql', q_r, k_ctx).astype(jnp.float32)
        logits = jnp.concatenate([s_win.reshape(b, h, ncb, NA_QB, n_win), s_ctx], axis=-1)
        p = jax.nn.softmax(logits, axis=-1).astype(v.dtype)
        p_win = p[..., :n_win].reshape(b, h, ncb, NA_QB, wr, NA_KBW)
        o = (jnp.einsum('bhcqrk,bhrckd->bhcqd', p_win, v_blk)
             + jnp.einsum('bhcql,bhld->bhcqd', p[..., n_win:], v_ctx))
        return o.reshape(b, h, GRID_W, d)

    o = lax.map(row_block, jnp.arange(rows))
    return jnp.transpose(o, (1, 2, 0, 3, 4)).reshape(b, h, n, d)

def _context_attention(q, k, v):
    s = jnp.einsum('bhqd,bhkd->bhqk', q, k).astype(jnp.float32) * NA_DH ** -0.5
    p = jax.nn.softmax(s, axis=-1).astype(v.dtype)
    return jnp.einsum('bhqk,bhkd->bhqd', p, v)

def _mixer_retention_na(h, hc, w_in, w_out, log_decay, rpb, update_ctx):
    b, n, _ = h.shape
    dtype = h.dtype
    log_gamma2 = jnp.log1p(-jnp.exp(log_decay.astype(jnp.float32)))
    cols = lambda t, off, width: t[..., off:off + width]
    p = h @ w_in
    pc = hc @ (w_in if update_ctx else w_in[:, :KV_COLS])
    rk_c = _split_heads(cols(pc, OFF_RK, RET_QKW), RET_HEADS)
    rv_c = _split_heads(cols(pc, OFF_RV, RET_VW), RET_HEADS)
    nk_c = _split_heads(cols(pc, OFF_NK, NA_W), NA_HEADS)
    nv_c = _split_heads(cols(pc, OFF_NV, NA_W), NA_HEADS)
    cos, sin = _axial_rope(n, RET_DK)
    rq = _apply_rope(_split_heads(cols(p, OFF_RQ, RET_QKW), RET_HEADS), cos, sin) * RET_DK ** -0.5
    rk = _apply_rope(_split_heads(cols(p, OFF_RK, RET_QKW), RET_HEADS), cos, sin)
    rv = _split_heads(cols(p, OFF_RV, RET_VW), RET_HEADS)
    rg = cols(p, OFF_RG, RET_VW)
    nq = _split_heads(cols(p, OFF_NQ, NA_W), NA_HEADS)
    nk = _split_heads(cols(p, OFF_NK, NA_W), NA_HEADS)
    nv = _split_heads(cols(p, OFF_NV, NA_W), NA_HEADS)
    if update_ctx:
        rq_c = _split_heads(cols(pc, OFF_RQ, RET_QKW), RET_HEADS) * RET_DK ** -0.5
        zeros = jnp.zeros((b, RET_HEADS, RET_DK, RET_DV), jnp.float32)
        o_ret_c, s_f, s_b = _bidir_retention(rq_c, rk_c, rv_c, log_gamma2, zeros, zeros)
    else:
        s_f, s_b = _retention_final_states(rk_c, rv_c, log_gamma2)
    o_ret, _, _ = _bidir_retention(rq, rk, rv, log_gamma2, s_f, s_b)
    y_ret = jax.nn.silu(rg) * _merge_heads(_head_group_norm(o_ret)).astype(dtype)
    y_na = _merge_heads(_neighbourhood_attention(nq, nk, nv, nk_c, nv_c, rpb))
    y = jnp.concatenate([y_ret, y_na], axis=-1) @ w_out
    if not update_ctx:
        return y, None
    rg_c = cols(pc, OFF_RG, RET_VW)
    nq_c = _split_heads(cols(pc, OFF_NQ, NA_W), NA_HEADS)
    y_ret_c = jax.nn.silu(rg_c) * _merge_heads(_head_group_norm(o_ret_c)).astype(dtype)
    y_na_c = _merge_heads(_context_attention(nq_c, nk_c, nv_c))
    yc = jnp.concatenate([y_ret_c, y_na_c], axis=-1) @ w_out
    return y, yc

def _pool_mixer(h, pool_w, pool_scale):
    b, n, d = h.shape
    hf = h.astype(jnp.float32).reshape(b, n, len(POOL_SIZES), POOL_GROUP)
    csum = jnp.pad(jnp.cumsum(hf, axis=1), ((0, 0), (1, 0), (0, 0), (0, 0)))
    pos = jnp.arange(n)
    outs = []
    for g, w in enumerate(POOL_SIZES):
        lo = jnp.clip(pos - w // 2, 0, n)
        hi = jnp.clip(pos + (w - w // 2), 0, n)
        cg = csum[:, :, g]
        mean = (cg[:, hi] - cg[:, lo]) / (hi - lo).astype(jnp.float32)[None, :, None]
        outs.append(mean - hf[:, :, g])
    z = jnp.stack(outs, axis=2).astype(h.dtype)
    y = jnp.einsum('bngc,gce->bnge', z, pool_w).reshape(b, n, d)
    return y * pool_scale

def _hier_moe(h, w_r1, b_r1, w_r2, b_r2, w_gate, w_up, w_down):
    b, n, d = h.shape
    t = h.reshape(b * n, d)
    logit_g = (t @ w_r1).astype(jnp.float32) + b_r1.astype(jnp.float32)
    grp = jnp.argmax(logit_g, axis=-1)
    gate_g = jnp.take_along_axis(jax.nn.softmax(logit_g, axis=-1), grp[:, None], axis=-1)
    logit_e = jnp.einsum('td,gde->tge', t, w_r2).astype(jnp.float32) + b_r2.astype(jnp.float32)
    logit_e = jnp.take_along_axis(logit_e, grp[:, None, None], axis=1)[:, 0]
    top_v, top_i = lax.top_k(logit_e, MOE_TOPK)
    w_sel = jax.nn.softmax(top_v, axis=-1) * gate_g
    eid = grp[:, None] * MOE_PER_GROUP + top_i
    combine = jnp.einsum('tk,tke->te', w_sel, jax.nn.one_hot(eid, MOE_EXPERTS, dtype=jnp.float32))

    def expert_step(acc, xs):
        wg, wu, wd, gcol = xs
        y = (jax.nn.silu(t @ wg) * (t @ wu)) @ wd
        return acc + y.astype(jnp.float32) * gcol[:, None], None

    acc, _ = lax.scan(expert_step, jnp.zeros((b * n, d), jnp.float32),
                      (w_gate, w_up, w_down, combine.T))
    return acc.astype(h.dtype).reshape(b, n, d)

def second_inputs(seed: int = 0) -> dict:
    key = jax.random.key(seed)
    ks = jax.random.split(key, 21)
    f32 = jnp.float32

    def nrm(k, shape, scale):
        return jax.random.normal(k, shape, f32) * scale

    n_ab = (DEPTH + 1) // 2
    n_pool = DEPTH // 2
    base_log_decay = -(5.0 + jnp.arange(RET_HEADS, dtype=f32)) * jnp.log(2.0)
    return {
        'x': nrm(ks[0], (BATCH, SEQ, D_MODEL), 1.0),
        'c': nrm(ks[1], (BATCH, D_MODEL), 1.0),
        'ctx': nrm(ks[2], (BATCH, CTX_LEN, D_MODEL), 1.0),
        'c_ctx': nrm(ks[3], (D_MODEL,), 1.0),
        'w_mod': nrm(ks[4], (DEPTH, D_MODEL, N_MOD * D_MODEL), 0.5 * D_MODEL ** -0.5),
        'b_mod': nrm(ks[5], (DEPTH, N_MOD * D_MODEL), 0.02),
        'ln_g': 1.0 + nrm(ks[6], (DEPTH, 2, D_MODEL), 0.02),
        'ln_b': nrm(ks[7], (DEPTH, 2, D_MODEL), 0.02),
        'ab_w_in': nrm(ks[8], (n_ab, D_MODEL, IN_COLS_2), D_MODEL ** -0.5),
        'ab_w_out': nrm(ks[9], (n_ab, MIX_W, D_MODEL), DEEPNORM_BETA * MIX_W ** -0.5),
        'ab_log_decay': base_log_decay + nrm(ks[10], (n_ab, 2, RET_HEADS), 0.05),
        'ab_rpb': nrm(ks[11], (n_ab, NA_HEADS, 2 * NA_WIN_R - 1, 2 * NA_WIN_C - 1), 0.1),
        'pool_w': nrm(ks[12], (n_pool, len(POOL_SIZES), POOL_GROUP, POOL_GROUP), DEEPNORM_BETA * POOL_GROUP ** -0.5),
        'pool_scale': 1.0 + nrm(ks[13], (n_pool, D_MODEL), 0.1),
        'moe_w_r1': nrm(ks[14], (DEPTH, D_MODEL, MOE_GROUPS), D_MODEL ** -0.5),
        'moe_b_r1': nrm(ks[15], (DEPTH, MOE_GROUPS), 0.01),
        'moe_w_r2': nrm(ks[16], (DEPTH, MOE_GROUPS, D_MODEL, MOE_PER_GROUP), D_MODEL ** -0.5),
        'moe_b_r2': nrm(ks[17], (DEPTH, MOE_GROUPS, MOE_PER_GROUP), 0.01),
        'moe_w_gate': nrm(ks[18], (DEPTH, MOE_EXPERTS, D_MODEL, MOE_HIDDEN), D_MODEL ** -0.5),
        'moe_w_up': nrm(ks[19], (DEPTH, MOE_EXPERTS, D_MODEL, MOE_HIDDEN), D_MODEL ** -0.5),
        'moe_w_down': nrm(ks[20], (DEPTH, MOE_EXPERTS, MOE_HIDDEN, D_MODEL), DEEPNORM_BETA * MOE_HIDDEN ** -0.5),
    }

def second_block(x, c, ctx, c_ctx, w_mod, b_mod, ln_g, ln_b, ab_w_in, ab_w_out, ab_log_decay, ab_rpb,
              pool_w, pool_scale, moe_w_r1, moe_b_r1, moe_w_r2, moe_b_r2, moe_w_gate, moe_w_up, moe_w_down):
    h, hc = x, ctx
    for i in range(DEPTH):
        j = i // 2
        carry_ctx = any(later % 2 == 0 for later in range(i + 1, DEPTH))
        moe_p = (moe_w_r1[i], moe_b_r1[i], moe_w_r2[i], moe_b_r2[i], moe_w_gate[i], moe_w_up[i], moe_w_down[i])
        m = _modulation(c, w_mod[i], b_mod[i])
        if i % 2 == 0 or carry_ctx:
            mc = _modulation(c_ctx, w_mod[i], b_mod[i])
        if i % 2 == 0:
            y, yc = _mixer_retention_na(_modulate(h, m[0], m[1]), _modulate(hc, mc[0], mc[1]),
                                        ab_w_in[j], ab_w_out[j], ab_log_decay[j], ab_rpb[j], carry_ctx)
        else:
            y = _pool_mixer(_modulate(h, m[0], m[1]), pool_w[j], pool_scale[j])
            if carry_ctx:
                yc = _pool_mixer(_modulate(hc, mc[0], mc[1]), pool_w[j], pool_scale[j])
        h = _post_norm(h, m[2] * y, ln_g[i, 0], ln_b[i, 0])
        h = _post_norm(h, m[5] * _hier_moe(_modulate(h, m[3], m[4]), *moe_p), ln_g[i, 1], ln_b[i, 1])
        if carry_ctx:
            hc = _post_norm(hc, mc[2] * yc, ln_g[i, 0], ln_b[i, 0])
            hc = _post_norm(hc, mc[5] * _hier_moe(_modulate(hc, mc[3], mc[4]), *moe_p), ln_g[i, 1], ln_b[i, 1])
    return h


def setup_inputs(seed=0):
    out = dict(first_inputs(seed))
    for name, value in second_inputs(seed + 1).items():
        if name != "x":
            out[name + "_2"] = value
    return out


def reference(
    x, positions, rel_bias, g_final, g_mix, w_in, swa_sinks, g_q_norm, w_q_up, g_kv_norm,
    w_kv_up, w_dw, b_dw, g_conv_ln, b_conv_ln, w_branch, w_out, g_mlp, w_up, w_down, c_2, ctx_2,
    c_ctx_2, w_mod_2, b_mod_2, ln_g_2, ln_b_2, ab_w_in_2, ab_w_out_2, ab_log_decay_2, ab_rpb_2,
    pool_w_2, pool_scale_2, moe_w_r1_2, moe_b_r1_2, moe_w_r2_2, moe_b_r2_2, moe_w_gate_2,
    moe_w_up_2, moe_w_down_2,
):
    x = first_block(
        x, positions, rel_bias, g_final, g_mix, w_in, swa_sinks, g_q_norm, w_q_up, g_kv_norm,
        w_kv_up, w_dw, b_dw, g_conv_ln, b_conv_ln, w_branch, w_out, g_mlp, w_up, w_down,
    )
    return second_block(
        x, c_2, ctx_2, c_ctx_2, w_mod_2, b_mod_2, ln_g_2, ln_b_2, ab_w_in_2, ab_w_out_2,
        ab_log_decay_2, ab_rpb_2, pool_w_2, pool_scale_2, moe_w_r1_2, moe_b_r1_2, moe_w_r2_2,
        moe_b_r2_2, moe_w_gate_2, moe_w_up_2, moe_w_down_2,
    )


_drawn_inputs = setup_inputs


def setup_inputs(seed=0):
    import zlib

    import numpy as np

    out = dict(_drawn_inputs(seed))
    spreads = {}
    factors = {'swa_sinks': 7.705,
     'g_q_norm': 8.0,
     'g_kv_norm': 4.817,
     'b_dw': 2.871,
     'b_conv_ln': 5.753,
     'ctx_2': 3.421,
     'b_mod_2': 5.042,
     'ab_log_decay_2': 28.64,
     'ab_rpb_2': 64.0,
     'pool_scale_2': 5.812,
     'moe_b_r1_2': 40.706,
     'moe_b_r2_2': 46.406}
    for name, (base, spread) in spreads.items():
        noise = np.random.default_rng([zlib.crc32(name.encode()), seed]).standard_normal(out[name].shape)
        drawn = base * np.exp(spread * noise) if base else spread * noise
        out[name] = jnp.asarray(drawn.astype(out[name].dtype))
    for name, factor in factors.items():
        out[name] = (out[name] * factor).astype(out[name].dtype)
    return out
```

```python
from contextlib import ExitStack

import numpy as np
import concourse.bass as bass
from concourse import mybir

F32 = mybir.dt.float32
I32 = mybir.dt.int32
ALU = mybir.AluOpType
ACT = mybir.ActivationFunctionType
AX = mybir.AxisListType

P = 128
T = 256
D = 1024
KT = D // P
LAYERS = 2
HEADS = 8
HD = 64
EPS = 1e-6
LN_EPS = 1e-5
ALPHA = (2 * LAYERS) ** 0.25
NEG = -1e30
TAPS = 31
CT = 4
QR, KVR = 256, 128
NOPE, ROPE = 64, 32
N_BUCKETS = 32
EXPERTS, GROUPS, PER_GROUP = 32, 4, 8
RET = 4
GRID = 64
POOL_SIZES = (2, 4, 8, 16)

CW = 4096
RING = 4
IN_CHUNKS = 11
MLP_CHUNKS = 16
LAYER_CHUNKS = IN_CHUNKS + 1 + 3 + 2 + MLP_CHUNKS
MOD_CHUNKS = 12
AB_CHUNKS = 7
C_MOD = LAYERS * LAYER_CHUNKS
C_AB = C_MOD + 2 * MOD_CHUNKS
C_ABOUT = C_AB + AB_CHUNKS
C_POOL = C_ABOUT + 2
N_CHUNKS = C_POOL + 1
EXPERT_CHUNKS = 3
GROUP_OF = 4
TURNS = EXPERTS // GROUP_OF
SLOTS = 64
MAX_ROUNDS = T // SLOTS


def chunk_in(layer, pair):
    c = pair // 2
    return LAYER_CHUNKS * layer + (c if c < 6 else c + 1)


def chunk_latent(layer):
    return LAYER_CHUNKS * layer + 6


def chunk_branch(layer, n):
    return LAYER_CHUNKS * layer + IN_CHUNKS + 1 + n


def chunk_out(layer, half):
    return LAYER_CHUNKS * layer + IN_CHUNKS + 4 + half


def chunk_mlp(layer):
    return LAYER_CHUNKS * layer + IN_CHUNKS + 6


BRANCH_ORDER = (0, 2, 1)



def columns(spec):
    at, out = 0, {}
    for name, n in spec:
        out[name] = (at, at + n)
        at += n
    return out, at


PARAM, N_PARAM = columns([
    ("g_final", KT), ("g_mix", 2 * KT), ("g_mlp", 2 * KT), ("g_q", 2 * 2), ("g_kv", 2),
    ("w_dw", 2 * CT * TAPS), ("b_dw", 2 * CT), ("g_conv", 2 * CT), ("b_conv", 2 * CT),
    ("cond", KT * 2), ("b_mod", 2 * 48), ("ln_g", 4 * KT), ("ln_b", 4 * KT), ("pool_scale", KT),
    ("sinks", 2 * HEADS), ("rel_bias", N_BUCKETS * HEADS), ("log_decay", 2 * RET),
    ("b_router", 2 * 36), ("w_router", 2 * KT * 36)])

CONST, N_CONST = columns([
    ("ident", P), ("ones", P), ("mask_cur", P), ("mask_prev", P), ("lower", P),
    ("swap64", P), ("before", P), ("slot_no", SLOTS), ("full", MAX_ROUNDS), ("na_mask", GRID), ("rope_freq", 1), ("rope_sign", 1), ("left_f", 2), ("left_b", 2),
    ("rank4", 2 * GROUPS), ("rank8", 2 * PER_GROUP)])

CONST2, N_CONST2 = columns([
    ("dist_f", 384), ("dist_b", 384), ("diag", 384), ("dec_f", T), ("dec_b", T),
    ("axial_cos", T), ("axial_sin", T)])


def bucket_thresholds():
    n = np.arange(0, 4096)
    nf = np.maximum(n, 16).astype(np.float32)
    large = 16 + (np.log(nf / np.float32(16)) / np.float32(np.log(8.0)) * np.float32(16)).astype(np.int32)
    b = np.where(n < 16, n, np.minimum(large, 31))
    return [int(np.argmax(b >= k)) for k in range(1, N_BUCKETS)]


def shape_constants():
    p = np.arange(P)
    c = np.zeros((P, N_CONST), np.float32)

    def put(name, v):
        a, b = CONST[name]
        c[:, a:b] = v

    put("ident", np.eye(P))
    put("ones", 1.0)
    put("mask_cur", np.where(p[None, :] <= p[:, None], 0.0, NEG))
    put("mask_prev", np.where(p[None, :] > p[:, None], 0.0, NEG))
    put("lower", p[None, :] <= p[:, None])
    put("before", p[:, None] < p[None, :])
    put("slot_no", np.arange(SLOTS)[None, :])
    put("full", SLOTS * np.arange(MAX_ROUNDS)[None, :])
    put("swap64", (p[:, None] + 64) % P == p[None, :])
    qc, kc = (p % GRID)[:, None], np.arange(GRID)[None, :]
    w0 = np.clip(qc - 8, 0, GRID - 16)
    put("na_mask", np.where((kc >= w0) & (kc < w0 + 16), 0.0, NEG))
    freq = np.exp(np.float32(-np.log(10000.0)) * np.arange(16, dtype=np.float32) / np.float32(16))
    put("rope_freq", freq[p % 16][:, None])
    put("rope_sign", np.where(p % 32 < 16, -1.0, 1.0)[:, None])
    token = p[:, None] + P * np.arange(2)[None, :]
    put("left_f", T - 1 - token)
    put("left_b", token)
    put("rank4", np.tile(np.arange(GROUPS, 0, -1), 2)[None, :])
    put("rank8", np.tile(np.arange(PER_GROUP, 0, -1), 2)[None, :])

    c2 = np.zeros((P, N_CONST2), np.float32)

    def put2(name, v):
        a, b = CONST2[name]
        c2[:, a:b] = v

    d = (np.arange(384)[None, :] - P) - p[:, None]
    put2("dist_f", np.maximum(d, 0))
    put2("dist_b", np.maximum(-d, 0))
    put2("diag", 1.0 + (d == 0))
    put2("dec_f", np.arange(T)[None, :] + 1)
    put2("dec_b", T - np.arange(T)[None, :])
    t = np.arange(T)
    inv = np.float32(10000.0) ** (-np.arange(32, dtype=np.float32) / np.float32(32))
    ang = np.concatenate([(t // GRID).astype(np.float32)[:, None] * inv,
                          (t % GRID).astype(np.float32)[:, None] * inv], axis=1)
    cos, sin = np.cos(ang).T, np.sin(ang).T
    put2("axial_cos", np.concatenate([cos, cos]))
    put2("axial_sin", np.concatenate([-sin, sin]))

    counts = np.zeros((P, 4, T), np.float32)
    for g, w in enumerate(POOL_SIZES):
        lo, hi = np.clip(t - w // 2, 0, T), np.clip(t + w - w // 2, 0, T)
        counts[:, g] = 1.0 / (hi - lo)
    return c, c2, counts.reshape(P, 4 * T)


class Signals:

    def __init__(self, nc, stack, counted):
        self.nc, self.stack, self.counted = nc, stack, counted
        self.sems, self.count, self.at = {}, {}, {}
        self.engine, self.owner = None, {}

    def sem(self, kind):
        if kind not in self.sems:
            self.sems[kind] = self.stack.enter_context(self.nc.semaphore(kind))
        return self.sems[kind]

    def give(self, ins, kind, *key):
        assert self.owner.setdefault(kind, self.engine) == self.engine, f"{kind}: one engine raises a semaphore"
        self.count[kind] = self.count.get(kind, 0) + 1
        if key:
            self.at[(kind, *key)] = (kind, self.count[kind])
        ins.then_inc(self.sem(kind), 1)
        return self.count[kind]

    def note(self, event, kind, value):
        self.at[event] = (kind, value)

    def of(self, *event):
        if self.counted:
            return self.counted[event]
        return self.at.get(event, ("not_counted_yet", 1))

    def wait(self, eng, *event):
        kind, value = self.of(*event)
        eng.wait_ge(self.sem(kind), value)

    def base(self, kind, value=None):
        if value is not None:
            self.count[kind] = value
        return self.count.get(kind, 0)


def two_blocks_kernel(nc, stream, experts, tokens, ctx_tokens, params, consts, consts2, pool_counts, positions,
                      na_bias, out, counted):
    stack = ExitStack()
    with stack:
        def sb(name, shape, dt=F32):
            return stack.enter_context(nc.sbuf_tensor(name, shape, dt))

        S = Signals(nc, stack, counted)

        ring = sb("ring", [P, RING, CW])
        x = sb("x", [P, KT, T])
        h = sb("h", [P, KT, T])
        scratch = sb("scratch", [P, KT, T])
        wide = sb("wide", [P, 8192])
        arena = sb("arena", [P, 14464])
        smax = sb("smax", [P, 6, 512])
        stat = sb("stat", [P, 2, 512])
        small = sb("small", [P, 384])
        par = sb("par", [P, N_PARAM])
        con = sb("con", [P, N_CONST])
        pos_i = sb("pos_i", [P, T + 2], I32)
        banks = [stack.enter_context(nc.psum_tensor(f"bank{i}", [P, 512], F32)) for i in range(4)]
        sums = [stack.enter_context(nc.psum_tensor(f"sums{i}", [P, 512], F32)) for i in range(4)]

        def prm(name, i=0, n=1):
            a = PARAM[name][0] + i
            return par[:, a:a + n]

        def cst(name, i=0, n=None):
            a, b = CONST[name]
            return con[:, a + i:(b if n is None else a + i + n)]

        ident, ones = cst("ident"), cst("ones")

        def carve(tensor, spec):
            at, views = 0, {}
            for name, *dims in spec:
                n = int(np.prod(dims))
                v = tensor[:, at:at + n]
                if len(dims) > 1:
                    v = v.rearrange("p (a b) -> p a b", a=dims[0])
                views[name] = v
                at += n
            return views

        A = carve(arena, [("qa", 4, T), ("ka", T), ("va", 2, P), ("cq", 2, T), ("ckv", T), ("qn", 4, T),
                          ("qp", 2, T), ("kn", 4, T), ("kp", T), ("vc", 2, 512), ("u", CT, 30 + T),
                          ("conv", CT, T), ("ya", 4, T), ("yc", 4, T), ("cos", T), ("sin", T),
                          ("away", 2, P), ("halfw", CT * TAPS), ("delta", N_BUCKETS * HEADS), ("pk", T)])
        B = carve(arena, [("rq", 4, T), ("rk", 4, T), ("rv", 2, 512), ("nq", 4, T), ("nk", 4, T),
                          ("nv", 2, 512), ("rg", 4, T), ("rkc", 2, 512), ("rvc", 2, 512), ("nkc", 4, T),
                          ("nvc", 2, 512), ("yn", 4, T), ("con2", N_CONST2)])
        PL = carve(arena, [("pad", 1, T + 16), ("lvl", 2, T + 16), ("z", KT, T), ("counts", 4, T)])
        gates = wide[:, 0:24 * T].rearrange("p (a b) -> p a b", a=24)
        wbias = wide[:, 24 * T:32 * T].rearrange("p (h a b) -> p h a b", h=HEADS, a=2)
        W2 = carve(wide, [("nbias", HEADS, 6 * GRID), ("decay", RET, 384), ("qd", 8, T), ("state", 8, P)])
        M = carve(wide, [("by_token", 2, D), ("gathered", KT, GROUP_OF * SLOTS), ("place", 2, GROUP_OF * SLOTS),
                         ("weighted", 2, GROUP_OF * 2 * SLOTS), ("turned", 512), ("y", 512), ("silu", T), ("hidden", T)])
        weight_of = smax[:, 0, 0:64].rearrange("p (t e) -> p t e", t=2)
        member = smax[:, 0, 64:128].rearrange("p (t e) -> p t e", t=2)
        rank = smax[:, 0, 128:192].rearrange("p (t e) -> p t e", t=2)
        rounds_i = sb("rounds", [P, 2], I32)
        hid = smax

        def flat2(v):
            return v.rearrange("p a b -> p (a b)")

        def rounds_of(eng, i):
            S.wait(eng, "rounds", i)
            return eng.value_load(rounds_i[0:1, 0:1], min_val=1, max_val=MAX_ROUNDS)

        def cst2(name):
            a, b = CONST2[name]
            return B["con2"][:, a:b]

        mod = [sb(f"mod{i}", [P, 48, 2]) for i in range(2)]
        loggam = small[:, 0:8]

        block = stack.enter_context(nc.Block())

        fills = {"n": 0, "free": [None] * 4}

        def bank_of(*fill):
            kind_bank = S.of("bank", *fill)
            return banks[kind_bank[1] % 4]

        def open_bank(pe, *fill):
            b = fills["n"] % 4
            last = fills["free"][b]
            if last is not None:
                S.wait(pe, "read", *last)
            S.note(("bank", *fill), "bank", b)
            fills["free"][b] = fill
            fills["n"] += 1
            return banks[b]

        def filled(ins, *fill):
            S.give(ins, "filled", *fill)

        def take(eng, *fill):
            S.wait(eng, "filled", *fill)
            return bank_of(*fill)

        def read(kind, value, *fill):
            S.note(("read", *fill), kind, value)

        @block.sync
        def _(sp):
            S.engine = "sync"

            def load_chunk(n, frees=None):
                if n >= RING:
                    S.wait(sp, "chunk_used", n - RING)
                if n == C_POOL:
                    S.wait(sp, "moe_summed", 0)
                sp.dma_start(ring[:, n % RING, :], stream[n]).then_inc(S.sem(f"slot_landed{n % RING}"), 16)

            def load_experts(i):
                S.wait(sp, "chunk_used", C_POOL - 1 if i == 0 else C_POOL)

                def turn(it, turn_no):
                    for q in range(EXPERT_CHUNKS * GROUP_OF):
                        e, t = q // EXPERT_CHUNKS, q % EXPERT_CHUNKS
                        if t == 0:
                            sp.wait_ge(S.sem(f"moe{i}_down_done"), it * 4 + (e + 1))
                        else:
                            sp.wait_ge(S.sem(f"moe{i}_up_done"), it * 4 + (e + 2))
                        n = i * EXPERTS * EXPERT_CHUNKS + q
                        src = experts[bass.ds(turn_no * 12 + n, 1), :, :].rearrange("a p c -> p (a c)")
                        sp.dma_start(ring[:, q % RING, :], src).then_inc(S.sem(f"moe{i}_landed{q % RING}"), 16)

                turn(0, 0)
                with sp.Fori(1, TURNS) as g:
                    turn(g, g)
                S.wait(sp, "rounds", i)
                more = sp.value_load(rounds_i[0:1, 1:2], min_val=0, max_val=MAX_ROUNDS - 1)
                with sp.If(more > 0):
                    with sp.Fori(0, more) as rnd:
                        with sp.Fori(0, TURNS) as g:
                            turn(rnd * TURNS + g + TURNS, g)

            sp.dma_start(x[:, :, :], tokens).then_inc(S.sem("tokens_landed"), 16)
            n = 0
            while n < N_CHUNKS:
                mlp = [l for l in range(LAYERS) if n == chunk_mlp(l) + RING]
                if n == C_POOL:
                    load_experts(0)
                if mlp:
                    kind, done = S.of("mlp_done_base", mlp[0])
                    with sp.Fori(0, MLP_CHUNKS // 4 - 1) as i:
                        for j in range(4):
                            sp.wait_ge(S.sem("mlp_chunk_done"), i * 4 + (done + j + 1))
                            src = stream[bass.ds(i * 4 + (n + j), 1), :, :].rearrange("a p c -> p (a c)")
                            sp.dma_start(ring[:, (n + j) % RING, :], src)\
                              .then_inc(S.sem(f"slot_landed{(n + j) % RING}"), 16)
                    n += MLP_CHUNKS - RING
                else:
                    load_chunk(n)
                    n += 1
            load_experts(1)
            S.wait(sp, "x_normed", "post", 1, 1)
            sp.dma_start(out, x[:, :, :]).then_inc(S.sem("stored"), 16)
            sp.wait_ge(S.sem("stored"), 16)

        @block.gpsimd
        def _(pool):
            S.engine = "gpsimd"

            pool.dma_start(par[:, :], params).then_inc(S.sem("params_landed"), 16)
            pool.dma_start(con[:, :], consts).then_inc(S.sem("consts_landed"), 16)
            pool.dma_start(pos_i[:, :], positions).then_inc(S.sem("positions_landed"), 16)
            S.give(pool.memset(A["u"][:, :, 0:30], 0.0), "pad_zeroed", "conv")
            for i in range(2):
                for j, kind in enumerate(("down_done", "down_done", "up_done", "up_done")):
                    pool.memset(small[:, 120 + 4 * i + j:121 + 4 * i + j], 0.0).then_inc(S.sem(f"moe{i}_{kind}"), 1)
            S.wait(pool, "x_added", 1, "mlp")
            pool.dma_start(B["con2"], consts2).then_inc(S.sem("consts2_landed"), 16)
            pool.dma_start(W2["nbias"], na_bias).then_inc(S.sem("na_bias_landed"), 16)
            S.wait(pool, "x_normed", "final")
            pool.dma_start(scratch[:, :, :], ctx_tokens).then_inc(S.sem("ctx_landed"), 16)
            S.wait(pool, "x_normed", "post", 0, 0)
            pool.dma_start(PL["counts"], pool_counts.rearrange("p (a b) -> p a b", a=4))\
                .then_inc(S.sem("counts_landed"), 16)
            S.give(pool.memset(PL["pad"], 0.0), "pad_zeroed", "pool")

        @block.tensor
        def _(pe):
            S.engine = "tensor"

            def chunk(n):
                pe.wait_ge(S.sem(f"slot_landed{n % RING}"), 16 * (n // RING + 1))
                return ring[:, n % RING, :]

            def used_with(n, kind, value):
                S.note(("chunk_used", n), kind, value)

            def product(dst, terms, first=True):
                for i, (a, b) in enumerate(terms):
                    mm = pe.matmul(dst, a, b, start=(first and i == 0), stop=(i == len(terms) - 1))
                return mm

            def over_features(src, tiles, *fill, halves=1):
                bank = open_bank(pe, *fill)
                for j in range(halves):
                    mm = product(bank[:, j * T:(j + 1) * T], [(ones, src(j, k)) for k in range(tiles[j])])
                filled(mm, *fill)

            def rms_sum(tag):
                S.wait(pe, "squares", *tag)
                over_features(lambda j, k: scratch[:, k, :], [KT], "sum", *tag)

            def transposed(dst, src):
                return pe.transpose(dst, src, ident)

            def column_pair(src, n, col, *fill):
                w = chunk(n).rearrange("p (k c) -> p k c", k=KT)
                bank = open_bank(pe, *fill)
                for j in range(2):
                    c = (col + j) * P
                    mm = product(bank[:, j * T:(j + 1) * T], [(w[:, k, c:c + P], src[:, k, :]) for k in range(KT)])
                filled(mm, *fill)

            pe.wait_ge(S.sem("consts_landed"), 16)
            pe.wait_ge(S.sem("params_landed"), 16)

            def in_pair(l, pair):
                n = chunk_in(l, pair)
                w = chunk(n).rearrange("p (k c) -> p k c", k=KT)
                bank = open_bank(pe, "in", l, pair)
                for j in range(2):
                    c = ((pair % 2) * 2 + j) * P
                    if pair == 2 and j == 1:
                        for t in range(2):
                            mm = product(bank[:, T + t * P:T + (t + 1) * P],
                                         [(h[:, k, t * P:(t + 1) * P], w[:, k, c:c + P]) for k in range(KT)])
                    elif not (pair == 4 and j == 1):
                        mm = product(bank[:, j * T:(j + 1) * T], [(w[:, k, c:c + P], h[:, k, :]) for k in range(KT)])
                filled(mm, "in", l, pair)
                used_with(n, *S.at[("filled", "in", l, pair)])

            def latent_up(l):
                S.wait(pe, "latent_normed", l)
                n = chunk_latent(l)
                w = chunk(n)
                wq = w[:, 0:2 * QR * 4].rearrange("p (k c) -> p k c", k=2)
                wkv = w[:, 2048:3072]
                cq, ckv = A["cq"], A["ckv"]
                for i in range(2):
                    bank = open_bank(pe, "qn", l, i)
                    for j in range(2):
                        c = (2 * i + j) * P
                        mm = product(bank[:, j * T:(j + 1) * T], [(wq[:, k, c:c + P], cq[:, k, :]) for k in range(2)])
                    filled(mm, "qn", l, i)
                for i in range(2):
                    bank = open_bank(pe, "qp", l, i)
                    for j in range(2):
                        c = 512 + 256 * j + i * P
                        mm = product(bank[:, j * T:(j + 1) * T], [(wq[:, k, c:c + P], cq[:, k, :]) for k in range(2)])
                    filled(mm, "qp", l, i)
                for i in range(2):
                    bank = open_bank(pe, "kn", l, i)
                    for j in range(2):
                        c = (2 * i + j) * P
                        mm = product(bank[:, j * T:(j + 1) * T], [(wkv[:, c:c + P], ckv)])
                    filled(mm, "kn", l, i)
                for t in range(2):
                    bank = open_bank(pe, "vc", l, t)
                    mm = product(bank[:, :], [(ckv[:, t * P:(t + 1) * P], wkv[:, 512:1024])])
                    filled(mm, "vc", l, t)
                used_with(n, *S.at[("filled", "vc", l, 1)])

            def scores(l, u):
                bank = open_bank(pe, "s", l, u)
                if u < HEADS:
                    a, b = (u % 2) * HD, (u % 2) * HD + 32 * (u // 2 % 2)
                    if u == 0:
                        S.wait(pe, "latent_keys", l)
                        S.wait(pe, "latent_queries", l)
                        S.wait(pe, "latent_rotated", l)
                    pairs = [(A["qn"][a:a + HD, u // 2, :], A["kn"][a:a + HD, u // 2, :]),
                             (A["qp"][b:b + 32, u // 4, :], A["kp"][b:b + 32, :])]
                else:
                    a = (u % 2) * HD
                    if u == HEADS:
                        S.wait(pe, "window_queries", l, 1)
                        S.wait(pe, "window_keys", l)
                    pairs = [(A["qa"][a:a + HD, (u - HEADS) // 2, :], A["ka"][a:a + HD, :])]
                for t, (c0, c1, nk) in enumerate([(0, P, P), (P, 3 * P, T)]):
                    mm = product(bank[:, c0:c1], [(q[:, t * P:(t + 1) * P], k[:, 0:nk]) for q, k in pairs])
                filled(mm, "s", l, u)

            def turn(l, u):
                S.wait(pe, "probs", l, u)
                bank = open_bank(pe, "t", l, u)
                for i in range(3):
                    mm = transposed(bank[:, i * P:(i + 1) * P], smax[:, 2 + u % 2, i * P:(i + 1) * P])
                filled(mm, "t", l, u)

            state = {}

            def weigh(l, u):
                if u % 2 == 0:
                    state["y"] = open_bank(pe, "y", l, u // 2)
                S.wait(pe, "probs_turned", l, u)
                bank, a = state["y"], (u % 2) * HD
                v, c = (A["vc"], u * HD) if u < HEADS else (A["va"], a)
                pT = smax[:, 4 + u % 2, :]
                product(bank[a:a + HD, 0:P], [(v[:, 0, c:c + HD], pT[:, 0:P])])
                mm = product(bank[a:a + HD, P:T], [(v[:, 0, c:c + HD], pT[:, P:T]), (v[:, 1, c:c + HD], pT[:, T:3 * P])])
                if u % 2 == 1:
                    filled(mm, "y", l, u // 2)
                else:
                    S.give(mm, "weighed", l, u)

            def branch(l, n, y):
                c = chunk_branch(l, BRANCH_ORDER.index(n))
                w = chunk(c).rearrange("p (k c) -> p k c", k=4)
                for i in range(4):
                    bank = open_bank(pe, "branch", l, n, i)
                    for j in range(2):
                        m = (2 * i + j) * P
                        mm = product(bank[:, j * T:(j + 1) * T], [(w[:, k, m:m + P], y[:, k, :]) for k in range(4)])
                    filled(mm, "branch", l, n, i)
                used_with(c, *S.at[("filled", "branch", l, n, 3)])

            def to_model(src, chunk_at, wait_for, *fill):
                for i in range(4):
                    n = chunk_at(i // 2)
                    if i == 0:
                        for w in wait_for:
                            S.wait(pe, *w)
                    column_pair_from = (i % 2) * 2
                    w = chunk(n).rearrange("p (k c) -> p k c", k=KT)
                    bank = open_bank(pe, *fill, i)
                    for j in range(2):
                        c = (column_pair_from + j) * P
                        mm = product(bank[:, j * T:(j + 1) * T], [(w[:, k, c:c + P], src(k)) for k in range(KT)])
                    filled(mm, *fill, i)
                    used_with(n, *S.at[("filled", *fill, i)])

            def zero_sums(*read_by):
                if read_by:
                    S.wait(pe, *read_by)
                zero = S_zero
                for b in range(4):
                    pe.matmul(sums[b][:, :], zero, x[:, 0:2, :].rearrange("p a b -> p (a b)"), start=True, stop=False, skip_group_check=True)

            S_zero = small[:, 256:384]

            def sum_tile(f, kt_w, hidden, last=None):
                for m in range(KT):
                    mm = pe.matmul(sums[m // 2][:, (m % 2) * T:(m % 2 + 1) * T], kt_w[:, m * P:(m + 1) * P], hidden,
                                   start=False, stop=False, skip_group_check=True)
                return mm

            def banks_free():
                for b in range(4):
                    if fills["free"][b] is not None:
                        S.wait(pe, "read", *fills["free"][b])

            def mlp(l):
                n0 = chunk_mlp(l)
                banks_free()
                fb, rb, db = S.base("filled"), S.of("mlp_hidden_base", l)[1], S.base("mlp_chunk_done")
                S.note(("mlp_filled_base", l), "filled", fb)
                S.note(("mlp_done_base", l), "mlp_chunk_done", db)

                def up(i, j):
                    slot = (n0 + j) % RING
                    pe.wait_ge(S.sem(f"slot_landed{slot}"), i * 16 + 16 * ((n0 + j) // RING + 1))
                    pe.wait_ge(S.sem("mlp_hidden"), i * 4 + (rb + j - 3))
                    w = ring[:, slot, 0:2048].rearrange("p (k c) -> p k c", k=KT)
                    for f in range(2):
                        mm = product(banks[j][:, f * T:(f + 1) * T],
                                     [(w[:, k, f * P:(f + 1) * P], h[:, k, :]) for k in range(KT)])
                    mm.then_inc(S.sem("filled"), 1)

                def down(i, j):
                    slot = (n0 + j) % RING
                    pe.wait_ge(S.sem("mlp_hidden"), i * 4 + (rb + j + 1))
                    w = ring[:, slot, 2048:4096].rearrange("p (f c) -> p f c", f=2)
                    for f in range(2):
                        mm = sum_tile(f, w[:, f, :], hid[:, 2 + j, f * T:(f + 1) * T])
                    mm.then_inc(S.sem("mlp_chunk_done"), 1)

                with pe.Fori(0, MLP_CHUNKS // 4) as i:
                    up(i, 0)
                    for j in range(1, 4):
                        up(i, j)
                        down(i, j - 1)
                    down(i, 3)
                S.base("filled", fb + MLP_CHUNKS)
                S.base("mlp_chunk_done", db + MLP_CHUNKS)
                for c in range(MLP_CHUNKS):
                    used_with(n0 + c, "mlp_chunk_done", db + c + 1)
                fills["n"] = 0
                for b in range(4):
                    fills["free"][b] = ("mlp_last", l, b)
                    S.note(("read", "mlp_last", l, b), "mlp_hidden", rb + MLP_CHUNKS - 3 + b)
                S.note(("mlp_summed", l), "mlp_chunk_done", db + MLP_CHUNKS)

            def block_1(l):
                rms_sum(("mix", l))
                S.wait(pe, "h_ready", "mix", l)
                for pair in range(10):
                    in_pair(l, pair)
                S.wait(pe, "latent_squares", l)
                over_features(lambda j, k: scratch[:, 2 * j + k, :], [2, 1], "sum", "latent", l, halves=2)
                in_pair(l, 10)
                in_pair(l, 11)
                latent_up(l)
                for u in range(2 * HEADS + 2):
                    if u < 2 * HEADS:
                        scores(l, u)
                        if u % 2 == 0 or u in (1, 3):
                            if 12 + state.setdefault(("gate", l), 0) < 22:
                                in_pair(l, 12 + state[("gate", l)])
                                state[("gate", l)] += 1
                    if 1 <= u <= 2 * HEADS:
                        turn(l, u - 1)
                    if u >= 2:
                        weigh(l, u - 2)
                S.wait(pe, "y_ready", "window", l)
                branch(l, 0, A["ya"])
                S.wait(pe, "conv_done", l)
                over_features(lambda j, k: A["conv"][:, k, :], [CT], "sum", "conv", l)
                branch(l, 2, A["yc"])
                S.wait(pe, "squares", "conv", l)
                over_features(lambda j, k: scratch[:, k, :], [CT], "sum2", "conv", l)
                S.wait(pe, "y_ready", "conv", l)
                branch(l, 1, A["conv"])
                to_model(lambda k: h[:, k, :], lambda half: chunk_out(l, half), [("mixed", l)], "out", l)
                rms_sum(("mlp", l))
                if l == 0:
                    S.wait(pe, "zero_ready", 0)
                zero_sums(*(("x_added", l - 1, "mlp") if l else ()))
                S.wait(pe, "h_ready", "mlp", l)
                mlp(l)

            for l in range(LAYERS):
                block_1(l)

            S.wait(pe, "cond_ready", 0)
            for i in range(2):
                bank = open_bank(pe, "mod", i)
                for t in range(48):
                    n = C_MOD + MOD_CHUNKS * i + t // 4
                    if t % 4 == 0:
                        w = chunk(n).rearrange("p (k c) -> p k c", k=KT)
                    c = (t % 4) * P
                    mm = product(bank[:, 2 * t:2 * t + 2],
                                 [(w[:, k, c:c + P], small[:, 8 + 2 * k:10 + 2 * k]) for k in range(KT)])
                    if t % 4 == 3 and t < 47:
                        S.give(mm, "mod_chunk_done", i, t)
                        used_with(n, *S.at[("mod_chunk_done", i, t)])
                filled(mm, "mod", i)
                used_with(n, *S.at[("filled", "mod", i)])
            rms_sum(("final",))

            def feature_cols(n, src, name):
                w = chunk(n).rearrange("p (k c) -> p k c", k=KT)
                for i in range(2):
                    bank = open_bank(pe, name, i)
                    for j in range(2):
                        c = (2 * i + j) * P
                        mm = product(bank[:, j * T:(j + 1) * T], [(w[:, k, c:c + P], src[:, k, :]) for k in range(KT)])
                    filled(mm, name, i)
                    used_with(n, *S.at[("filled", name, i)])

            def token_rows(n, src, name):
                w = chunk(n).rearrange("p (k c) -> p k c", k=KT)
                for t in range(2):
                    bank = open_bank(pe, name, t)
                    mm = product(bank[:, :], [(src[:, k, t * P:(t + 1) * P], w[:, k, :]) for k in range(KT)])
                    filled(mm, name, t)
                    used_with(n, *S.at[("filled", name, t)])

            S.wait(pe, "h_ready", "mod", 0, 0)
            feature_cols(C_AB, h, "rk")
            S.wait(pe, "ctx_modulated", 0)
            token_rows(C_AB, scratch, "rkc")
            token_rows(C_AB + 1, h, "rv")
            token_rows(C_AB + 1, scratch, "rvc")
            feature_cols(C_AB + 2, h, "nk")
            feature_cols(C_AB + 2, scratch, "nkc")
            token_rows(C_AB + 3, h, "nv")
            token_rows(C_AB + 3, scratch, "nvc")
            feature_cols(C_AB + 4, h, "rq")
            for which in ("rk", "rq"):
                for i in range(2):
                    S.wait(pe, "projected", which, i)
                    bank = open_bank(pe, "swap", which, i)
                    for j in range(2):
                        mm = product(bank[:, j * T:(j + 1) * T], [(cst("swap64"), B[which][:, 2 * i + j, :])])
                    filled(mm, "swap", which, i)
            for d in range(2):
                bank = open_bank(pe, "state", d)
                for hd in range(RET):
                    S.wait(pe, "keys_decayed", d, hd)
                    kd = smax[:, (4 * d + hd) % 6, 0:2 * P].rearrange("p (t c) -> p t c", t=2)
                    mm = product(bank[:, hd * P:(hd + 1) * P],
                                 [(kd[:, t, :], B["rvc"][:, t, hd * P:(hd + 1) * P]) for t in range(2)])
                    if hd < RET - 1:
                        S.give(mm, "state_done", d, hd)
                filled(mm, "state", d)
            feature_cols(C_AB + 5, h, "rg")
            feature_cols(C_AB + 6, h, "nq")
            for hd in range(RET):
                if hd == 0:
                    S.wait(pe, "rotated", "rk", 1)
                    S.wait(pe, "rotated", "rq", 1)
                bank = open_bank(pe, "att", hd)
                for j in range(2):
                    mm = product(bank[:, j * T:(j + 1) * T], [(B["rk"][:, hd, j * P:(j + 1) * P], B["rq"][:, hd, :])])
                filled(mm, "att", hd)
            for i in range(2):
                bank = open_bank(pe, "ret", i)
                for j in range(2):
                    hd = 2 * i + j
                    S.wait(pe, "att_decayed", hd)
                    if hd == 0:
                        S.wait(pe, "states_kept", 1)
                        S.wait(pe, "queries_decayed", 0)
                    at = smax[:, 2 + hd, :]
                    mm = product(bank[:, j * T:(j + 1) * T],
                                 [(B["rv"][:, t, hd * P:(hd + 1) * P], at[:, t * T:(t + 1) * T]) for t in range(2)]
                                 + [(W2["state"][:, 4 * d + hd, :], W2["qd"][:, 4 * d + hd, :]) for d in range(2)])
                filled(mm, "ret", i)
            for what, src in (("sum", lambda hd: B["rkc"].rearrange("p a (b t) -> p (a b) t", b=2)[:, hd, :]),
                              ("sum2", lambda hd: scratch[:, hd, :])):
                for i in range(2):
                    if what == "sum":
                        S.wait(pe, "retained", i)
                    else:
                        S.wait(pe, "squares", "head", i)
                    bank = open_bank(pe, what, "head", i)
                    for j in range(2):
                        mm = product(bank[:, j * T:(j + 1) * T], [(ones, src(2 * i + j))])
                    filled(mm, what, "head", i)

            def na_scores(u):
                hd, t = u // 2, u % 2
                a = (hd % 2) * HD
                if u == 0:
                    S.wait(pe, "projected", "nq", 1)
                    S.wait(pe, "projected", "nkc", 1)
                bank = open_bank(pe, "s", "na", u)
                q = B["nq"][a:a + HD, hd // 2, t * P:(t + 1) * P]
                product(bank[:, 0:T], [(q, B["nk"][a:a + HD, hd // 2, :])])
                mm = product(bank[:, T:2 * T], [(q, B["nkc"][a:a + HD, hd // 2, :])])
                filled(mm, "s", "na", u)

            def na_turn(u):
                S.wait(pe, "probs", "na", u)
                bank = open_bank(pe, "t", "na", u)
                for i in range(4):
                    mm = transposed(bank[:, i * P:(i + 1) * P], smax[:, 2 + u % 2, i * P:(i + 1) * P])
                filled(mm, "t", "na", u)

            def na_weigh(u):
                hd, t = u // 2, u % 2
                a, c = (hd % 2) * HD, hd * HD
                S.wait(pe, "probs_turned", "na", u)
                pT = smax[:, 4 + u % 2, :]
                mm = product(sums[u // 4][a:a + HD, t * P:(t + 1) * P],
                             [(B["nv"][:, k, c:c + HD], pT[:, k * P:(k + 1) * P]) for k in range(2)]
                             + [(B["nvc"][:, k, c:c + HD], pT[:, (2 + k) * P:(3 + k) * P]) for k in range(2)])
                if u % 4 == 3:
                    filled(mm, "y", "na", u // 4)
                else:
                    S.give(mm, "weighed", "na", u)

            for u in range(16 + 2):
                if u < 16:
                    na_scores(u)
                if 1 <= u <= 16:
                    na_turn(u - 1)
                if u >= 2:
                    na_weigh(u - 2)
            to_model(lambda k: (B["rg"] if k < 4 else B["yn"])[:, k % 4, :], lambda half: C_ABOUT + half,
                     [("ret_ready", 0), ("y_ready", "na")], "ab_out")

            def layer_norm_sums(i, s):
                S.wait(pe, "added", i, s)
                over_features(lambda j, k: x[:, k, :], [KT], "sum", "post", i, s)
                S.wait(pe, "squares", "post", i, s)
                over_features(lambda j, k: scratch[:, k, :], [KT], "sum2", "post", i, s)

            def moe(i):
                S.wait(pe, "h_ready", "mod", i, 1)
                bank = open_bank(pe, "router", i)
                for t in range(2):
                    mm = product(bank[:, t * 64:t * 64 + 36],
                                 [(h[:, k, t * P:(t + 1) * P], prm("w_router", (i * KT + k) * 36, 36)) for k in range(KT)])
                filled(mm, "router", i)
                for t in range(2):
                    for half in range(2):
                        bank = open_bank(pe, "rows", i, t, half)
                        for k in range(4):
                            mm = transposed(bank[:, k * P:(k + 1) * P], h[:, 4 * half + k, t * P:(t + 1) * P])
                        filled(mm, "rows", i, t, half)
                zero_sums("x_added", 1, "mlp") if i == 0 else zero_sums("added", 0, 1)
                S.wait(pe, "members", i)
                bank = open_bank(pe, "rank", i)
                product(bank[:, 0:32], [(cst("before"), member[:, 0, :])])
                product(bank[:, 32:64], [(ones, member[:, 0, :]), (cst("before"), member[:, 1, :])])
                filled(product(bank[:, 64:96], [(ones, member[:, 0, :]), (ones, member[:, 1, :])]), "rank", i)
                S.wait(pe, "rows_kept", i, 1, 1)
                banks_free()

                def raised(kind, it, add, per_turn):
                    pe.wait_ge(S.sem(f"moe{i}_{kind}"), it * per_turn + add)

                def give(ins, kind):
                    ins.then_inc(S.sem(f"moe{i}_{kind}"), 1)

                def landed(it, q):
                    raised(f"landed{q % RING}", it, 16 * (q // RING + 1), 48)
                    return ring[:, q % RING, :]

                def gather(it):
                    raised("placed", it, 1, 1)
                    for j in range(4):
                        bank = banks[3 - j]
                        for a in range(2):
                            k = 2 * j + a
                            mm = product(bank[:, a * T:(a + 1) * T],
                                         [(M["by_token"][:, t, k * P:(k + 1) * P], M["place"][:, t, :]) for t in range(2)])
                        give(mm, "gather_done")

                def gate_up(it, e):
                    if e == 0:
                        raised("gather_kept", it, 4, 4)
                    for c in range(2):
                        w = landed(it, 3 * e + c).rearrange("p (k c) -> p k c", k=4)
                        for kk in range(4):
                            k = 4 * c + kk
                            for half in range(2):
                                mm = pe.matmul(banks[0][64 * half:64 * half + 64, :],
                                               M["gathered"][:, k, e * SLOTS:(e + 1) * SLOTS],
                                               w[:, kk, 512 * half:512 * half + 512], start=(k == 0), stop=(k == KT - 1))
                    give(mm, "up_done")

                def turn(it, e):
                    raised("hidden", it, e + 1, 4)
                    for j in range(2):
                        transposed(banks[1][:, j * P:(j + 1) * P], M["hidden"][:, j * P:(j + 1) * P])
                    for t in range(2):
                        mm = transposed(banks[1][:, T + t * P:T + (t + 1) * P],
                                        M["weighted"][:, t, 2 * e * SLOTS:2 * (e + 1) * SLOTS])
                    give(mm, "turn_done")

                def down(it, e):
                    raised("turned", it, e + 1, 4)
                    w = landed(it, 3 * e + 2).rearrange("p (k c) -> p k c", k=4)
                    for k in range(4):
                        hT = M["turned"][:, (k % 2) * P + (k // 2) * 64:(k % 2) * P + (k // 2) * 64 + 64]
                        for half in range(2):
                            mm = pe.matmul(banks[2][64 * half:64 * half + 64, :], hT, w[:, k, 512 * half:512 * half + 512],
                                           start=(k == 0), stop=(k == 3))
                    give(mm, "down_done")

                def spread(it, e):
                    raised("y_kept", it, e + 1, 4)
                    for m in (0, 4, 1, 5, 2, 6, 3, 7):
                        a, c = 64 * (m // 4), (m % 4) * P
                        pe.matmul(sums[m // 2][:, (m % 2) * T:(m % 2 + 1) * T], M["y"][a:a + 64, c:c + P],
                                  M["turned"][a:a + 64, T:2 * T], start=False, stop=False, skip_group_check=True)

                with pe.Fori(0, rounds_of(pe, i)) as rnd:
                    with pe.Fori(0, TURNS) as g:
                        it = rnd * TURNS + g
                        gather(it)
                        for e in range(GROUP_OF):
                            gate_up(it, e)
                            if e:
                                spread(it, e - 1)
                            turn(it, e)
                            down(it, e)
                        spread(it, GROUP_OF - 1)
                for b in range(4):
                    mm = pe.matmul(sums[b][:, :], S_zero, flat2(x[:, 0:2, :]), start=False, stop=True, skip_group_check=True)
                S.give(mm, "moe_summed", i)
                fills["n"] = 0
                fills["free"] = [None] * 4

            layer_norm_sums(0, 0)
            moe(0)
            layer_norm_sums(0, 1)
            w = chunk(C_POOL)[:, 0:2048].rearrange("p (g k c) -> p g k c", g=4, k=2)
            for g in range(4):
                S.wait(pe, "pooled", g)
                bank = open_bank(pe, "pool", g)
                for j in range(2):
                    mm = product(bank[:, j * T:(j + 1) * T],
                                 [(w[:, g, k, j * P:(j + 1) * P], PL["z"][:, 2 * g + k, :]) for k in range(2)])
                filled(mm, "pool", g)
            used_with(C_POOL, *S.at[("filled", "pool", 3)])
            layer_norm_sums(1, 0)
            moe(1)
            layer_norm_sums(1, 1)

        @block.scalar
        def _(act):
            S.engine = "scalar"

            def done(ins, *fill):
                read("act_read", S.give(ins, "act_read"), *fill)

            def root(tag, n=T):
                S.wait(act, "variance", *tag)
                S.give(act.activation(stat[:, 1, 0:n], stat[:, 0, 0:n], ACT.Sqrt), "root", *tag)

            def copy_out(dst, src, kind, key, fill, scale=None):
                bank = take(act, *fill)
                ins = act.activation(dst, src(bank), ACT.Copy, scale=1.0 if scale is None else scale)
                read(kind, S.give(ins, kind, *key), *fill)

            act.wait_ge(S.sem("params_landed"), 16)
            S.give(act.activation(small[:, 8:24], prm("cond", 0, 16), ACT.Silu), "cond_ready", 0)
            S.give(act.activation(small[:, 24:32], prm("log_decay", 0, 8), ACT.Exp), "decay_exp", 0)
            S.wait(act, "decay_arg", 0)
            S.give(act.activation(small[:, 40:48], small[:, 32:40], ACT.Ln), "decay_ln", 0)
            S.wait(act, "angles", 0)
            act.activation(A["sin"], scratch[:, 0, :], ACT.Sin)
            S.give(act.activation(A["cos"], scratch[:, 1, :], ACT.Sin, bias=float(np.pi / 2)), "rope_tables", 0)

            def softmax_exps(l, u):
                S.wait(act, "row_max", l, u)
                st = u % 2 * 16
                if u >= 2:
                    S.wait(act, "filled", "t", l, u - 2)
                act.activation(smax[:, 2 + u % 2, 0:P], smax[:, u % 2, 0:P], ACT.Exp,
                               bias=small[:, 48 + st:49 + st], accum_out=small[:, 50 + st:51 + st])
                ins = act.activation(smax[:, 2 + u % 2, P:3 * P], smax[:, u % 2, P:3 * P], ACT.Exp,
                                     bias=small[:, 49 + st:50 + st], accum_out=small[:, 51 + st:52 + st])
                if u >= HEADS:
                    s = prm("sinks", l * HEADS + sink_of(u))
                    for t in range(2):
                        ins = act.activation(small[:, 52 + st + t:53 + st + t], s, ACT.Exp,
                                             bias=small[:, 48 + st + t:49 + st + t])
                S.give(ins, "exps", l, u)

            def turned(l, u, n):
                bank = take(act, "t", l, u)
                if u >= 2:
                    S.wait(act, *weighed(l, u - 2))
                ins = act.activation(smax[:, 4 + u % 2, 0:n], bank[:, 0:n], ACT.Copy)
                read("probs_turned", S.give(ins, "probs_turned", l, u), "t", l, u)

            def weighed(l, u):
                if l == "na":
                    return ("filled", "y", "na", u // 4) if u % 4 == 3 else ("weighed", "na", u)
                return ("filled", "y", l, u // 2) if u % 2 else ("weighed", l, u)

            def tanh_gates(l, pair):
                g = pair - 10
                bank = take(act, "in", l, pair)
                dst = gates[:, 2 * g:2 * g + 2, :].rearrange("p a b -> p (a b)")
                ins = act.activation(dst, bank[:, :], ACT.Tanh, scale=0.5)
                read("gates_ready", S.give(ins, "gates_ready", l, pair), "in", l, pair)

            def block_1(l):
                root(("mix", l))
                for i in range(2):
                    copy_out(A["qa"][:, 2 * i:2 * i + 2, :].rearrange("p a b -> p (a b)"), lambda b: b[:, :],
                             "window_queries", (l, i), ("in", l, i))
                bank = take(act, "in", l, 2)
                act.activation(A["ka"], bank[:, 0:T], ACT.Copy)
                ins = act.activation(A["va"].rearrange("p a b -> p (a b)"), bank[:, T:2 * T], ACT.Copy)
                read("window_keys", S.give(ins, "window_keys", l), "in", l, 2)
                bank = take(act, "in", l, 3)
                act.activation(A["cq"].rearrange("p a b -> p (a b)"), bank[:, :], ACT.Copy)
                done(act.activation(scratch[:, 0:2, :].rearrange("p a b -> p (a b)"), bank[:, :], ACT.Square), "in", l, 3)
                bank = take(act, "in", l, 4)
                act.activation(A["ckv"], bank[:, 0:T], ACT.Copy)
                ins = act.activation(scratch[:, 2, :], bank[:, 0:T], ACT.Square)
                read("latent_squares", S.give(ins, "latent_squares", l), "in", l, 4)
                for j in range(CT):
                    bank = take(act, "in", l, 6 + j)
                    if j >= 2:
                        S.wait(act, "glu", l, j - 2)
                    S.give(act.activation(stat_glu(j), bank[:, T:2 * T], ACT.Tanh, scale=0.5), "glu_tanh", l, j)
                root(("latent", l), 512)
                tanh_gates(l, 10)
                tanh_gates(l, 11)
                for i in range(2):
                    copy_out(A["qn"][:, 2 * i:2 * i + 2, :].rearrange("p a b -> p (a b)"), lambda b: b[:, :],
                             "latent_queries", ((l,) if i else (l, "first")), ("qn", l, i))
                for i in range(2):
                    copy_out(A["kn"][:, 2 * i:2 * i + 2, :].rearrange("p a b -> p (a b)"), lambda b: b[:, :],
                             "latent_nope", (l, i), ("kn", l, i))
                for t in range(2):
                    copy_out(A["vc"][:, t, :], lambda b: b[:, :], "latent_keys", ((l,) if t else (l, "first")),
                             ("vc", l, t))
                g = 12
                for u in range(2 * HEADS + 2):
                    if u < 2 * HEADS:
                        softmax_exps(l, u)
                        if (u % 2 == 0 or u in (1, 3)) and g < 22:
                            tanh_gates(l, g)
                            g += 1
                    if 1 <= u <= 2 * HEADS:
                        turned(l, u - 1, 3 * P)
                    if u >= 3 and u % 2 == 1:
                        pair = (u - 3) // 2
                        attended(l, pair)
                root(("conv", l))
                for j in range(CT):
                    S.wait(act, "conv_normed", l, j)
                    ins = act.activation(A["conv"][:, j, :], scratch[:, j, :], ACT.Silu,
                                         scale=prm("g_conv", l * CT + j), bias=prm("b_conv", l * CT + j))
                S.give(ins, "y_ready", "conv", l)
                root(("mlp", l))
                fb, hb, rb = S.of("mlp_filled_base", l)[1], S.of("mlp_hidden_base", l)[1], S.base("relued")
                S.note(("relued_base", l), "relued", rb)
                with act.Fori(0, MLP_CHUNKS // 4) as i:
                    for j in range(4):
                        act.wait_ge(S.sem("filled"), i * 4 + (fb + j + 1))
                        act.wait_ge(S.sem("mlp_hidden"), i * 4 + (hb + j - 1))
                        act.activation(hid[:, j % 2, :], banks[j][:, :], ACT.Relu).then_inc(S.sem("relued"), 1)
                S.base("relued", rb + MLP_CHUNKS)

            def attended(l, pair):
                y = A["yc"] if pair < 4 else A["ya"]
                kind = "y_ready" if pair == 7 else "y_kept"
                copy_out(y[:, pair % 4, :], lambda b: b[:, 0:T], kind,
                         ("window", l) if pair == 7 else (l, pair), ("y", l, pair))

            def stat_glu(j):
                return smax[:, 0, (j % 2) * T:(j % 2 + 1) * T]

            for l in range(LAYERS):
                block_1(l)

            root(("final",))
            S.wait(act, "loggam", 0)
            act.wait_ge(S.sem("consts2_landed"), 16)
            for hd in range(RET):
                S.wait(act, "exponent", hd)
                ins = act.activation(W2["decay"][:, hd, :], W2["decay"][:, hd, :], ACT.Exp)
                S.give(ins, "decay_exps", hd)
            for d, name in enumerate(("dec_f", "dec_b")):
                for hd in range(RET):
                    ins = act.activation(W2["qd"][:, 4 * d + hd, :], cst2(name), ACT.Exp,
                                         scale=loggam[:, 4 * d + hd:4 * d + hd + 1])
            S.give(ins, "query_decays", 0)
            for d, name in enumerate(("left_f", "left_b")):
                for hd in range(RET):
                    ins = act.activation(small[:, 96 + 2 * (4 * d + hd):98 + 2 * (4 * d + hd)], cst(name), ACT.Exp,
                                         scale=loggam[:, 4 * d + hd:4 * d + hd + 1])
            S.give(ins, "key_decays", 0)

            def keep(name, tiles=2, scale=None):
                for i in range(tiles):
                    t = B[name]
                    n = t.shape[1] // 2
                    dst = t[:, n * i:n * i + n, :].rearrange("p a b -> p (a b)")
                    copy_out(dst, lambda b: b[:, :], "projected", (name, i), (name, i), scale)

            keep("rk")
            keep("rkc")
            keep("rv")
            keep("rvc")
            keep("nk")
            keep("nkc")
            keep("nv")
            keep("nvc")
            keep("rq", scale=float(P) ** -0.5)
            for d in range(2):
                copy_out(W2["state"][:, 4 * d:4 * d + 4, :].rearrange("p a b -> p (a b)"), lambda b: b[:, :],
                         "states_kept", (d,), ("state", d))
            for i in range(2):
                bank = take(act, "rg", i)
                ins = act.activation(B["rg"][:, 2 * i:2 * i + 2, :].rearrange("p a b -> p (a b)"), bank[:, :], ACT.Silu)
                read("projected", S.give(ins, "projected", "rg", i), "rg", i)
            keep("nq")
            for i in range(2):
                copy_out(B["rkc"][:, i, :], lambda b: b[:, :], "retained", (i,), ("ret", i))
            for i in range(2):
                S.wait(act, "variance", "head", i)
                S.give(act.activation(smax[:, 2 + i, :], smax[:, 2 + i, :], ACT.Sqrt), "root", "head", i)
            for u in range(16 + 2):
                if u < 16:
                    S.wait(act, "row_max", "na", u)
                    st = u % 2 * 16
                    if u >= 2:
                        S.wait(act, "filled", "t", "na", u - 2)
                    ins = act.activation(smax[:, 2 + u % 2, :], smax[:, u % 2, :], ACT.Exp,
                                         bias=small[:, 48 + st:49 + st], accum_out=small[:, 50 + st:51 + st])
                    S.give(ins, "exps", "na", u)
                if 1 <= u <= 16:
                    turned("na", u - 1, 512)
                if u >= 2 and (u - 2) % 4 == 3:
                    pair = (u - 2) // 4
                    S.wait(act, "filled", "y", "na", pair)
                    ins = act.activation(B["yn"][:, pair, :], sums[pair][:, 0:T], ACT.Copy)
                    if pair == 3:
                        S.give(ins, "y_ready", "na")

            def moe(i):
                for t in range(2):
                    for half in range(2):
                        copy_out(M["by_token"][:, t, 512 * half:512 * half + 512], lambda b: b[:, :], "rows_kept",
                                 (i, t, half), ("rows", i, t, half))
                S.wait(act, "router_shifted", i)
                S.give(act.activation(small[:, 0:8], small[:, 0:8], ACT.Exp), "router_exps", i)
                S.wait(act, "top_shifted", i)
                S.give(act.activation(small[:, 8:10], small[:, 8:10], ACT.Exp), "top_exps", i)
                with act.Fori(0, rounds_of(act, i)) as rnd:
                    with act.Fori(0, TURNS) as g:
                        it = rnd * TURNS + g
                        for j in range(4):
                            act.wait_ge(S.sem(f"moe{i}_gather_done"), it * 4 + (j + 1))
                            act.activation(flat2(M["gathered"][:, 2 * j:2 * j + 2, :]), banks[3 - j][:, :], ACT.Copy)\
                               .then_inc(S.sem(f"moe{i}_gather_kept"), 1)
                        for e in range(GROUP_OF):
                            act.wait_ge(S.sem(f"moe{i}_up_done"), it * 4 + (e + 3))
                            act.activation(M["silu"], banks[0][:, 0:T], ACT.Silu).then_inc(S.sem(f"moe{i}_silued"), 1)
                            act.wait_ge(S.sem(f"moe{i}_turn_done"), it * 4 + (e + 1))
                            act.activation(M["turned"], banks[1][:, :], ACT.Copy).then_inc(S.sem(f"moe{i}_turned"), 1)

            root(("post", 0, 0))
            moe(0)
            root(("post", 0, 1))
            root(("post", 1, 0))
            moe(1)
            root(("post", 1, 1))

        @block.vector
        def _(dve):
            S.engine = "vector"

            def link(ins):
                n = S.give(ins, "dve_step")
                dve.wait_ge(S.sem("dve_step"), n)

            def done(ins, *fill):
                read("dve_read", S.give(ins, "dve_read"), *fill)

            def give_link(ins, kind, *key):
                n = S.give(ins, kind, *key)
                dve.wait_ge(S.sem(kind), n)

            def flat(v):
                return v.rearrange("p a b -> p (a b)")

            def squares(src, tag, tiles=KT):
                half = tiles // 2
                dve.tensor_tensor(flat(scratch[:, 0:half, :]), flat(src[:, 0:half, :]), flat(src[:, 0:half, :]), ALU.mult)
                S.give(dve.tensor_tensor(flat(scratch[:, half:tiles, :]), flat(src[:, half:tiles, :]),
                                         flat(src[:, half:tiles, :]), ALU.mult), "squares", *tag)

            def variance(tag, n, eps, fill, col=0):
                bank = take(dve, *fill)
                ins = dve.tensor_scalar(stat[:, 0, 0:T], bank[:, 0:T], 1.0 / n, eps, ALU.mult, ALU.add)
                read("variance", S.give(ins, "variance", *tag), *fill)

            def inverse_root(tag, n=T):
                S.wait(dve, "root", *tag)
                link(dve.reciprocal(stat[:, 1, 0:n], stat[:, 1, 0:n]))

            def rms(tag, gain, dst, kind, last_read=None):
                squares(x, tag)
                variance(tag, D, EPS, ("sum", *tag))
                inverse_root(tag)
                for k in range(KT):
                    ins = dve.scalar_tensor_tensor(out=dst[:, k, :], in0=x[:, k, :], scalar=prm(*gain(k)),
                                                   in1=stat[:, 1, 0:T], op0=ALU.mult, op1=ALU.mult)
                S.give(ins, kind, *tag)

            dve.wait_ge(S.sem("params_landed"), 16)
            dve.wait_ge(S.sem("consts_landed"), 16)
            dve.wait_ge(S.sem("positions_landed"), 16)
            dve.wait_ge(S.sem("tokens_landed"), 16)
            S.give(dve.memset(small[:, 256:384], 0.0), "zero_ready", 0)
            for j in range(4):
                S.give(dve.memset(small[:, 80 + j:81 + j], 0.0), "mlp_hidden")
            S.wait(dve, "decay_exp", 0)
            give_link(dve.tensor_scalar(small[:, 32:40], small[:, 24:32], -1.0, 1.0, ALU.mult, ALU.add), "decay_arg", 0)
            one_minus, equal = small[:, 88:96], small[:, 240:248]
            turns = scratch[:, 3, :]
            link(dve.tensor_copy(A["pk"], pos_i[:, 0:T]))
            link(dve.tensor_scalar(scratch[:, 0, :], A["pk"], cst("rope_freq"), None, ALU.mult))
            link(dve.tensor_scalar(turns, scratch[:, 0, :], float(1 / (2 * np.pi)), 12582912.0, ALU.mult, ALU.add))
            link(dve.tensor_scalar(turns, turns, -12582912.0, None, ALU.add))
            c1 = 6.28125
            link(dve.scalar_tensor_tensor(out=scratch[:, 0, :], in0=turns, scalar=-c1, in1=scratch[:, 0, :],
                                          op0=ALU.mult, op1=ALU.add))
            link(dve.scalar_tensor_tensor(out=scratch[:, 0, :], in0=turns, scalar=-float(2 * np.pi - c1),
                                          in1=scratch[:, 0, :], op0=ALU.mult, op1=ALU.add))
            link(dve.tensor_scalar(scratch[:, 0, :], scratch[:, 0, :], 3.1415925, -3.1415925, ALU.min, ALU.max))
            link(dve.tensor_scalar(scratch[:, 1, :], scratch[:, 0, :], -1.0, None, ALU.mult))
            give_link(dve.tensor_tensor(scratch[:, 1, :], scratch[:, 0, :], scratch[:, 1, :], ALU.min), "angles", 0)
            S.wait(dve, "rope_tables", 0)
            link(dve.tensor_scalar(A["sin"], A["sin"], cst("rope_sign"), None, ALU.mult))
            S.wait(dve, "decay_ln", 0)
            link(dve.tensor_scalar(one_minus, small[:, 32:40], -1.0, 1.0, ALU.mult, ALU.add))
            link(dve.tensor_scalar(equal, one_minus, 0.0, None, ALU.is_equal))
            link(dve.tensor_tensor(one_minus, one_minus, equal, ALU.add))
            link(dve.reciprocal(one_minus, one_minus))
            link(dve.tensor_tensor(one_minus, one_minus, small[:, 40:48], ALU.mult))
            link(dve.tensor_tensor(one_minus, one_minus, equal, ALU.subtract))
            S.give(dve.tensor_tensor(loggam, one_minus, small[:, 24:32], ALU.mult), "loggam", 0)

            away = A["away"]
            link(dve.tensor_copy(small[:, 248:250], pos_i[:, T:T + 2]))
            link(dve.tensor_scalar(away[:, 0, :], A["pk"][:, 0:P], -1.0, small[:, 248:249], ALU.mult, ALU.add))
            link(dve.tensor_scalar(scratch[:, 4, 0:P], A["pk"][:, P:T], -1.0, small[:, 249:250], ALU.mult, ALU.add))
            link(dve.tensor_scalar(scratch[:, 4, P:T], A["pk"][:, 0:P], -1.0, small[:, 249:250], ALU.mult, ALU.add))
            link(dve.tensor_tensor(scratch[:, 4, 0:P], scratch[:, 4, 0:P], scratch[:, 4, P:T], ALU.subtract))
            link(dve.tensor_tensor(scratch[:, 4, 0:P], scratch[:, 4, 0:P], cst("lower"), ALU.mult))
            link(dve.tensor_tensor(away[:, 1, :], scratch[:, 4, 0:P], scratch[:, 4, P:T], ALU.add))
            dve.tensor_copy(A["delta"][:, 0:HEADS], prm("rel_bias", 0, HEADS))
            link(dve.tensor_tensor(A["delta"][:, HEADS:], prm("rel_bias", HEADS, 31 * HEADS),
                                   prm("rel_bias", 0, 31 * HEADS), ALU.subtract))
            link(dve.memset(wide[:, 24 * T:32 * T], 0.0))
            for hd in range(HEADS):
                v = flat(wbias[:, hd])
                ins = dve.tensor_scalar(v, v, A["delta"][:, hd:hd + 1], None, ALU.add)
            link(ins)
            thresholds = bucket_thresholds()
            steps = iter(range(1, N_BUCKETS))

            def bias_steps(n):
                for _ in range(n):
                    b = next(steps, None)
                    if b is None:
                        return
                    reached = scratch[:, 6 + b % 2, :]
                    link(dve.tensor_scalar(reached, flat(away), float(thresholds[b - 1]), None, ALU.is_ge))
                    for hd in range(HEADS):
                        v = flat(wbias[:, hd])
                        ins = dve.scalar_tensor_tensor(out=v, in0=reached, scalar=A["delta"][:, b * HEADS + hd:b * HEADS + hd + 1],
                                                       in1=v, op0=ALU.mult, op1=ALU.add)
                    link(ins)

            def rotate(bank, dst, kind, fill, *key):
                tmp = smax[:, 2, 0:T]
                dve.tensor_tensor(dst, bank[:, 0:T], A["cos"], ALU.mult)
                link(dve.tensor_tensor(tmp, bank[:, T:2 * T], A["sin"], ALU.mult))
                n = S.give(dve.tensor_tensor(dst, dst, tmp, ALU.add), kind, *key)
                read(kind, n, *fill)
                dve.wait_ge(S.sem(kind), n)

            conv_at = {}

            def conv_taps(l, n):
                i = conv_at.setdefault(l, 0)
                for i in range(i, min(i + n, TAPS * CT)):
                    tap, j = i // CT, i % CT
                    acc = A["conv"][:, j, :]
                    src = A["u"][:, j, tap:tap + T]
                    w = A["halfw"][:, j * TAPS + tap:j * TAPS + tap + 1]
                    if tap == 0:
                        ins = dve.tensor_scalar(acc, src, w, prm("b_dw", l * CT + j), ALU.mult, ALU.add)
                    else:
                        dve.wait_ge(S.sem("conv_tap"), S.count["conv_tap"] - 3)
                        ins = dve.scalar_tensor_tensor(out=acc, in0=src, scalar=w, in1=acc, op0=ALU.mult, op1=ALU.add)
                    S.give(ins, "conv_tap")
                    conv_at[l] = i + 1
                if conv_at[l] == TAPS * CT and n:
                    conv_at[l] = TAPS * CT
                    S.note(("conv_done", l), "conv_tap", S.count["conv_tap"])

            def scores(l, u):
                bank = take(dve, "s", l, u)
                st = 48 + u % 2 * 16
                s = smax[:, u % 2, :]
                if u < HEADS:
                    scale = float(NOPE + ROPE) ** -0.5
                    dve.scalar_tensor_tensor(out=s[:, 0:P], in0=bank[:, 0:P], scalar=scale, in1=cst("mask_cur"),
                                             op0=ALU.mult, op1=ALU.add)
                    dve.tensor_scalar(s[:, P:T], bank[:, P:T], scale, None, ALU.mult)
                    ins = dve.scalar_tensor_tensor(out=s[:, T:3 * P], in0=bank[:, T:3 * P], scalar=scale,
                                                   in1=cst("mask_cur"), op0=ALU.mult, op1=ALU.add)
                    n = S.give(ins, "dve_read")
                    read("dve_read", n, "s", l, u)
                    dve.wait_ge(S.sem("dve_read"), n)
                else:
                    hd = sink_of(u)
                    scale = float(HD) ** -0.5
                    dve.scalar_tensor_tensor(out=s[:, 0:P], in0=bank[:, 0:P], scalar=scale, in1=wbias[:, hd, 0, :],
                                             op0=ALU.mult, op1=ALU.add)
                    dve.scalar_tensor_tensor(out=s[:, P:T], in0=bank[:, P:T], scalar=scale, in1=wbias[:, hd, 1, :],
                                             op0=ALU.mult, op1=ALU.add)
                    ins = dve.scalar_tensor_tensor(out=s[:, T:3 * P], in0=bank[:, T:3 * P], scalar=scale,
                                                   in1=wbias[:, hd, 1, :], op0=ALU.mult, op1=ALU.add)
                    n = S.give(ins, "dve_read")
                    read("dve_read", n, "s", l, u)
                    dve.wait_ge(S.sem("dve_read"), n)
                    dve.tensor_tensor(s[:, 0:P], s[:, 0:P], cst("mask_cur"), ALU.add)
                    dve.tensor_tensor(s[:, P:T], s[:, P:T], cst("mask_prev"), ALU.add)
                    link(dve.tensor_tensor(s[:, T:3 * P], s[:, T:3 * P], cst("mask_cur"), ALU.add))
                dve.tensor_reduce(small[:, st:st + 1], s[:, 0:P], AX.X, ALU.max)
                link(dve.tensor_reduce(small[:, st + 1:st + 2], s[:, P:3 * P], AX.X, ALU.max))
                if u < HEADS:
                    ins = dve.tensor_scalar(small[:, st:st + 2], small[:, st:st + 2], -1.0, None, ALU.mult)
                else:
                    ins = dve.tensor_scalar(small[:, st:st + 2], small[:, st:st + 2], prm("sinks", l * HEADS + sink_of(u)),
                                            -1.0, ALU.max, ALU.mult)
                S.give(ins, "row_max", l, u)

            def normalise(l, u):
                st = 48 + u % 2 * 16
                S.wait(dve, "exps", l, u)
                if l != "na" and u >= HEADS:
                    link(dve.tensor_tensor(small[:, st + 2:st + 4], small[:, st + 2:st + 4], small[:, st + 4:st + 6], ALU.add))
                n = 1 if l == "na" else 2
                link(dve.reciprocal(small[:, st + 2:st + 2 + n], small[:, st + 2:st + 2 + n]))
                p = smax[:, 2 + u % 2, :]
                if l == "na":
                    ins = dve.tensor_scalar(p, p, small[:, st + 2:st + 3], None, ALU.mult)
                else:
                    dve.tensor_scalar(p[:, 0:P], p[:, 0:P], small[:, st + 2:st + 3], None, ALU.mult)
                    ins = dve.tensor_scalar(p[:, P:3 * P], p[:, P:3 * P], small[:, st + 3:st + 4], None, ALU.mult)
                S.give(ins, "probs", l, u)

            def mix_in(l, n, first, last):
                for i in range(4):
                    bank = take(dve, "branch", l, n, i)
                    S.wait(dve, "gates_ready", l, 21)
                    g = flat(gates[:, 8 * n + 2 * i:8 * n + 2 * i + 2, :])
                    dst = flat(h[:, 2 * i:2 * i + 2, :])
                    if first:
                        done(dve.scalar_tensor_tensor(out=dst, in0=g, scalar=1.0, in1=bank[:, :], op0=ALU.add, op1=ALU.mult),
                             "branch", l, n, i)
                    else:
                        tmp = smax[:, 2 * (i % 2), :]
                        m = S.give(dve.scalar_tensor_tensor(out=tmp, in0=g, scalar=1.0, in1=bank[:, :], op0=ALU.add,
                                                            op1=ALU.mult), "dve_read")
                        read("dve_read", m, "branch", l, n, i)
                        dve.wait_ge(S.sem("dve_read"), m)
                        ins = dve.tensor_tensor(dst, dst, tmp, ALU.add)
                        if last and i == 3:
                            S.give(ins, "mixed", l)

            def centre(tag, src, tiles, n, fill):
                bank = take(dve, *fill)
                for k in range(tiles):
                    ins = dve.scalar_tensor_tensor(out=src[:, k, :], in0=bank[:, 0:T], scalar=-1.0 / n, in1=src[:, k, :],
                                                   op0=ALU.mult, op1=ALU.add)
                m = S.give(ins, "dve_read")
                read("dve_read", m, *fill)
                dve.wait_ge(S.sem("dve_read"), m)
                squares(src, tag, tiles)

            def block_1(l):
                rms(("mix", l), lambda k: ("g_mix", l * KT + k), h, "h_ready")
                link(dve.tensor_scalar(A["halfw"], prm("w_dw", l * CT * TAPS, CT * TAPS), 0.5, None, ALU.mult))
                if l == 0:
                    bias_steps(6)
                rotate(take(dve, "in", l, 5), A["kp"], "key_rotated", ("in", l, 5), l)
                if l == 0:
                    S.wait(dve, "pad_zeroed", "conv")
                for j in range(CT):
                    bank = take(dve, "in", l, 6 + j)
                    S.wait(dve, "glu_tanh", l, j)
                    ins = dve.scalar_tensor_tensor(out=A["u"][:, j, 30:], in0=smax[:, 0, (j % 2) * T:(j % 2 + 1) * T],
                                                   scalar=1.0, in1=bank[:, 0:T], op0=ALU.add, op1=ALU.mult)
                    read("glu", S.give(ins, "glu", l, j), "in", l, 6 + j)
                S.wait(dve, "glu", l, 3)
                bank = take(dve, "sum", "latent", l)
                dve.tensor_scalar(stat[:, 0, 0:T], bank[:, 0:T], 1.0 / QR, EPS, ALU.mult, ALU.add)
                ins = dve.tensor_scalar(stat[:, 0, T:2 * T], bank[:, T:2 * T], 1.0 / KVR, EPS, ALU.mult, ALU.add)
                read("variance", S.give(ins, "variance", "latent", l), "sum", "latent", l)
                inverse_root(("latent", l), 512)
                for k in range(2):
                    dve.scalar_tensor_tensor(out=A["cq"][:, k, :], in0=A["cq"][:, k, :], scalar=prm("g_q", 2 * l + k),
                                             in1=stat[:, 1, 0:T], op0=ALU.mult, op1=ALU.mult)
                ins = dve.scalar_tensor_tensor(out=A["ckv"], in0=A["ckv"], scalar=prm("g_kv", l),
                                               in1=stat[:, 1, T:2 * T], op0=ALU.mult, op1=ALU.mult)
                S.give(ins, "latent_normed", l)
                for i in range(2):
                    rotate(take(dve, "qp", l, i), A["qp"][:, i, :],
                           "latent_rotated", ("qp", l, i), *((l,) if i else (l, "first")))
                for u in range(2 * HEADS + 1):
                    if u < 2 * HEADS:
                        if l == 0 and u == HEADS:
                            bias_steps(N_BUCKETS)
                        scores(l, u)
                    if u >= 1:
                        normalise(l, u - 1)
                    if l == 0 and u < HEADS:
                        bias_steps(3)
                    conv_taps(l, 4 if l == 0 and u < HEADS else 12)
                conv_taps(l, TAPS * CT)
                mix_in(l, 0, True, False)
                centre(("conv", l), A["conv"], CT, 512, ("sum", "conv", l))
                mix_in(l, 2, False, False)
                variance(("conv", l), 512, EPS, ("sum2", "conv", l))
                inverse_root(("conv", l))
                for j in range(CT):
                    ins = dve.tensor_tensor(scratch[:, j, :], A["conv"][:, j, :], stat[:, 1, 0:T], ALU.mult)
                    S.give(ins, "conv_normed", l, j)
                mix_in(l, 1, False, True)
                for i in range(4):
                    bank = take(dve, "out", l, i)
                    dst = flat(x[:, 2 * i:2 * i + 2, :])
                    ins = dve.scalar_tensor_tensor(out=dst, in0=bank[:, :], scalar=0.5, in1=dst, op0=ALU.mult, op1=ALU.add)
                    n = S.give(ins, "x_added", l, "out", i)
                    read("x_added", n, "out", l, i)
                dve.wait_ge(S.sem("x_added"), n)
                rms(("mlp", l), lambda k: ("g_mlp", l * KT + k), h, "h_ready")
                rb, hb = S.of("relued_base", l)[1], S.base("mlp_hidden")
                S.note(("mlp_hidden_base", l), "mlp_hidden", hb)
                with dve.Fori(0, MLP_CHUNKS // 4) as i:
                    for j in range(4):
                        dve.wait_ge(S.sem("relued"), i * 4 + (rb + j + 1))
                        dve.tensor_tensor(hid[:, 2 + j, :], hid[:, j % 2, :], hid[:, j % 2, :], ALU.mult)\
                           .then_inc(S.sem("mlp_hidden"), 1)
                S.base("mlp_hidden", hb + MLP_CHUNKS)
                S.wait(dve, "mlp_summed", l)
                for b in range(4):
                    dst = flat(x[:, 2 * b:2 * b + 2, :])
                    ins = dve.tensor_tensor(dst, dst, sums[b][:, :], ALU.add)
                give_link(ins, "x_added", l, "mlp")

            for l in range(LAYERS):
                block_1(l)

            def take_mod(i):
                bank = take(dve, "mod", i)
                b = prm("b_mod", 48 * i, 48).unsqueeze(2).to_broadcast([P, 48, 2])
                v = bank[:, 0:96].rearrange("p (t c) -> p t c", c=2)
                m = S.give(dve.tensor_tensor(mod[i][:, :, :], v, b, ALU.add), "dve_read")
                read("dve_read", m, "mod", i)
                dve.wait_ge(S.sem("dve_read"), m)
                for j in (1, 4):
                    ins = dve.tensor_scalar(mod[i][:, 8 * j:8 * j + 8, :], mod[i][:, 8 * j:8 * j + 8, :], 1.0, None, ALU.add)
                link(ins)

            def modv(i, j, k, c=0):
                return mod[i][:, 8 * j + k, c:c + 1]

            def modulate(dst, src, i, shift, scale, c=0):
                for k in range(KT):
                    ins = dve.tensor_scalar(dst[:, k, :], src[:, k, :], modv(i, scale, k, c), modv(i, shift, k, c),
                                            ALU.mult, ALU.add)
                return ins

            take_mod(0)
            take_mod(1)
            rms(("final",), lambda k: ("g_final", k), x, "x_normed")
            S.wait(dve, "x_normed", "final")
            S.give(modulate(h, x, 0, 0, 1), "h_ready", "mod", 0, 0)
            dve.wait_ge(S.sem("ctx_landed"), 16)
            S.give(modulate(scratch, scratch, 0, 0, 1, 1), "ctx_modulated", 0)
            dve.wait_ge(S.sem("consts2_landed"), 16)
            for hd in range(RET):
                link(dve.tensor_scalar(W2["decay"][:, hd, :], cst2("dist_f"), loggam[:, hd:hd + 1], None, ALU.mult))
                S.give(dve.scalar_tensor_tensor(out=W2["decay"][:, hd, :], in0=cst2("dist_b"),
                                                scalar=loggam[:, 4 + hd:5 + hd], in1=W2["decay"][:, hd, :],
                                                op0=ALU.mult, op1=ALU.add), "exponent", hd)
            for hd in range(RET):
                S.wait(dve, "decay_exps", hd)
                ins = dve.tensor_tensor(W2["decay"][:, hd, :], W2["decay"][:, hd, :], cst2("diag"), ALU.mult)
            link(ins)
            dve.wait_ge(S.sem("na_bias_landed"), 16)
            nb = W2["nbias"].rearrange("p h (e c) -> p (h e) c", c=GRID)
            m = cst("na_mask").unsqueeze(1).to_broadcast([P, 48, GRID])
            link(dve.tensor_tensor(nb, nb, m, ALU.add))
            for which in ("rk", "rq"):
                for i in range(2):
                    bank = take(dve, "swap", which, i)
                    src = B[which][:, 2 * i:2 * i + 2, :]
                    cos = cst2("axial_cos").unsqueeze(1).to_broadcast([P, 2, T])
                    sin = cst2("axial_sin").unsqueeze(1).to_broadcast([P, 2, T])
                    tmp = smax[:, 5, :].rearrange("p (a b) -> p a b", a=2)
                    m = S.give(dve.tensor_tensor(tmp, bank[:, :].rearrange("p (a b) -> p a b", a=2), sin, ALU.mult), "dve_read")
                    read("dve_read", m, "swap", which, i)
                    ins = dve.tensor_tensor(src, src, cos, ALU.mult)
                    link(ins)
                    give_link(dve.tensor_tensor(src, src, tmp, ALU.add), "rotated", which, i)
            S.wait(dve, "key_decays", 0)
            for d in range(2):
                for hd in range(RET):
                    S.wait(dve, "projected", "rvc", 1)
                    u = 4 * d + hd
                    if u >= 6:
                        S.wait(dve, "state_done", 0, u - 6)
                    kd = smax[:, u % 6, 0:2 * P].rearrange("p (t c) -> p t c", t=2)
                    for t in range(2):
                        ins = dve.tensor_scalar(kd[:, t, :], B["rkc"][:, t, hd * P:(hd + 1) * P],
                                                small[:, 96 + 2 * u + t:97 + 2 * u + t], None, ALU.mult)
                    S.give(ins, "keys_decayed", d, hd)
            S.wait(dve, "query_decays", 0)
            for d in range(2):
                for hd in range(RET):
                    v = W2["qd"][:, 4 * d + hd, :]
                    ins = dve.tensor_tensor(v, v, B["rq"][:, hd, :], ALU.mult)
            S.give(ins, "queries_decayed", 0)
            S.wait(dve, "filled", "state", 1)
            for hd in range(RET):
                bank = take(dve, "att", hd)
                at = smax[:, 2 + hd, :]
                dve.tensor_tensor(at[:, 0:T], bank[:, 0:T], W2["decay"][:, hd, P:3 * P], ALU.mult)
                ins = dve.tensor_tensor(at[:, T:2 * T], bank[:, T:2 * T], W2["decay"][:, hd, 0:T], ALU.mult)
                read("att_decayed", S.give(ins, "att_decayed", hd), "att", hd)
            o = B["rkc"].rearrange("p a (b t) -> p (a b) t", b=2)
            for i in range(2):
                bank = take(dve, "sum", "head", i)
                v = flat(o[:, 2 * i:2 * i + 2, :])
                ins = dve.scalar_tensor_tensor(out=v, in0=bank[:, :], scalar=-1.0 / P, in1=v, op0=ALU.mult, op1=ALU.add)
                m = S.give(ins, "dve_read")
                read("dve_read", m, "sum", "head", i)
                dve.wait_ge(S.sem("dve_read"), m)
                S.give(dve.tensor_tensor(flat(scratch[:, 2 * i:2 * i + 2, :]), v, v, ALU.mult), "squares", "head", i)
            for i in range(2):
                bank = take(dve, "sum2", "head", i)
                ins = dve.tensor_scalar(smax[:, 2 + i, :], bank[:, :], 1.0 / P, LN_EPS, ALU.mult, ALU.add)
                read("variance", S.give(ins, "variance", "head", i), "sum2", "head", i)
            for i in range(2):
                S.wait(dve, "root", "head", i)
                v, r = flat(o[:, 2 * i:2 * i + 2, :]), smax[:, 2 + i, :]
                link(dve.reciprocal(r, r))
                link(dve.tensor_tensor(v, v, r, ALU.mult))
                S.wait(dve, "projected", "rg", i)
                g = flat(B["rg"][:, 2 * i:2 * i + 2, :])
                ins = dve.tensor_tensor(g, g, v, ALU.mult)
            S.give(ins, "ret_ready", 0)
            for u in range(16 + 1):
                if u < 16:
                    hd, t = u // 2, u % 2
                    bank = take(dve, "s", "na", u)
                    st = 48 + u % 2 * 16
                    s = smax[:, u % 2, :]
                    e0 = 2 - 2 * t
                    dve.scalar_tensor_tensor(out=s[:, 0:T], in0=bank[:, 0:T], scalar=float(HD) ** -0.5,
                                             in1=W2["nbias"][:, hd, e0 * GRID:(e0 + 4) * GRID], op0=ALU.mult, op1=ALU.add)
                    ins = dve.tensor_scalar(s[:, T:2 * T], bank[:, T:2 * T], float(HD) ** -0.5, None, ALU.mult)
                    m = S.give(ins, "dve_read")
                    read("dve_read", m, "s", "na", u)
                    dve.wait_ge(S.sem("dve_read"), m)
                    link(dve.tensor_reduce(small[:, st:st + 1], s, AX.X, ALU.max))
                    S.give(dve.tensor_scalar(small[:, st:st + 1], small[:, st:st + 1], -1.0, None, ALU.mult), "row_max", "na", u)
                if u >= 1:
                    normalise("na", u - 1)

            def post_norm(i, s):
                tag = ("post", i, s)
                centre(tag, x, KT, D, ("sum", *tag))
                variance(tag, D, LN_EPS, ("sum2", *tag))
                inverse_root(tag)
                for k in range(KT):
                    ins = dve.scalar_tensor_tensor(out=x[:, k, :], in0=x[:, k, :], scalar=prm("ln_g", (2 * i + s) * KT + k),
                                                   in1=stat[:, 1, 0:T], op0=ALU.mult, op1=ALU.mult)
                link(ins)
                for k in range(KT):
                    ins = dve.tensor_scalar(x[:, k, :], x[:, k, :], prm("ln_b", (2 * i + s) * KT + k), None, ALU.add)
                give_link(ins, "x_normed", *tag)

            def residual(i, s, j, bank_for, kind, gate=None):
                v = flat(x[:, :, :])
                link(dve.tensor_scalar(v, v, float(ALPHA), None, ALU.mult))
                for b in range(4):
                    bank, fill = bank_for(b)
                    for q in range(2):
                        k = 2 * b + q
                        g = gate(k) if gate else modv(i, j, k)
                        ins = dve.scalar_tensor_tensor(out=x[:, k, :], in0=bank[:, q * T:(q + 1) * T], scalar=g,
                                                       in1=x[:, k, :], op0=ALU.mult, op1=ALU.add)
                    if b == 3:
                        n = S.give(ins, "added", i, s)
                        kind = "added"
                    else:
                        n = S.give(ins, "dve_read")
                        kind = "dve_read"
                    if fill:
                        read(kind, n, *fill)
                dve.wait_ge(S.sem("added"), S.count["added"])

            def ab_bank(b):
                fill = ("ab_out", b)
                return take(dve, *fill), fill

            residual(0, 0, 2, ab_bank, None)
            post_norm(0, 0)

            def one_hot(dst, vals, top, rank, tmp, tmp1, n):
                link(dve.tensor_reduce(top, vals, AX.X, ALU.max))
                link(dve.tensor_tensor(tmp, vals, top.unsqueeze(2).to_broadcast([P, 2, n]), ALU.is_ge))
                link(dve.tensor_tensor(tmp, tmp, rank, ALU.mult))
                link(dve.tensor_reduce(tmp1, tmp, AX.X, ALU.max))
                link(dve.tensor_tensor(dst, tmp, tmp1.unsqueeze(2).to_broadcast([P, 2, n]), ALU.is_equal))

            def route(i):
                r = smax[:, 2, :]

                def piece(a, *dims):
                    v = r[:, a:a + int(np.prod(dims))]
                    return v.rearrange("p (a b) -> p a b", a=dims[0]) if len(dims) == 2 else v

                lg, tmp4, oh4 = piece(0, 2, 36), piece(72, 2, 4), piece(80, 2, 4)
                m4, c4, gate = piece(88, 2), piece(90, 2), piece(92, 2)
                le, tmp8, oh1, oh2 = piece(96, 2, 8), piece(112, 2, 8), piece(128, 2, 8), piece(144, 2, 8)
                m1, m2, c1, w1, w2 = piece(160, 2), piece(162, 2), piece(164, 2), piece(166, 2), piece(168, 2)
                prod = r[:, 192:256].rearrange("p (t g e) -> p t g e", t=2, g=4)
                bank = take(dve, "router", i)
                for t in range(2):
                    ins = dve.tensor_tensor(lg[:, t, :], bank[:, t * 64:t * 64 + 36], prm("b_router", 36 * i, 36), ALU.add)
                m = S.give(ins, "dve_read")
                read("dve_read", m, "router", i)
                dve.wait_ge(S.sem("dve_read"), m)
                g = lg[:, :, 0:4]
                one_hot(oh4, g, m4, cst("rank4").rearrange("p (a b) -> p a b", a=2), tmp4, c4, GROUPS)
                S.give(dve.tensor_tensor(small[:, 0:8].rearrange("p (a b) -> p a b", a=2), g,
                                         m4.unsqueeze(2).to_broadcast([P, 2, 4]), ALU.subtract), "router_shifted", i)
                for t in range(2):
                    ins = dve.tensor_tensor(prod[:, t], lg[:, t, 4:36].rearrange("p (g e) -> p g e", g=4),
                                            oh4[:, t].unsqueeze(2).to_broadcast([P, 4, 8]), ALU.mult)
                link(ins)
                link(dve.tensor_reduce(le, prod.rearrange("p t g e -> p t e g"), AX.X, ALU.add))
                rank8 = cst("rank8").rearrange("p (a b) -> p a b", a=2)
                one_hot(oh1, le, m1, rank8, tmp8, c1, PER_GROUP)
                link(dve.scalar_tensor_tensor(out=le, in0=oh1, scalar=-3e38, in1=le, op0=ALU.mult, op1=ALU.add))
                one_hot(oh2, le, m2, rank8, tmp8, c1, PER_GROUP)
                S.give(dve.tensor_tensor(small[:, 8:10], m2, m1, ALU.subtract), "top_shifted", i)
                link(dve.tensor_tensor(tmp8, oh1, oh2, ALU.add))
                by_group = "p (g e) -> p g e"
                for t in range(2):
                    ins = dve.tensor_tensor(member[:, t, :].rearrange(by_group, g=4),
                                            tmp8[:, t].unsqueeze(1).to_broadcast([P, 4, 8]),
                                            oh4[:, t].unsqueeze(2).to_broadcast([P, 4, 8]), ALU.mult)
                give_link(ins, "members", i)
                S.wait(dve, "router_exps", i)
                link(dve.tensor_reduce(gate, small[:, 0:8].rearrange("p (a b) -> p a b", a=2), AX.X, ALU.add))
                S.wait(dve, "top_exps", i)
                link(dve.tensor_scalar(w1, small[:, 8:10], 1.0, None, ALU.add))
                link(dve.tensor_tensor(w1, w1, gate, ALU.mult))
                link(dve.reciprocal(w1, w1))
                link(dve.tensor_tensor(w2, w1, small[:, 8:10], ALU.mult))
                link(dve.tensor_tensor(oh1, oh1, w1.unsqueeze(2).to_broadcast([P, 2, 8]), ALU.mult))
                link(dve.tensor_tensor(oh2, oh2, w2.unsqueeze(2).to_broadcast([P, 2, 8]), ALU.mult))
                link(dve.tensor_tensor(oh1, oh1, oh2, ALU.add))
                for t in range(2):
                    ins = dve.tensor_tensor(weight_of[:, t, :].rearrange(by_group, g=4),
                                            oh1[:, t].unsqueeze(1).to_broadcast([P, 4, 8]),
                                            oh4[:, t].unsqueeze(2).to_broadcast([P, 4, 8]), ALU.mult)
                link(ins)
                bank = take(dve, "rank", i)
                dve.scalar_tensor_tensor(out=flat2(rank), in0=bank[:, 0:64], scalar=1.0, in1=flat2(member),
                                         op0=ALU.add, op1=ALU.mult)
                fullest, more = small[:, 10:11], small[:, 12:14]
                n = S.give(dve.tensor_reduce(fullest, bank[:, 64:96], AX.X, ALU.max), "dve_read")
                read("dve_read", n, "rank", i)
                dve.wait_ge(S.sem("dve_read"), n)
                link(dve.tensor_scalar(flat2(rank), flat2(rank), -1.0, None, ALU.add))
                link(dve.tensor_scalar(small[:, 16:16 + MAX_ROUNDS], cst("full"), fullest, None, ALU.is_lt))
                link(dve.tensor_reduce(more[:, 0:1], small[:, 16:16 + MAX_ROUNDS], AX.X, ALU.add))
                link(dve.tensor_scalar(more[:, 0:1], more[:, 0:1], 1.0, None, ALU.max))
                link(dve.tensor_scalar(more[:, 1:2], more[:, 0:1], -1.0, None, ALU.add))
                give_link(dve.tensor_copy(rounds_i[:, :], more), "rounds", i)

            def moe(i):
                S.give(modulate(h, x, i, 3, 4), "h_ready", "mod", i, 1)
                route(i)
                with dve.Fori(0, rounds_of(dve, i)) as rnd:
                    with dve.Fori(0, TURNS) as g:
                        it = rnd * TURNS + g
                        four = [P, GROUP_OF, SLOTS]
                        for t in range(2):
                            ranks = rank[:, t, bass.ds(g * 4, 4)].unsqueeze(2).to_broadcast(four)
                            ins = dve.tensor_tensor(M["place"][:, t, :].rearrange("p (e s) -> p e s", e=GROUP_OF),
                                                    cst("slot_no").unsqueeze(1).to_broadcast(four), ranks, ALU.is_equal)
                        ins.then_inc(S.sem(f"moe{i}_placed"), 1)
                        dve.wait_ge(S.sem(f"moe{i}_placed"), it + 1)
                        twice = [P, GROUP_OF, 2, SLOTS]
                        for t in range(2):
                            w = weight_of[:, t, bass.ds(g * 4, 4)].unsqueeze(2).unsqueeze(3).to_broadcast(twice)
                            place = M["place"][:, t, :].rearrange("p (e s) -> p e s", e=GROUP_OF).unsqueeze(2)
                            dve.tensor_tensor(M["weighted"][:, t, :].rearrange("p (e a s) -> p e a s", e=GROUP_OF, a=2),
                                              place.to_broadcast(twice), w, ALU.mult)
                        for e in range(GROUP_OF):
                            dve.wait_ge(S.sem(f"moe{i}_silued"), it * 4 + (e + 1))
                            dve.tensor_tensor(M["hidden"], banks[0][:, T:2 * T], M["silu"], ALU.mult)\
                               .then_inc(S.sem(f"moe{i}_hidden"), 1)
                            dve.wait_ge(S.sem(f"moe{i}_down_done"), it * 4 + (e + 3))
                            dve.tensor_copy(M["y"], banks[2][:, :]).then_inc(S.sem(f"moe{i}_y_kept"), 1)
                    dve.tensor_scalar(flat2(rank), flat2(rank), -float(SLOTS), None, ALU.add)\
                       .then_inc(S.sem(f"moe{i}_ranks_left"), 1)
                    dve.wait_ge(S.sem(f"moe{i}_ranks_left"), rnd + 1)
                S.wait(dve, "moe_summed", i)
                residual(i, 1, 5, lambda b: (sums[b], None), None)
                post_norm(i, 1)

            moe(0)
            S.give(modulate(h, x, 1, 0, 1), "h_ready", "mod", 1, 0)
            S.wait(dve, "h_ready", "mod", 1, 0)
            S.wait(dve, "pad_zeroed", "pool")
            dve.wait_ge(S.sem("counts_landed"), 16)
            pad = PL["pad"][:, 0, :]
            for k in range(KT):
                g = k // 2
                link(dve.tensor_copy(pad[:, 8:8 + T], h[:, k, :]))
                cur, at, left, right = pad, 8, 1, 0
                lo, hi = 0, T + 16
                for level in range(g + 1):
                    half = POOL_SIZES[level] // 2
                    left, right = (1, 0) if level == 0 else (half // 2, half // 2)
                    nxt = PL["lvl"][:, level % 2, :]
                    lo, hi = lo + left, hi - right
                    link(dve.tensor_tensor(nxt[:, lo:hi], cur[:, lo - left:hi - left], cur[:, lo + right:hi + right], ALU.add))
                    cur = nxt
                link(dve.tensor_tensor(cur[:, 8:8 + T], cur[:, 8:8 + T], PL["counts"][:, g, :], ALU.mult))
                ins = dve.tensor_tensor(PL["z"][:, k, :], cur[:, 8:8 + T], h[:, k, :], ALU.subtract)
                if k % 2 == 1:
                    S.give(ins, "pooled", g)
            for k in range(KT):
                ins = dve.tensor_tensor(small[:, 8 + k:9 + k], prm("pool_scale", k), modv(1, 2, k), ALU.mult)
            link(ins)

            def pool_bank(b):
                fill = ("pool", b)
                return take(dve, *fill), fill

            residual(1, 0, 2, pool_bank, None, gate=lambda k: small[:, 8 + k:9 + k])
            post_norm(1, 0)
            moe(1)
    return S


def sink_of(u):
    j = u - HEADS
    return j // 2 + 4 * (j % 2)


def by_partition(w):
    return w.reshape(w.shape[0] // P, P, w.shape[1]).transpose(1, 0, 2)


def pack_weights(a):
    out = np.zeros((N_CHUNKS, P, CW), np.float32)

    def put(n, v, at=0):
        v = v.reshape(P, -1)
        out[n, :, at:at + v.shape[1]] = v

    r = np.arange
    for l in range(LAYERS):
        w = by_partition(a["w_in"][l])
        pe = 2176 + r(32)
        tiles = []
        for j in range(4):
            tiles.append(np.concatenate([j * 64 + r(64), (j + 4) * 64 + r(64)]))
        tiles += [512 + r(128), 640 + r(128), 1792 + r(128), 1920 + r(128), 2048 + r(128), None,
                  np.tile(pe, 4), np.tile(np.concatenate([pe[16:], pe[:16]]), 4)]
        for j in range(4):
            tiles += [768 + 128 * j + r(128), 1280 + 128 * j + r(128)]
        tiles += [2208 + 128 * j + r(128) for j in range(24)]
        for i, cols in enumerate(tiles):
            if cols is not None:
                v = out[chunk_in(l, i // 2)].reshape(P, KT, 512)
                v[:, :, (i % 4) * P:(i % 4 + 1) * P] = w[:, :, cols]
        q = by_partition(a["w_q_up"][l]).reshape(P, 2, HEADS, NOPE + ROPE)
        qr = q[:, :, (0, 2, 1, 3, 4, 6, 5, 7), NOPE:]
        q = np.concatenate([q[..., :NOPE].reshape(P, 2, 512), qr.reshape(P, 2, 256),
                            np.concatenate([qr[..., 16:], qr[..., :16]], -1).reshape(P, 2, 256)], axis=2)
        kv = a["w_kv_up"][l].reshape(P, HEADS, 128)
        put(chunk_latent(l), q)
        put(chunk_latent(l), kv[..., :64], 2048)
        put(chunk_latent(l), kv[..., 64:], 2560)
        for n in range(3):
            w = a["w_branch"][l, n]
            if n == 0:
                w = w[np.concatenate(tiles[:4])]
            put(chunk_branch(l, BRANCH_ORDER.index(n)), by_partition(w))
        w = by_partition(a["w_out"][l])
        for half in range(2):
            put(chunk_out(l, half), w[:, :, 512 * half:512 * half + 512])
        up, down = by_partition(a["w_up"][l]), by_partition(a["w_down"][l])
        for c in range(MLP_CHUNKS):
            put(chunk_mlp(l) + c, up[:, :, 256 * c:256 * c + 256])
            put(chunk_mlp(l) + c, down[:, 2 * c:2 * c + 2, :], 2048)
    for i in range(2):
        w = by_partition(a["w_mod_2"][i])
        for c in range(MOD_CHUNKS):
            put(C_MOD + MOD_CHUNKS * i + c, w[:, :, 512 * c:512 * c + 512])
    w = by_partition(a["ab_w_in_2"][0])
    order = [0, 512, 1024, 1536, 2048, 2560, 3072]
    for c, at in enumerate(order):
        put(C_AB + c, w[:, :, at:at + 512])
    w = by_partition(a["ab_w_out_2"][0])
    for half in range(2):
        put(C_ABOUT + half, w[:, :, 512 * half:512 * half + 512])
    put(C_POOL, a["pool_w_2"][0].reshape(4, 2, P, 256).transpose(2, 0, 1, 3))
    return out


def pack_experts(a):
    out = np.empty((2, EXPERTS, EXPERT_CHUNKS, P, CW), np.float32)
    up = out[:, :, 0:2].reshape(2, EXPERTS, 2, P, 4, 2, 2, 256)
    for j, name in enumerate(("moe_w_gate_2", "moe_w_up_2")):
        w = a[name].reshape(2, EXPERTS, 2, 4, P, 2, 256)
        up[:, :, :, :, :, :, j, :] = w.transpose(0, 1, 2, 4, 3, 5, 6)
    out[:, :, 0:2] = up.reshape(2, EXPERTS, 2, P, CW)
    out[:, :, 2] = a["moe_w_down_2"].reshape(2, EXPERTS, 4, P, D).transpose(0, 1, 3, 2, 4).reshape(2, EXPERTS, P, CW)
    return out.reshape(2 * EXPERTS * EXPERT_CHUNKS, P, CW)


def pack_params(a):
    out = np.zeros((P, N_PARAM), np.float32)

    def put(name, v):
        i, j = PARAM[name]
        out[:, i:j] = v

    def cols(v):
        return v.reshape(-1, P).T

    for name, key in (("g_final", "g_final"), ("g_mix", "g_mix"), ("g_mlp", "g_mlp"), ("g_q", "g_q_norm"),
                      ("g_kv", "g_kv_norm"), ("b_dw", "b_dw"), ("g_conv", "g_conv_ln"), ("b_conv", "b_conv_ln"),
                      ("b_mod", "b_mod_2"), ("ln_g", "ln_g_2"), ("ln_b", "ln_b_2"), ("pool_scale", "pool_scale_2")):
        put(name, cols(a[key]))
    put("w_dw", a["w_dw"][:, :, 0, :].reshape(2, TAPS, CT, P).transpose(3, 0, 2, 1).reshape(P, -1))
    cond = np.stack([cols(a["c_2"][0]), cols(a["c_ctx_2"])], axis=2)
    put("cond", cond.reshape(P, -1))
    for name, key in (("sinks", "swa_sinks"), ("rel_bias", "rel_bias"), ("log_decay", "ab_log_decay_2")):
        put(name, a[key].reshape(1, -1))
    put("b_router", np.concatenate([a["moe_b_r1_2"], a["moe_b_r2_2"].reshape(2, 32)], axis=1).reshape(1, -1))
    w = np.concatenate([a["moe_w_r1_2"], a["moe_w_r2_2"].transpose(0, 2, 1, 3).reshape(2, D, 32)], axis=2)
    put("w_router", w.reshape(2, KT, P, 36).transpose(2, 0, 1, 3).reshape(P, -1))
    return out


def pack_neighbour_bias(rpb):
    out = np.zeros((P, HEADS, 6, GRID), np.float32)
    for p in range(P):
        half, qc = p // GRID, p % GRID
        lo, hi = max(0, qc - 15), min(GRID, qc + 16)
        out[p, :, :, lo:hi] = rpb[:, 5 - half:11 - half, lo - qc + 15:hi - qc + 15]
    return out.reshape(P, HEADS, 6 * GRID)


def layout(inputs):
    a = {k: np.asarray(v) for k, v in inputs.items()}
    pos = a["positions"].reshape(T)
    positions = np.concatenate([np.tile(pos[None, :], (P, 1)), pos.reshape(2, P).T], axis=1)
    c, c2, counts = shape_constants()
    return {
        "stream": pack_weights(a),
        "experts": pack_experts(a),
        "tokens": by_partition(a["x"][0].T),
        "ctx_tokens": by_partition(a["ctx_2"][0].T),
        "params": pack_params(a),
        "consts": c,
        "consts2": c2,
        "pool_counts": counts,
        "positions": positions,
        "na_bias": pack_neighbour_bias(a["ab_rpb_2"][0]),
    }


def program(nc, shapes):
    ins = {}
    for name, (shape, dtype) in shapes.items():
        ins[name] = nc.dram_tensor(f"in_{name}", shape, mybir.dt.from_np(dtype), kind="ExternalInput").ap()
    out = nc.dram_tensor("out_x", [P, KT, T], F32, kind="ExternalOutput").ap()
    return ins, out


def kernel(**inputs):
    import concourse.bacc as bacc
    from concourse.bass_utils import run_bass_kernel_spmd

    arrays = {k: np.ascontiguousarray(v) for k, v in layout(inputs).items()}
    shapes = {k: (v.shape, v.dtype) for k, v in arrays.items()}
    counted = {}
    for _ in range(2):
        nc = bacc.Bacc("TRN2", target_bir_lowering=False, num_devices=1)
        ins, out = program(nc, shapes)
        counted = two_blocks_kernel(nc, **ins, out=out, counted=counted).at
    r = run_bass_kernel_spmd(nc, [{f"in_{k}": v for k, v in arrays.items()}], core_ids=[0])
    y = r.results[0]["out_x"]
    return y.transpose(2, 1, 0).reshape(1, T, D)
```

```python
from contextlib import ExitStack

import numpy as np
import concourse.bass as bass
from concourse import mybir

F32 = mybir.dt.float32
F32R = mybir.dt.float32r
I32 = mybir.dt.int32
ALU = mybir.AluOpType
ACT = mybir.ActivationFunctionType
AX = mybir.AxisListType

P = 128
T = 256
D = 1024
KT = D // P
LAYERS = 2
HEADS = 8
HD = 64
EPS = 1e-6
LN_EPS = 1e-5
ALPHA = (2 * LAYERS) ** 0.25
NEG = -1e30
TAPS = 31
CT = 4
QR, KVR = 256, 128
NOPE, ROPE = 64, 32
N_BUCKETS = 32
EXPERTS, GROUPS, PER_GROUP = 32, 4, 8
RET = 4
GRID = 64
POOL_SIZES = (2, 4, 8, 16)

CW = 4096
RING = 4
MLP_CHUNKS = 16
MOD_CHUNKS = 12
AB_CHUNKS = 7
GATE_UNITS = {u: 12 + i for i, u in enumerate((0, 1, 2, 3, 4, 6, 8, 10, 12, 14))}
MOD_UNITS = {u: i for i, u in enumerate((1, 3, 5, 7, 9, 11, 13, 15, 16, 17))}


def layer_order():
    order = [("in", c) for c in range(6)] + [("latent", 0)]
    for u in range(18):
        if GATE_UNITS.get(u, 1) % 2 == 0:
            order.append(("in", GATE_UNITS[u] // 2))
        if u in MOD_UNITS:
            order.append(("mod", MOD_UNITS[u]))
    order += [("branch", 0), ("mod", 10), ("branch", 1), ("mod", 11), ("branch", 2), ("out", 0), ("out", 1)]
    return order + [("mlp", c) for c in range(MLP_CHUNKS)]


PLACE = {what: n for n, what in enumerate(layer_order())}
LAYER_CHUNKS = len(PLACE)
C_AB = LAYERS * LAYER_CHUNKS
C_ABOUT = C_AB + AB_CHUNKS
C_POOL = C_ABOUT + 2
N_CHUNKS = C_POOL + 1
EXPERT_CHUNKS = 3
GROUP_OF = 4
TURNS = EXPERTS // GROUP_OF
SLOTS = 64
MAX_ROUNDS = T // SLOTS


def chunk_of(layer, what, n=0):
    return LAYER_CHUNKS * layer + PLACE[what, n]


def chunk_in(layer, pair):
    return chunk_of(layer, "in", pair // 2)


def chunk_mlp(layer):
    return chunk_of(layer, "mlp")


BRANCH_ORDER = (0, 2, 1)



def columns(spec):
    at, out = 0, {}
    for name, n in spec:
        out[name] = (at, at + n)
        at += n
    return out, at


PARAM, N_PARAM = columns([
    ("g_final", KT), ("g_mix", 2 * KT), ("g_mlp", 2 * KT), ("g_q", 2 * 2), ("g_kv", 2),
    ("w_dw", 2 * CT * TAPS), ("b_dw", 2 * CT), ("g_conv", 2 * CT), ("b_conv", 2 * CT),
    ("cond", KT * 2), ("b_mod", 2 * 48), ("ln_g", 4 * KT), ("ln_b", 4 * KT), ("pool_scale", KT),
    ("sinks", 2 * HEADS), ("rel_bias", N_BUCKETS * HEADS), ("log_decay", 2 * RET),
    ("b_router", 2 * 36), ("w_router", 2 * KT * 36)])

CONST, N_CONST = columns([
    ("ident", P), ("ones", P), ("mask_cur", P), ("mask_prev", P), ("lower", P),
    ("swap64", P), ("before", P), ("slot_no", SLOTS), ("full", MAX_ROUNDS), ("na_mask", GRID), ("rope_freq", 1), ("rope_sign", 1), ("sum4", 2), ("left_f", 2), ("left_b", 2),
    ("rank4", 2 * GROUPS), ("rank8", 2 * PER_GROUP)])

CONST2, N_CONST2 = columns([
    ("dist_f", 384), ("dist_b", 384), ("diag", 384), ("dec_f", T), ("dec_b", T),
    ("axial_cos", T), ("axial_sin", T)])


def bucket_thresholds():
    n = np.arange(0, 4096)
    nf = np.maximum(n, 16).astype(np.float32)
    large = 16 + (np.log(nf / np.float32(16)) / np.float32(np.log(8.0)) * np.float32(16)).astype(np.int32)
    b = np.where(n < 16, n, np.minimum(large, 31))
    return [int(np.argmax(b >= k)) for k in range(1, N_BUCKETS)]


def shape_constants():
    p = np.arange(P)
    c = np.zeros((P, N_CONST), np.float32)

    def put(name, v):
        a, b = CONST[name]
        c[:, a:b] = v

    put("ident", np.eye(P))
    put("ones", 1.0)
    put("mask_cur", np.where(p[None, :] <= p[:, None], 0.0, NEG))
    put("mask_prev", np.where(p[None, :] > p[:, None], 0.0, NEG))
    put("lower", p[None, :] <= p[:, None])
    put("before", p[:, None] < p[None, :])
    put("slot_no", np.arange(SLOTS)[None, :])
    put("full", SLOTS * np.arange(MAX_ROUNDS)[None, :])
    put("swap64", (p[:, None] + 64) % P == p[None, :])
    qc, kc = (p % GRID)[:, None], np.arange(GRID)[None, :]
    w0 = np.clip(qc - 8, 0, GRID - 16)
    put("na_mask", np.where((kc >= w0) & (kc < w0 + 16), 0.0, NEG))
    freq = np.exp(np.float32(-np.log(10000.0)) * np.arange(16, dtype=np.float32) / np.float32(16))
    put("rope_freq", freq[p % 16][:, None])
    put("rope_sign", np.where(p % 32 < 16, -1.0, 1.0)[:, None])
    token = p[:, None] + P * np.arange(2)[None, :]
    put("sum4", p[:, None] % 32 == np.arange(2)[None, :])
    put("left_f", T - 1 - token)
    put("left_b", token)
    put("rank4", np.tile(np.arange(GROUPS, 0, -1), 2)[None, :])
    put("rank8", np.tile(np.arange(PER_GROUP, 0, -1), 2)[None, :])

    c2 = np.zeros((P, N_CONST2), np.float32)

    def put2(name, v):
        a, b = CONST2[name]
        c2[:, a:b] = v

    d = (np.arange(384)[None, :] - P) - p[:, None]
    put2("dist_f", np.maximum(d, 0))
    put2("dist_b", np.maximum(-d, 0))
    put2("diag", 1.0 + (d == 0))
    put2("dec_f", np.arange(T)[None, :] + 1)
    put2("dec_b", T - np.arange(T)[None, :])
    t = np.arange(T)
    inv = np.float32(10000.0) ** (-np.arange(32, dtype=np.float32) / np.float32(32))
    ang = np.concatenate([(t // GRID).astype(np.float32)[:, None] * inv,
                          (t % GRID).astype(np.float32)[:, None] * inv], axis=1)
    cos, sin = np.cos(ang).T, np.sin(ang).T
    put2("axial_cos", np.concatenate([cos, cos]))
    put2("axial_sin", np.concatenate([-sin, sin]))

    counts = np.zeros((P, 4, T), np.float32)
    for g, w in enumerate(POOL_SIZES):
        lo, hi = np.clip(t - w // 2, 0, T), np.clip(t + w - w // 2, 0, T)
        counts[:, g] = 1.0 / (hi - lo)
    return c, c2, counts.reshape(P, 4 * T)


class Signals:

    def __init__(self, nc, stack, counted):
        self.nc, self.stack, self.counted = nc, stack, counted
        self.sems, self.count, self.at = {}, {}, {}
        self.engine, self.owner = None, {}

    def sem(self, kind):
        if kind not in self.sems:
            self.sems[kind] = self.stack.enter_context(self.nc.semaphore(kind))
        return self.sems[kind]

    def give(self, ins, kind, *key):
        assert self.owner.setdefault(kind, self.engine) == self.engine, f"{kind}: one engine raises a semaphore"
        self.count[kind] = self.count.get(kind, 0) + 1
        if key:
            self.at[(kind, *key)] = (kind, self.count[kind])
        ins.then_inc(self.sem(kind), 1)
        return self.count[kind]

    def note(self, event, kind, value):
        self.at[event] = (kind, value)

    def of(self, *event):
        if self.counted:
            return self.counted[event]
        return self.at.get(event, ("not_counted_yet", 1))

    def wait(self, eng, *event):
        kind, value = self.of(*event)
        eng.wait_ge(self.sem(kind), value)

    def base(self, kind, value=None):
        if value is not None:
            self.count[kind] = value
        return self.count.get(kind, 0)


def two_blocks_kernel(nc, stream, experts, tokens, ctx_tokens, params, consts, consts2, pool_counts, positions,
                      na_bias, out, counted):
    stack = ExitStack()
    with stack:
        def sb(name, shape, dt=F32):
            return stack.enter_context(nc.sbuf_tensor(name, shape, dt))

        S = Signals(nc, stack, counted)

        shared = {"ring": [P, RING, CW], "h": [P, KT, T], "scratch": [P, KT, T], "arena": [P, 14464], "smax": [P, 6, 512]}
        with ExitStack() as first_names:
            whole = {n: first_names.enter_context(nc.sbuf_tensor(n, v, F32)) for n, v in shared.items()}
        split = {n: sb(f"{n}_split", v, F32R) for n, v in shared.items()}
        ring = whole["ring"]
        x = sb("x", [P, KT, T])
        h = whole["h"]
        scratch = whole["scratch"]
        wide = sb("wide", [P, 8192])
        arena = whole["arena"]
        smax = whole["smax"]
        stat = sb("stat", [P, 2, 512])
        small = sb("small", [P, 384])
        par = sb("par", [P, N_PARAM])
        con = sb("con", [P, N_CONST])
        pos_i = sb("pos_i", [P, T + 2], I32)
        banks = [stack.enter_context(nc.psum_tensor(f"bank{i}", [P, 512], F32)) for i in range(4)]
        sums = [stack.enter_context(nc.psum_tensor(f"sums{i}", [P, 512], F32)) for i in range(4)]

        def prm(name, i=0, n=1):
            a = PARAM[name][0] + i
            return par[:, a:a + n]

        def cst(name, i=0, n=None):
            a, b = CONST[name]
            return con[:, a + i:(b if n is None else a + i + n)]

        ident, ones = cst("ident"), cst("ones")

        def carve(tensor, spec):
            at, views = 0, {}
            for name, *dims in spec:
                n = int(np.prod(dims))
                v = tensor[:, at:at + n]
                if len(dims) > 1:
                    v = v.rearrange("p (a b) -> p a b", a=dims[0])
                views[name] = v
                at += n
            return views

        A = carve(arena, [("qa", 4, T), ("ka", T), ("va", 2, P), ("cq", 2, T), ("ckv", T), ("qn", 4, T),
                          ("qp", 2, T), ("kn", 4, T), ("kp", T), ("vc", 2, 512),
                          ("conv", CT, T), ("ya", 4, T), ("yc", 4, T), ("u", CT, 30 + T), ("cos", T), ("sin", T),
                          ("away", 2, P), ("halfw", CT * TAPS), ("delta", N_BUCKETS * HEADS), ("pk", T),
                          ("mod_rows", 2, 512)])
        HI = carve(split["arena"], [("up", 2, CW // 2), ("down", 2, CW // 2)])
        B = carve(arena, [("rq", 4, T), ("rk", 4, T), ("rv", 2, 512), ("nq", 4, T), ("nk", 4, T),
                          ("nv", 2, 512), ("rg", 4, T), ("rkc", 2, 512), ("rvc", 2, 512), ("nkc", 4, T),
                          ("nvc", 2, 512), ("yn", 4, T), ("con2", N_CONST2)])
        PL = carve(arena, [("pad", 1, T + 16), ("lvl", 2, T + 16), ("z", KT, T), ("counts", 4, T)])
        gates = wide[:, 0:24 * T].rearrange("p (a b) -> p a b", a=24)
        wbias = wide[:, 24 * T:32 * T].rearrange("p (h a b) -> p h a b", h=HEADS, a=2)
        W2 = carve(wide, [("nbias", HEADS, 6 * GRID), ("decay", RET, 384), ("qd", 8, T), ("state", 8, P)])
        M = carve(wide, [("by_token", 2, D), ("gathered", KT, GROUP_OF * SLOTS), ("place", 2, GROUP_OF * SLOTS),
                         ("weighted", 2, GROUP_OF * 2 * SLOTS), ("turned", 512), ("y", 512), ("silu", T), ("hidden", T)])
        weight_of = smax[:, 0, 0:64].rearrange("p (t e) -> p t e", t=2)
        member = smax[:, 0, 64:128].rearrange("p (t e) -> p t e", t=2)
        rank = smax[:, 0, 128:192].rearrange("p (t e) -> p t e", t=2)
        rounds_i = sb("rounds", [P, 2], I32)
        hid = smax

        def flat2(v):
            return v.rearrange("p a b -> p (a b)")

        def rounds_of(eng, i):
            S.wait(eng, "rounds", i)
            return eng.value_load(rounds_i[0:1, 0:1], min_val=1, max_val=MAX_ROUNDS)

        def cst2(name):
            a, b = CONST2[name]
            return B["con2"][:, a:b]

        mod = [sb(f"mod{i}", [P, 48, 2]) for i in range(2)]
        loggam = small[:, 0:8]
        cond = sb("cond", [P, KT, 32])

        block = stack.enter_context(nc.Block())

        fills = {"n": 0, "free": [None] * 4}

        def bank_of(*fill):
            kind_bank = S.of("bank", *fill)
            return banks[kind_bank[1] % 4]

        def open_bank(pe, *fill):
            b = fills["n"] % 4
            last = fills["free"][b]
            if last is not None:
                S.wait(pe, "read", *last)
            S.note(("bank", *fill), "bank", b)
            fills["free"][b] = fill
            fills["n"] += 1
            return banks[b]

        def filled(ins, *fill):
            S.give(ins, "filled", *fill)

        def take(eng, *fill):
            S.wait(eng, "filled", *fill)
            return bank_of(*fill)

        def read(kind, value, *fill):
            S.note(("read", *fill), kind, value)

        @block.sync
        def _(sp):
            S.engine = "sync"

            def load_chunk(n, frees=None):
                if n >= RING:
                    S.wait(sp, "chunk_used", n - RING)
                if n == C_POOL:
                    S.wait(sp, "moe_summed", 0)
                sp.dma_start(ring[:, n % RING, :], stream[n]).then_inc(S.sem(f"slot_landed{n % RING}"), 16)

            def load_experts(i):
                S.wait(sp, "chunk_used", C_POOL - 1 if i == 0 else C_POOL)

                def turn(it, turn_no):
                    for q in range(EXPERT_CHUNKS * GROUP_OF):
                        e, t = q // EXPERT_CHUNKS, q % EXPERT_CHUNKS
                        if t == 0:
                            sp.wait_ge(S.sem(f"moe{i}_down_done"), it * 4 + (e + 1))
                        else:
                            sp.wait_ge(S.sem(f"moe{i}_up_done"), it * 4 + (e + 2))
                        n = i * EXPERTS * EXPERT_CHUNKS + q
                        src = experts[bass.ds(turn_no * 12 + n, 1), :, :].rearrange("a p c -> p (a c)")
                        sp.dma_start(ring[:, q % RING, :], src).then_inc(S.sem(f"moe{i}_landed{q % RING}"), 16)

                turn(0, 0)
                with sp.Fori(1, TURNS) as g:
                    turn(g, g)
                S.wait(sp, "rounds", i)
                more = sp.value_load(rounds_i[0:1, 1:2], min_val=0, max_val=MAX_ROUNDS - 1)
                with sp.If(more > 0):
                    with sp.Fori(0, more) as rnd:
                        with sp.Fori(0, TURNS) as g:
                            turn(rnd * TURNS + g + TURNS, g)

            sp.dma_start(con[:, :], consts).then_inc(S.sem("consts_landed"), 16)
            sp.dma_start(x[:, :, :], tokens).then_inc(S.sem("tokens_landed"), 16)
            sp.dma_start(par[:, :], params).then_inc(S.sem("params_landed"), 16)
            n = 0
            while n < N_CHUNKS:
                mlp = [l for l in range(LAYERS) if n == chunk_mlp(l) + RING]
                if n == C_POOL:
                    load_experts(0)
                if mlp:
                    kind, done = S.of("mlp_done_base", mlp[0])
                    with sp.Fori(0, MLP_CHUNKS // 4 - 1) as i:
                        for j in range(4):
                            sp.wait_ge(S.sem("mlp_chunk_done"), i * 4 + (done + j + 1))
                            src = stream[bass.ds(i * 4 + (n + j), 1), :, :].rearrange("a p c -> p (a c)")
                            sp.dma_start(ring[:, (n + j) % RING, :], src)\
                              .then_inc(S.sem(f"slot_landed{(n + j) % RING}"), 16)
                    n += MLP_CHUNKS - RING
                else:
                    load_chunk(n)
                    n += 1
            load_experts(1)
            S.wait(sp, "x_normed", "post", 1, 1)
            sp.dma_start(out, x[:, :, :]).then_inc(S.sem("stored"), 16)
            sp.wait_ge(S.sem("stored"), 16)

        @block.gpsimd
        def _(pool):
            S.engine = "gpsimd"

            pool.dma_start(pos_i[:, :], positions).then_inc(S.sem("positions_landed"), 16)
            S.give(pool.memset(cond[:, :, :], 0.0), "cond_zeroed", 0)
            S.give(pool.memset(A["u"][:, :, 0:30], 0.0), "pad_zeroed", "conv")
            for i in range(2):
                for j, kind in enumerate(("down_done", "down_done", "up_done", "up_done")):
                    pool.memset(small[:, 120 + 4 * i + j:121 + 4 * i + j], 0.0).then_inc(S.sem(f"moe{i}_{kind}"), 1)
            S.wait(pool, "x_added", 1, "mlp")
            pool.dma_start(B["con2"], consts2).then_inc(S.sem("consts2_landed"), 16)
            pool.dma_start(W2["nbias"], na_bias).then_inc(S.sem("na_bias_landed"), 16)
            S.wait(pool, "x_normed", "final")
            pool.dma_start(scratch[:, :, :], ctx_tokens).then_inc(S.sem("ctx_landed"), 16)
            S.wait(pool, "x_normed", "post", 0, 0)
            pool.dma_start(PL["counts"], pool_counts.rearrange("p (a b) -> p a b", a=4))\
                .then_inc(S.sem("counts_landed"), 16)
            S.give(pool.memset(PL["pad"], 0.0), "pad_zeroed", "pool")

        @block.tensor
        def _(pe):
            S.engine = "tensor"

            def chunk(n):
                pe.wait_ge(S.sem(f"slot_landed{n % RING}"), 16 * (n // RING + 1))
                return ring[:, n % RING, :]

            def used_with(n, kind, value):
                S.note(("chunk_used", n), kind, value)

            def product(dst, terms, first=True):
                for i, (a, b) in enumerate(terms):
                    mm = pe.matmul(dst, a, b, start=(first and i == 0), stop=(i == len(terms) - 1))
                return mm

            def over_features(src, tiles, *fill, halves=1, squares_of=None):
                bank = open_bank(pe, *fill)
                if squares_of:
                    for k in range(0, tiles[0], 2):
                        S.wait(pe, "squares", *squares_of, k // 2)
                        for q in range(k, k + 2):
                            mm = pe.matmul(bank[:, 0:T], ones, src(0, q), start=(q == 0), stop=(q == tiles[0] - 1))
                    filled(mm, *fill)
                    return
                for j in range(halves):
                    mm = product(bank[:, j * T:(j + 1) * T], [(ones, src(j, k)) for k in range(tiles[j])])
                filled(mm, *fill)

            def rms_sum(tag):
                over_features(lambda j, k: scratch[:, k, :], [KT], "sum", *tag, squares_of=tag)

            def transposed(dst, src):
                return pe.transpose(dst, src, ident)

            def column_pair(src, n, col, *fill):
                w = chunk(n).rearrange("p (k c) -> p k c", k=KT)
                bank = open_bank(pe, *fill)
                for j in range(2):
                    c = (col + j) * P
                    mm = product(bank[:, j * T:(j + 1) * T], [(w[:, k, c:c + P], src[:, k, :]) for k in range(KT)])
                filled(mm, *fill)

            pe.wait_ge(S.sem("consts_landed"), 16)

            def in_pair(l, pair):
                n = chunk_in(l, pair)
                w = chunk(n).rearrange("p (k c) -> p k c", k=KT)
                bank = open_bank(pe, "in", l, pair)
                for j in range(2):
                    c = ((pair % 2) * 2 + j) * P
                    if pair == 2 and j == 1:
                        for t in range(2):
                            mm = product(bank[:, T + t * P:T + (t + 1) * P],
                                         [(h[:, k, t * P:(t + 1) * P], w[:, k, c:c + P]) for k in range(KT)])
                    elif not (pair == 4 and j == 1):
                        mm = product(bank[:, j * T:(j + 1) * T], [(w[:, k, c:c + P], h[:, k, :]) for k in range(KT)])
                filled(mm, "in", l, pair)
                used_with(n, *S.at[("filled", "in", l, pair)])

            def latent_up(l):
                S.wait(pe, "latent_normed", l)
                n = chunk_of(l, "latent")
                w = chunk(n)
                wq = w[:, 0:2 * QR * 4].rearrange("p (k c) -> p k c", k=2)
                wkv = w[:, 2048:3072]
                cq, ckv = A["cq"], A["ckv"]
                for i in range(2):
                    bank = open_bank(pe, "qn", l, i)
                    for j in range(2):
                        c = (2 * i + j) * P
                        mm = product(bank[:, j * T:(j + 1) * T], [(wq[:, k, c:c + P], cq[:, k, :]) for k in range(2)])
                    filled(mm, "qn", l, i)
                for i in range(2):
                    bank = open_bank(pe, "qp", l, i)
                    for j in range(2):
                        c = 512 + 256 * j + i * P
                        mm = product(bank[:, j * T:(j + 1) * T], [(wq[:, k, c:c + P], cq[:, k, :]) for k in range(2)])
                    filled(mm, "qp", l, i)
                for i in range(2):
                    bank = open_bank(pe, "kn", l, i)
                    for j in range(2):
                        c = (2 * i + j) * P
                        mm = product(bank[:, j * T:(j + 1) * T], [(wkv[:, c:c + P], ckv)])
                    filled(mm, "kn", l, i)
                for t in range(2):
                    bank = open_bank(pe, "vc", l, t)
                    mm = product(bank[:, :], [(ckv[:, t * P:(t + 1) * P], wkv[:, 512:1024])])
                    filled(mm, "vc", l, t)
                used_with(n, *S.at[("filled", "vc", l, 1)])

            def scores(l, u):
                bank = open_bank(pe, "s", l, u)
                if u < HEADS:
                    a, b = (u % 2) * HD, (u % 2) * HD + 32 * (u // 2 % 2)
                    if u == 0:
                        S.wait(pe, "latent_keys", l)
                        S.wait(pe, "latent_queries", l)
                        S.wait(pe, "latent_rotated", l)
                    pairs = [(A["qn"][a:a + HD, u // 2, :], A["kn"][a:a + HD, u // 2, :]),
                             (A["qp"][b:b + 32, u // 4, :], A["kp"][b:b + 32, :])]
                else:
                    a = (u % 2) * HD
                    if u == HEADS:
                        S.wait(pe, "window_queries", l, 1)
                        S.wait(pe, "window_keys", l)
                    pairs = [(A["qa"][a:a + HD, (u - HEADS) // 2, :], A["ka"][a:a + HD, :])]
                for t, (c0, c1, nk) in enumerate([(0, P, P), (P, 3 * P, T)]):
                    mm = product(bank[:, c0:c1], [(q[:, t * P:(t + 1) * P], k[:, 0:nk]) for q, k in pairs])
                filled(mm, "s", l, u)

            def turn(l, u):
                S.wait(pe, "probs", l, u)
                bank = open_bank(pe, "t", l, u)
                for i in range(3):
                    mm = transposed(bank[:, i * P:(i + 1) * P], smax[:, u % 4, i * P:(i + 1) * P])
                filled(mm, "t", l, u)

            state = {}

            def weigh(l, u):
                if u % 2 == 0:
                    state["y"] = open_bank(pe, "y", l, u // 2)
                S.wait(pe, "probs_turned", l, u)
                bank, a = state["y"], (u % 2) * HD
                v, c = (A["vc"], u * HD) if u < HEADS else (A["va"], a)
                pT = smax[:, 4 + u % 2, :]
                product(bank[a:a + HD, 0:P], [(v[:, 0, c:c + HD], pT[:, 0:P])])
                mm = product(bank[a:a + HD, P:T], [(v[:, 0, c:c + HD], pT[:, P:T]), (v[:, 1, c:c + HD], pT[:, T:3 * P])])
                if u % 2 == 1:
                    filled(mm, "y", l, u // 2)
                else:
                    S.give(mm, "weighed", l, u)

            def branch(l, n, y):
                c = chunk_of(l, "branch", BRANCH_ORDER.index(n))
                w = chunk(c).rearrange("p (k c) -> p k c", k=4)
                for i in range(4):
                    bank = open_bank(pe, "branch", l, n, i)
                    for j in range(2):
                        m = (2 * i + j) * P
                        mm = product(bank[:, j * T:(j + 1) * T], [(w[:, k, m:m + P], y[:, k, :]) for k in range(4)])
                    filled(mm, "branch", l, n, i)
                used_with(c, *S.at[("filled", "branch", l, n, 3)])

            def to_model(src, chunk_at, wait_for, *fill):
                for i in range(4):
                    n = chunk_at(i // 2)
                    if i == 0:
                        for w in wait_for:
                            S.wait(pe, *w)
                    column_pair_from = (i % 2) * 2
                    w = chunk(n).rearrange("p (k c) -> p k c", k=KT)
                    bank = open_bank(pe, *fill, i)
                    for j in range(2):
                        c = (column_pair_from + j) * P
                        mm = product(bank[:, j * T:(j + 1) * T], [(w[:, k, c:c + P], src(k)) for k in range(KT)])
                    filled(mm, *fill, i)
                    used_with(n, *S.at[("filled", *fill, i)])

            def zero_sums(*read_by):
                if read_by:
                    S.wait(pe, *read_by)
                zero = S_zero
                for b in range(4):
                    mm = pe.matmul(sums[b][:, :], zero, con[:, 0:512], start=True, stop=False, skip_group_check=True)
                return mm

            S_zero = small[:, 256:384]

            def banks_free():
                for b in range(4):
                    if fills["free"][b] is not None:
                        S.wait(pe, "read", *fills["free"][b])

            def mlp(l):
                n0 = chunk_mlp(l)
                banks_free()
                fb, rb, db = S.base("filled"), S.of("mlp_hidden_base", l)[1], S.base("mlp_chunk_done")
                S.note(("mlp_filled_base", l), "filled", fb)
                S.note(("mlp_done_base", l), "mlp_chunk_done", db)

                lb = S.of("mlp_low_base", l)[1]

                def three(dst, w_hi, w_lo, v_hi, v_lo, start, stop):
                    pe.matmul(dst, w_hi, v_hi, start=start, stop=False, skip_group_check=True)
                    pe.matmul(dst, w_hi, v_lo, start=False, stop=False, skip_group_check=True)
                    return pe.matmul(dst, w_lo, v_hi, start=False, stop=stop, skip_group_check=True)

                def up(i, j):
                    slot = (n0 + j) % RING
                    pe.wait_ge(S.sem("mlp_low"), i * 8 + (lb + 2 * j + 1))
                    pe.wait_ge(S.sem("mlp_hidden"), i * 4 + (rb + j - 3))
                    lo = split["ring"][:, slot, 0:2048].rearrange("p (k c) -> p k c", k=KT)
                    hi = HI["up"][:, j % 2, :].rearrange("p (k c) -> p k c", k=KT)
                    for f in range(2):
                        for k in range(KT):
                            c = slice(f * P, (f + 1) * P)
                            mm = three(banks[j][:, f * T:(f + 1) * T], hi[:, k, c], lo[:, k, c],
                                       split["h"][:, k, :], split["scratch"][:, k, :], k == 0, k == KT - 1)
                    mm.then_inc(S.sem("filled"), 1)

                def down(i, j):
                    slot = (n0 + j) % RING
                    pe.wait_ge(S.sem("mlp_low"), i * 8 + (lb + 2 * j + 2))
                    pe.wait_ge(S.sem("mlp_hidden"), i * 4 + (rb + j + 1))
                    lo = split["ring"][:, slot, 2048:4096].rearrange("p (f c) -> p f c", f=2)
                    hi = HI["down"][:, j % 2, :].rearrange("p (f c) -> p f c", f=2)
                    for f in range(2):
                        v = slice(f * T, (f + 1) * T)
                        for m in range(KT):
                            c = slice(m * P, (m + 1) * P)
                            mm = three(sums[m // 2][:, (m % 2) * T:(m % 2 + 1) * T], hi[:, f, c], lo[:, f, c],
                                       split["smax"][:, 2 + j % 2, v], split["smax"][:, 4 + j % 2, v], False, False)
                    mm.then_inc(S.sem("mlp_chunk_done"), 1)

                with pe.Fori(0, MLP_CHUNKS // 4) as i:
                    up(i, 0)
                    for j in range(1, 4):
                        up(i, j)
                        down(i, j - 1)
                    down(i, 3)
                S.base("filled", fb + MLP_CHUNKS)
                S.base("mlp_chunk_done", db + MLP_CHUNKS)
                for c in range(MLP_CHUNKS):
                    used_with(n0 + c, "mlp_chunk_done", db + c + 1)
                fills["n"] = 0
                for b in range(4):
                    fills["free"][b] = ("mlp_last", l, b)
                    S.note(("read", "mlp_last", l, b), "mlp_hidden", rb + MLP_CHUNKS - 3 + b)
                S.note(("mlp_summed", l), "mlp_chunk_done", db + MLP_CHUNKS)

            def mod_site(l, c):
                if c < MOD_CHUNKS:
                    n = chunk_of(l, "mod", c)
                    w = chunk(n).rearrange("p (k c) -> p k c", k=KT)
                    if c >= 2:
                        S.wait(pe, "mod_copied", l, c - 2)
                    elif l:
                        S.wait(pe, "x_added", l - 1, "mlp")
                    else:
                        S.wait(pe, "cond_ready", 0)
                    for k in range(KT):
                        g = 32 * (k % 4)
                        mm = pe.matmul(sums[c % 2][g:g + 32, :], cond[:, k, :], w[:, k, :], start=(k < 4), stop=(k >= 4))
                    S.give(mm, "mod_product", l, c)
                    used_with(n, *S.at[("mod_product", l, c)])
                if c:
                    S.wait(pe, "mod_copied", l, c - 1)
                    if c >= 2:
                        S.wait(pe, "mod_kept", l, c - 2)
                    for t in range(4):
                        mm = pe.matmul(sums[2][:, 2 * t:2 * t + 2], A["mod_rows"][:, (c - 1) % 2, t * P:(t + 1) * P], cst("sum4"),
                                       start=True, stop=True)
                    S.give(mm, "mod_turned", l, c - 1)

            def block_1(l):
                rms_sum(("mix", l))
                S.wait(pe, "h_ready", "mix", l)
                for pair in range(10):
                    in_pair(l, pair)
                S.wait(pe, "latent_squares", l)
                over_features(lambda j, k: smax[:, 3 + j, k * T:(k + 1) * T], [2, 1], "sum", "latent", l, halves=2)
                in_pair(l, 10)
                in_pair(l, 11)
                latent_up(l)
                for u in range(2 * HEADS + 3):
                    if u < 2 * HEADS:
                        scores(l, u)
                    if u in GATE_UNITS:
                        in_pair(l, GATE_UNITS[u])
                    if u in MOD_UNITS:
                        mod_site(l, MOD_UNITS[u])
                    if 2 <= u < 2 * HEADS + 2:
                        turn(l, u - 2)
                    if u >= 3:
                        weigh(l, u - 3)
                S.wait(pe, "y_ready", "window", l)
                branch(l, 0, A["ya"])
                mod_site(l, 10)
                S.wait(pe, "conv_done", l)
                over_features(lambda j, k: A["conv"][:, k, :], [CT], "sum", "conv", l)
                branch(l, 2, A["yc"])
                mod_site(l, 11)
                over_features(lambda j, k: scratch[:, k, :], [CT], "sum2", "conv", l, squares_of=("conv", l))
                S.wait(pe, "y_ready", "conv", l)
                branch(l, 1, A["conv"])
                to_model(lambda k: h[:, k, :], lambda half: chunk_of(l, "out", half), [("mixed", l)], "out", l)
                mod_site(l, MOD_CHUNKS)
                rms_sum(("mlp", l))
                if l == 0:
                    S.wait(pe, "zero_ready", 0)
                S.give(zero_sums("mod_kept", l, MOD_CHUNKS - 1), "mlp_chunk_done")
                S.wait(pe, "h_ready", "mlp", l)
                mlp(l)

            for l in range(LAYERS):
                block_1(l)

            rms_sum(("final",))

            def feature_cols(n, src, name):
                w = chunk(n).rearrange("p (k c) -> p k c", k=KT)
                for i in range(2):
                    bank = open_bank(pe, name, i)
                    for j in range(2):
                        c = (2 * i + j) * P
                        mm = product(bank[:, j * T:(j + 1) * T], [(w[:, k, c:c + P], src[:, k, :]) for k in range(KT)])
                    filled(mm, name, i)
                    used_with(n, *S.at[("filled", name, i)])

            def token_rows(n, src, name):
                w = chunk(n).rearrange("p (k c) -> p k c", k=KT)
                for t in range(2):
                    bank = open_bank(pe, name, t)
                    mm = product(bank[:, :], [(src[:, k, t * P:(t + 1) * P], w[:, k, :]) for k in range(KT)])
                    filled(mm, name, t)
                    used_with(n, *S.at[("filled", name, t)])

            S.wait(pe, "h_ready", "mod", 0, 0)
            feature_cols(C_AB, h, "rk")
            S.wait(pe, "ctx_modulated", 0)
            token_rows(C_AB, scratch, "rkc")
            token_rows(C_AB + 1, h, "rv")
            token_rows(C_AB + 1, scratch, "rvc")
            feature_cols(C_AB + 2, h, "nk")
            feature_cols(C_AB + 2, scratch, "nkc")
            token_rows(C_AB + 3, h, "nv")
            token_rows(C_AB + 3, scratch, "nvc")
            feature_cols(C_AB + 4, h, "rq")
            for which in ("rk", "rq"):
                for i in range(2):
                    S.wait(pe, "projected", which, i)
                    bank = open_bank(pe, "swap", which, i)
                    for j in range(2):
                        mm = product(bank[:, j * T:(j + 1) * T], [(cst("swap64"), B[which][:, 2 * i + j, :])])
                    filled(mm, "swap", which, i)
            for d in range(2):
                bank = open_bank(pe, "state", d)
                for hd in range(RET):
                    S.wait(pe, "keys_decayed", d, hd)
                    kd = smax[:, (4 * d + hd) % 6, 0:2 * P].rearrange("p (t c) -> p t c", t=2)
                    mm = product(bank[:, hd * P:(hd + 1) * P],
                                 [(kd[:, t, :], B["rvc"][:, t, hd * P:(hd + 1) * P]) for t in range(2)])
                    if hd < RET - 1:
                        S.give(mm, "state_done", d, hd)
                filled(mm, "state", d)
            feature_cols(C_AB + 5, h, "rg")
            feature_cols(C_AB + 6, h, "nq")
            for hd in range(RET):
                if hd == 0:
                    S.wait(pe, "rotated", "rk", 1)
                    S.wait(pe, "rotated", "rq", 1)
                bank = open_bank(pe, "att", hd)
                for j in range(2):
                    mm = product(bank[:, j * T:(j + 1) * T], [(B["rk"][:, hd, j * P:(j + 1) * P], B["rq"][:, hd, :])])
                filled(mm, "att", hd)
            for i in range(2):
                bank = open_bank(pe, "ret", i)
                for j in range(2):
                    hd = 2 * i + j
                    S.wait(pe, "att_decayed", hd)
                    if hd == 0:
                        S.wait(pe, "states_kept", 1)
                        S.wait(pe, "queries_decayed", 0)
                    at = smax[:, 2 + hd, :]
                    mm = product(bank[:, j * T:(j + 1) * T],
                                 [(B["rv"][:, t, hd * P:(hd + 1) * P], at[:, t * T:(t + 1) * T]) for t in range(2)]
                                 + [(W2["state"][:, 4 * d + hd, :], W2["qd"][:, 4 * d + hd, :]) for d in range(2)])
                filled(mm, "ret", i)
            for what, src in (("sum", lambda hd: B["rkc"].rearrange("p a (b t) -> p (a b) t", b=2)[:, hd, :]),
                              ("sum2", lambda hd: scratch[:, hd, :])):
                for i in range(2):
                    if what == "sum":
                        S.wait(pe, "retained", i)
                    else:
                        S.wait(pe, "squares", "head", i)
                    bank = open_bank(pe, what, "head", i)
                    for j in range(2):
                        mm = product(bank[:, j * T:(j + 1) * T], [(ones, src(2 * i + j))])
                    filled(mm, what, "head", i)

            def na_scores(u):
                hd, t = u // 2, u % 2
                a = (hd % 2) * HD
                if u == 0:
                    S.wait(pe, "projected", "nq", 1)
                    S.wait(pe, "projected", "nkc", 1)
                bank = open_bank(pe, "s", "na", u)
                q = B["nq"][a:a + HD, hd // 2, t * P:(t + 1) * P]
                product(bank[:, 0:T], [(q, B["nk"][a:a + HD, hd // 2, :])])
                mm = product(bank[:, T:2 * T], [(q, B["nkc"][a:a + HD, hd // 2, :])])
                filled(mm, "s", "na", u)

            def na_turn(u):
                S.wait(pe, "probs", "na", u)
                bank = open_bank(pe, "t", "na", u)
                for i in range(4):
                    mm = transposed(bank[:, i * P:(i + 1) * P], smax[:, u % 4, i * P:(i + 1) * P])
                filled(mm, "t", "na", u)

            def na_weigh(u):
                hd, t = u // 2, u % 2
                a, c = (hd % 2) * HD, hd * HD
                S.wait(pe, "probs_turned", "na", u)
                pT = smax[:, 4 + u % 2, :]
                mm = product(sums[u // 4][a:a + HD, t * P:(t + 1) * P],
                             [(B["nv"][:, k, c:c + HD], pT[:, k * P:(k + 1) * P]) for k in range(2)]
                             + [(B["nvc"][:, k, c:c + HD], pT[:, (2 + k) * P:(3 + k) * P]) for k in range(2)])
                if u % 4 == 3:
                    filled(mm, "y", "na", u // 4)
                else:
                    S.give(mm, "weighed", "na", u)

            for u in range(16 + 3):
                if u < 16:
                    na_scores(u)
                if 2 <= u < 18:
                    na_turn(u - 2)
                if u >= 3:
                    na_weigh(u - 3)
            to_model(lambda k: (B["rg"] if k < 4 else B["yn"])[:, k % 4, :], lambda half: C_ABOUT + half,
                     [("ret_ready", 0), ("y_ready", "na")], "ab_out")

            def layer_norm_sums(i, s):
                S.wait(pe, "added", i, s)
                over_features(lambda j, k: x[:, k, :], [KT], "sum", "post", i, s)
                over_features(lambda j, k: scratch[:, k, :], [KT], "sum2", "post", i, s, squares_of=("post", i, s))

            def moe(i):
                S.wait(pe, "h_ready", "mod", i, 1)
                bank = open_bank(pe, "router", i)
                for t in range(2):
                    mm = product(bank[:, t * 64:t * 64 + 36],
                                 [(h[:, k, t * P:(t + 1) * P], prm("w_router", (i * KT + k) * 36, 36)) for k in range(KT)])
                filled(mm, "router", i)
                for t in range(2):
                    for half in range(2):
                        bank = open_bank(pe, "rows", i, t, half)
                        for k in range(4):
                            mm = transposed(bank[:, k * P:(k + 1) * P], h[:, 4 * half + k, t * P:(t + 1) * P])
                        filled(mm, "rows", i, t, half)
                zero_sums("x_added", 1, "mlp") if i == 0 else zero_sums("added", 0, 1)
                S.wait(pe, "members", i)
                bank = open_bank(pe, "rank", i)
                product(bank[:, 0:32], [(cst("before"), member[:, 0, :])])
                product(bank[:, 32:64], [(ones, member[:, 0, :]), (cst("before"), member[:, 1, :])])
                filled(product(bank[:, 64:96], [(ones, member[:, 0, :]), (ones, member[:, 1, :])]), "rank", i)
                S.wait(pe, "rows_kept", i, 1, 1)
                banks_free()

                def raised(kind, it, add, per_turn):
                    pe.wait_ge(S.sem(f"moe{i}_{kind}"), it * per_turn + add)

                def give(ins, kind):
                    ins.then_inc(S.sem(f"moe{i}_{kind}"), 1)

                def landed(it, q):
                    raised(f"landed{q % RING}", it, 16 * (q // RING + 1), 48)
                    return ring[:, q % RING, :]

                def gather(it):
                    raised("placed", it, 1, 1)
                    for j in range(4):
                        bank = banks[3 - j]
                        for a in range(2):
                            k = 2 * j + a
                            mm = product(bank[:, a * T:(a + 1) * T],
                                         [(M["by_token"][:, t, k * P:(k + 1) * P], M["place"][:, t, :]) for t in range(2)])
                        give(mm, "gather_done")

                def gate_up(it, e):
                    if e == 0:
                        raised("gather_kept", it, 4, 4)
                    for c in range(2):
                        w = landed(it, 3 * e + c).rearrange("p (k c) -> p k c", k=4)
                        for kk in range(4):
                            k = 4 * c + kk
                            for half in range(2):
                                mm = pe.matmul(banks[0][64 * half:64 * half + 64, :],
                                               M["gathered"][:, k, e * SLOTS:(e + 1) * SLOTS],
                                               w[:, kk, 512 * half:512 * half + 512], start=(k == 0), stop=(k == KT - 1))
                    give(mm, "up_done")

                def turn(it, e):
                    raised("hidden", it, e + 1, 4)
                    for j in range(2):
                        transposed(banks[1][:, j * P:(j + 1) * P], M["hidden"][:, j * P:(j + 1) * P])
                    for t in range(2):
                        mm = transposed(banks[1][:, T + t * P:T + (t + 1) * P],
                                        M["weighted"][:, t, 2 * e * SLOTS:2 * (e + 1) * SLOTS])
                    give(mm, "turn_done")

                def down(it, e):
                    raised("turned", it, e + 1, 4)
                    w = landed(it, 3 * e + 2).rearrange("p (k c) -> p k c", k=4)
                    for k in range(4):
                        hT = M["turned"][:, (k % 2) * P + (k // 2) * 64:(k % 2) * P + (k // 2) * 64 + 64]
                        for half in range(2):
                            mm = pe.matmul(banks[2][64 * half:64 * half + 64, :], hT, w[:, k, 512 * half:512 * half + 512],
                                           start=(k == 0), stop=(k == 3))
                    give(mm, "down_done")

                def spread(it, e):
                    raised("y_kept", it, e + 1, 4)
                    for m in (0, 4, 1, 5, 2, 6, 3, 7):
                        a, c = 64 * (m // 4), (m % 4) * P
                        pe.matmul(sums[m // 2][:, (m % 2) * T:(m % 2 + 1) * T], M["y"][a:a + 64, c:c + P],
                                  M["turned"][a:a + 64, T:2 * T], start=False, stop=False, skip_group_check=True)

                with pe.Fori(0, rounds_of(pe, i)) as rnd:
                    with pe.Fori(0, TURNS) as g:
                        it = rnd * TURNS + g
                        gather(it)
                        for e in range(GROUP_OF):
                            gate_up(it, e)
                            if e:
                                spread(it, e - 1)
                            turn(it, e)
                            down(it, e)
                        spread(it, GROUP_OF - 1)
                for b in range(4):
                    mm = pe.matmul(sums[b][:, :], S_zero, con[:, 0:512], start=False, stop=True, skip_group_check=True)
                S.give(mm, "moe_summed", i)
                fills["n"] = 0
                fills["free"] = [None] * 4

            layer_norm_sums(0, 0)
            moe(0)
            layer_norm_sums(0, 1)
            w = chunk(C_POOL)[:, 0:2048].rearrange("p (g k c) -> p g k c", g=4, k=2)
            for g in range(4):
                S.wait(pe, "pooled", g)
                bank = open_bank(pe, "pool", g)
                for j in range(2):
                    mm = product(bank[:, j * T:(j + 1) * T],
                                 [(w[:, g, k, j * P:(j + 1) * P], PL["z"][:, 2 * g + k, :]) for k in range(2)])
                filled(mm, "pool", g)
            used_with(C_POOL, *S.at[("filled", "pool", 3)])
            layer_norm_sums(1, 0)
            moe(1)
            layer_norm_sums(1, 1)

        @block.scalar
        def _(act):
            S.engine = "scalar"

            def done(ins, *fill):
                read("act_read", S.give(ins, "act_read"), *fill)

            def root(tag, n=T):
                S.wait(act, "variance", *tag)
                S.give(act.activation(stat[:, 1, 0:n], stat[:, 0, 0:n], ACT.Sqrt), "root", *tag)

            def copy_out(dst, src, kind, key, fill, scale=None):
                bank = take(act, *fill)
                ins = act.activation(dst, src(bank), ACT.Copy, scale=1.0 if scale is None else scale)
                read(kind, S.give(ins, kind, *key), *fill)

            def first_steps():
                act.wait_ge(S.sem("params_landed"), 16)
                S.wait(act, "cond_zeroed", 0)
                S.give(act.activation(cond[:, :, 0:2], prm("cond", 0, 16).rearrange("p (k c) -> p k c", c=2), ACT.Silu),
                       "cond_ready", 0)
                S.give(act.activation(small[:, 24:32], prm("log_decay", 0, 8), ACT.Exp), "decay_exp", 0)
                S.wait(act, "decay_arg", 0)
                S.give(act.activation(small[:, 40:48], small[:, 32:40], ACT.Ln), "decay_ln", 0)
                S.wait(act, "angles", 0)
                act.activation(A["sin"], scratch[:, 0, :], ACT.Sin)
                S.give(act.activation(A["cos"], scratch[:, 1, :], ACT.Sin, bias=float(np.pi / 2)), "rope_tables", 0)

            def copy_mod(l, c):
                bank = sums[c % 2]
                S.wait(act, "mod_product", l, c)
                if c >= 2:
                    S.wait(act, "mod_turned", l, c - 2)
                elif l:
                    S.wait(act, "x_added", l - 1, "mlp")
                S.give(act.activation(A["mod_rows"][:, c % 2, :], bank[:, :], ACT.Copy), "mod_copied", l, c)

            def softmax_exps(l, u):
                S.wait(act, "row_max", l, u)
                st = u % 4 * 8
                act.activation(smax[:, u % 4, 0:P], smax[:, u % 4, 0:P], ACT.Exp,
                               bias=small[:, 48 + st:49 + st], accum_out=small[:, 50 + st:51 + st])
                ins = act.activation(smax[:, u % 4, P:3 * P], smax[:, u % 4, P:3 * P], ACT.Exp,
                                     bias=small[:, 49 + st:50 + st], accum_out=small[:, 51 + st:52 + st])
                if u >= HEADS:
                    s = prm("sinks", l * HEADS + sink_of(u))
                    for t in range(2):
                        ins = act.activation(small[:, 52 + st + t:53 + st + t], s, ACT.Exp,
                                             bias=small[:, 48 + st + t:49 + st + t])
                S.give(ins, "exps", l, u)

            def turned(l, u, n):
                bank = take(act, "t", l, u)
                if u >= 2:
                    S.wait(act, *weighed(l, u - 2))
                ins = act.activation(smax[:, 4 + u % 2, 0:n], bank[:, 0:n], ACT.Copy)
                read("probs_turned", S.give(ins, "probs_turned", l, u), "t", l, u)

            def weighed(l, u):
                if l == "na":
                    return ("filled", "y", "na", u // 4) if u % 4 == 3 else ("weighed", "na", u)
                return ("filled", "y", l, u // 2) if u % 2 else ("weighed", l, u)

            def tanh_gates(l, pair):
                g = pair - 10
                bank = take(act, "in", l, pair)
                dst = gates[:, 2 * g:2 * g + 2, :].rearrange("p a b -> p (a b)")
                ins = act.activation(dst, bank[:, :], ACT.Tanh, scale=0.5)
                read("gates_ready", S.give(ins, "gates_ready", l, pair), "in", l, pair)

            def block_1(l):
                root(("mix", l))
                if l == 0:
                    first_steps()
                for i in range(2):
                    copy_out(A["qa"][:, 2 * i:2 * i + 2, :].rearrange("p a b -> p (a b)"), lambda b: b[:, :],
                             "window_queries", (l, i), ("in", l, i))
                bank = take(act, "in", l, 2)
                act.activation(A["ka"], bank[:, 0:T], ACT.Copy)
                ins = act.activation(A["va"].rearrange("p a b -> p (a b)"), bank[:, T:2 * T], ACT.Copy)
                read("window_keys", S.give(ins, "window_keys", l), "in", l, 2)
                bank = take(act, "in", l, 3)
                act.activation(A["cq"].rearrange("p a b -> p (a b)"), bank[:, :], ACT.Copy)
                done(act.activation(smax[:, 3, :], bank[:, :], ACT.Square), "in", l, 3)
                bank = take(act, "in", l, 4)
                act.activation(A["ckv"], bank[:, 0:T], ACT.Copy)
                ins = act.activation(smax[:, 4, 0:T], bank[:, 0:T], ACT.Square)
                read("latent_squares", S.give(ins, "latent_squares", l), "in", l, 4)
                for j in range(CT):
                    bank = take(act, "in", l, 6 + j)
                    if j >= 2:
                        S.wait(act, "glu", l, j - 2)
                    S.give(act.activation(stat_glu(j), bank[:, T:2 * T], ACT.Tanh, scale=0.5), "glu_tanh", l, j)
                root(("latent", l), 512)
                tanh_gates(l, 10)
                tanh_gates(l, 11)
                for i in range(2):
                    copy_out(A["qn"][:, 2 * i:2 * i + 2, :].rearrange("p a b -> p (a b)"), lambda b: b[:, :],
                             "latent_queries", ((l,) if i else (l, "first")), ("qn", l, i))
                for i in range(2):
                    copy_out(A["kn"][:, 2 * i:2 * i + 2, :].rearrange("p a b -> p (a b)"), lambda b: b[:, :],
                             "latent_nope", (l, i), ("kn", l, i))
                for t in range(2):
                    copy_out(A["vc"][:, t, :], lambda b: b[:, :], "latent_keys", ((l,) if t else (l, "first")),
                             ("vc", l, t))
                for u in range(2 * HEADS + 3):
                    if u < 2 * HEADS:
                        softmax_exps(l, u)
                    if u in GATE_UNITS:
                        tanh_gates(l, GATE_UNITS[u])
                    if u in MOD_UNITS:
                        copy_mod(l, MOD_UNITS[u])
                    if 2 <= u < 2 * HEADS + 2:
                        turned(l, u - 2, 3 * P)
                    if u >= 4 and u % 2 == 0:
                        attended(l, (u - 4) // 2)
                copy_mod(l, 10)
                copy_mod(l, 11)
                root(("conv", l))
                for j in range(CT):
                    S.wait(act, "conv_normed", l, j)
                    ins = act.activation(A["conv"][:, j, :], scratch[:, j, :], ACT.Silu,
                                         scale=prm("g_conv", l * CT + j), bias=prm("b_conv", l * CT + j))
                S.give(ins, "y_ready", "conv", l)
                root(("mlp", l))
                for i in range(4):
                    S.wait(act, "h_whole", l, i)
                    S.give(act.activation(flat2(split["h"][:, 2 * i:2 * i + 2, :]), flat2(scratch[:, 2 * i:2 * i + 2, :]), ACT.Copy),
                           "h_high", l, i)
                n0 = chunk_mlp(l)
                fb, hb, rb = S.of("mlp_filled_base", l)[1], S.of("mlp_hidden_base", l)[1], S.base("relued")
                db, wb = S.of("mlp_done_base", l)[1], S.base("mlp_high")
                S.note(("relued_base", l), "relued", rb)
                S.note(("mlp_high_base", l), "mlp_high", wb)

                def high(i, j, part):
                    slot = (n0 + j) % RING
                    act.wait_ge(S.sem(f"slot_landed{slot}"), i * 16 + 16 * ((n0 + j) // RING + 1))
                    if j or not isinstance(i, int) or i:
                        act.wait_ge(S.sem("filled" if part == 0 else "mlp_chunk_done"),
                                    i * 4 + ((fb if part == 0 else db) + j - 1))
                    act.activation(HI[("up", "down")[part]][:, j % 2, :], ring[:, slot, 2048 * part:2048 * part + 2048],
                                   ACT.Copy).then_inc(S.sem("mlp_high"), 1)

                def step(i, last=False):
                    for j in range(4):
                        final = last and j == 3
                        if not final:
                            high(i, j + 1, 0)
                        act.wait_ge(S.sem("filled"), i * 4 + (fb + j + 1))
                        act.wait_ge(S.sem("mlp_hidden"), i * 4 + (hb + j - 1))
                        act.activation(hid[:, j % 2, :], banks[j][:, :], ACT.Relu).then_inc(S.sem("relued"), 1)
                        if not final:
                            high(i, j + 1, 1)

                S.wait(act, "filled", "branch", l, 1, 3)
                high(0, 0, 0)
                high(0, 0, 1)
                with act.Fori(0, MLP_CHUNKS // 4 - 1) as i:
                    step(i)
                step(MLP_CHUNKS // 4 - 1, last=True)
                S.base("relued", rb + MLP_CHUNKS)
                S.base("mlp_high", wb + 2 * MLP_CHUNKS)

            def attended(l, pair):
                y = A["yc"] if pair < 4 else A["ya"]
                kind = "y_ready" if pair == 7 else "y_kept"
                copy_out(y[:, pair % 4, :], lambda b: b[:, 0:T], kind,
                         ("window", l) if pair == 7 else (l, pair), ("y", l, pair))

            def stat_glu(j):
                return smax[:, 0, (j % 2) * T:(j % 2 + 1) * T]

            for l in range(LAYERS):
                block_1(l)

            root(("final",))
            S.wait(act, "loggam", 0)
            act.wait_ge(S.sem("consts2_landed"), 16)
            for hd in range(RET):
                S.wait(act, "exponent", hd)
                ins = act.activation(W2["decay"][:, hd, :], W2["decay"][:, hd, :], ACT.Exp)
                S.give(ins, "decay_exps", hd)
            for d, name in enumerate(("dec_f", "dec_b")):
                for hd in range(RET):
                    ins = act.activation(W2["qd"][:, 4 * d + hd, :], cst2(name), ACT.Exp,
                                         scale=loggam[:, 4 * d + hd:4 * d + hd + 1])
            S.give(ins, "query_decays", 0)
            for d, name in enumerate(("left_f", "left_b")):
                for hd in range(RET):
                    ins = act.activation(small[:, 96 + 2 * (4 * d + hd):98 + 2 * (4 * d + hd)], cst(name), ACT.Exp,
                                         scale=loggam[:, 4 * d + hd:4 * d + hd + 1])
            S.give(ins, "key_decays", 0)

            def keep(name, tiles=2, scale=None):
                for i in range(tiles):
                    t = B[name]
                    n = t.shape[1] // 2
                    dst = t[:, n * i:n * i + n, :].rearrange("p a b -> p (a b)")
                    copy_out(dst, lambda b: b[:, :], "projected", (name, i), (name, i), scale)

            keep("rk")
            keep("rkc")
            keep("rv")
            keep("rvc")
            keep("nk")
            keep("nkc")
            keep("nv")
            keep("nvc")
            keep("rq", scale=float(P) ** -0.5)
            for d in range(2):
                copy_out(W2["state"][:, 4 * d:4 * d + 4, :].rearrange("p a b -> p (a b)"), lambda b: b[:, :],
                         "states_kept", (d,), ("state", d))
            for i in range(2):
                bank = take(act, "rg", i)
                ins = act.activation(B["rg"][:, 2 * i:2 * i + 2, :].rearrange("p a b -> p (a b)"), bank[:, :], ACT.Silu)
                read("projected", S.give(ins, "projected", "rg", i), "rg", i)
            keep("nq")
            for i in range(2):
                copy_out(B["rkc"][:, i, :], lambda b: b[:, :], "retained", (i,), ("ret", i))
            for i in range(2):
                S.wait(act, "variance", "head", i)
                S.give(act.activation(smax[:, 2 + i, :], smax[:, 2 + i, :], ACT.Sqrt), "root", "head", i)
            for u in range(16 + 3):
                if u < 16:
                    S.wait(act, "row_max", "na", u)
                    st = u % 4 * 8
                    ins = act.activation(smax[:, u % 4, :], smax[:, u % 4, :], ACT.Exp,
                                         bias=small[:, 48 + st:49 + st], accum_out=small[:, 50 + st:51 + st])
                    S.give(ins, "exps", "na", u)
                if 2 <= u < 18:
                    turned("na", u - 2, 512)
                if u >= 3 and (u - 3) % 4 == 3:
                    pair = (u - 3) // 4
                    S.wait(act, "filled", "y", "na", pair)
                    ins = act.activation(B["yn"][:, pair, :], sums[pair][:, 0:T], ACT.Copy)
                    if pair == 3:
                        S.give(ins, "y_ready", "na")

            def moe(i):
                for t in range(2):
                    for half in range(2):
                        copy_out(M["by_token"][:, t, 512 * half:512 * half + 512], lambda b: b[:, :], "rows_kept",
                                 (i, t, half), ("rows", i, t, half))
                S.wait(act, "router_shifted", i)
                S.give(act.activation(small[:, 0:8], small[:, 0:8], ACT.Exp), "router_exps", i)
                S.wait(act, "top_shifted", i)
                S.give(act.activation(small[:, 8:10], small[:, 8:10], ACT.Exp), "top_exps", i)
                with act.Fori(0, rounds_of(act, i)) as rnd:
                    with act.Fori(0, TURNS) as g:
                        it = rnd * TURNS + g
                        for j in range(4):
                            act.wait_ge(S.sem(f"moe{i}_gather_done"), it * 4 + (j + 1))
                            act.activation(flat2(M["gathered"][:, 2 * j:2 * j + 2, :]), banks[3 - j][:, :], ACT.Copy)\
                               .then_inc(S.sem(f"moe{i}_gather_kept"), 1)
                        for e in range(GROUP_OF):
                            act.wait_ge(S.sem(f"moe{i}_up_done"), it * 4 + (e + 3))
                            act.activation(M["silu"], banks[0][:, 0:T], ACT.Silu).then_inc(S.sem(f"moe{i}_silued"), 1)
                            act.wait_ge(S.sem(f"moe{i}_turn_done"), it * 4 + (e + 1))
                            act.activation(M["turned"], banks[1][:, :], ACT.Copy).then_inc(S.sem(f"moe{i}_turned"), 1)

            root(("post", 0, 0))
            moe(0)
            root(("post", 0, 1))
            root(("post", 1, 0))
            moe(1)
            root(("post", 1, 1))

        @block.vector
        def _(dve):
            S.engine = "vector"

            def link(ins):
                n = S.give(ins, "dve_step")
                dve.wait_ge(S.sem("dve_step"), n)

            def done(ins, *fill):
                read("dve_read", S.give(ins, "dve_read"), *fill)

            def give_link(ins, kind, *key):
                n = S.give(ins, kind, *key)
                dve.wait_ge(S.sem(kind), n)

            def flat(v):
                return v.rearrange("p a b -> p (a b)")

            def squares(src, tag, tiles=KT):
                for k in range(0, tiles, 2):
                    v = flat(src[:, k:k + 2, :])
                    S.give(dve.tensor_tensor(flat(scratch[:, k:k + 2, :]), v, v, ALU.mult), "squares", *tag, k // 2)

            def variance(tag, n, eps, fill, col=0):
                bank = take(dve, *fill)
                ins = dve.tensor_scalar(stat[:, 0, 0:T], bank[:, 0:T], 1.0 / n, eps, ALU.mult, ALU.add)
                read("variance", S.give(ins, "variance", *tag), *fill)

            def inverse_root(tag, n=T):
                S.wait(dve, "root", *tag)
                link(dve.reciprocal(stat[:, 1, 0:n], stat[:, 1, 0:n]))

            def rms(tag, gain, dst, kind, last_read=None):
                squares(x, tag)
                variance(tag, D, EPS, ("sum", *tag))
                inverse_root(tag)
                dve.wait_ge(S.sem("params_landed"), 16)
                for k in range(KT):
                    ins = dve.scalar_tensor_tensor(out=dst[:, k, :], in0=x[:, k, :], scalar=prm(*gain(k)),
                                                   in1=stat[:, 1, 0:T], op0=ALU.mult, op1=ALU.mult)
                S.give(ins, kind, *tag)

            dve.wait_ge(S.sem("tokens_landed"), 16)
            S.give(dve.memset(small[:, 256:384], 0.0), "zero_ready", 0)
            for j in range(4):
                S.give(dve.memset(small[:, 80 + j:81 + j], 0.0), "mlp_hidden")
            def first_steps():
                dve.wait_ge(S.sem("positions_landed"), 16)
                S.wait(dve, "decay_exp", 0)
                give_link(dve.tensor_scalar(small[:, 32:40], small[:, 24:32], -1.0, 1.0, ALU.mult, ALU.add), "decay_arg", 0)
                one_minus, equal = small[:, 88:96], small[:, 240:248]
                turns = scratch[:, 3, :]
                link(dve.tensor_copy(A["pk"], pos_i[:, 0:T]))
                link(dve.tensor_scalar(scratch[:, 0, :], A["pk"], cst("rope_freq"), None, ALU.mult))
                link(dve.tensor_scalar(turns, scratch[:, 0, :], float(1 / (2 * np.pi)), 12582912.0, ALU.mult, ALU.add))
                link(dve.tensor_scalar(turns, turns, -12582912.0, None, ALU.add))
                c1 = 6.28125
                link(dve.scalar_tensor_tensor(out=scratch[:, 0, :], in0=turns, scalar=-c1, in1=scratch[:, 0, :],
                                              op0=ALU.mult, op1=ALU.add))
                link(dve.scalar_tensor_tensor(out=scratch[:, 0, :], in0=turns, scalar=-float(2 * np.pi - c1),
                                              in1=scratch[:, 0, :], op0=ALU.mult, op1=ALU.add))
                link(dve.tensor_scalar(scratch[:, 0, :], scratch[:, 0, :], 3.1415925, -3.1415925, ALU.min, ALU.max))
                link(dve.tensor_scalar(scratch[:, 1, :], scratch[:, 0, :], -1.0, None, ALU.mult))
                give_link(dve.tensor_tensor(scratch[:, 1, :], scratch[:, 0, :], scratch[:, 1, :], ALU.min), "angles", 0)
                S.wait(dve, "rope_tables", 0)
                link(dve.tensor_scalar(A["sin"], A["sin"], cst("rope_sign"), None, ALU.mult))
                S.wait(dve, "decay_ln", 0)
                link(dve.tensor_scalar(one_minus, small[:, 32:40], -1.0, 1.0, ALU.mult, ALU.add))
                link(dve.tensor_scalar(equal, one_minus, 0.0, None, ALU.is_equal))
                link(dve.tensor_tensor(one_minus, one_minus, equal, ALU.add))
                link(dve.reciprocal(one_minus, one_minus))
                link(dve.tensor_tensor(one_minus, one_minus, small[:, 40:48], ALU.mult))
                link(dve.tensor_tensor(one_minus, one_minus, equal, ALU.subtract))
                S.give(dve.tensor_tensor(loggam, one_minus, small[:, 24:32], ALU.mult), "loggam", 0)

                away = A["away"]
                link(dve.tensor_copy(small[:, 248:250], pos_i[:, T:T + 2]))
                link(dve.tensor_scalar(away[:, 0, :], A["pk"][:, 0:P], -1.0, small[:, 248:249], ALU.mult, ALU.add))
                link(dve.tensor_scalar(scratch[:, 4, 0:P], A["pk"][:, P:T], -1.0, small[:, 249:250], ALU.mult, ALU.add))
                link(dve.tensor_scalar(scratch[:, 4, P:T], A["pk"][:, 0:P], -1.0, small[:, 249:250], ALU.mult, ALU.add))
                link(dve.tensor_tensor(scratch[:, 4, 0:P], scratch[:, 4, 0:P], scratch[:, 4, P:T], ALU.subtract))
                link(dve.tensor_tensor(scratch[:, 4, 0:P], scratch[:, 4, 0:P], cst("lower"), ALU.mult))
                link(dve.tensor_tensor(away[:, 1, :], scratch[:, 4, 0:P], scratch[:, 4, P:T], ALU.add))
                dve.tensor_copy(A["delta"][:, 0:HEADS], prm("rel_bias", 0, HEADS))
                link(dve.tensor_tensor(A["delta"][:, HEADS:], prm("rel_bias", HEADS, 31 * HEADS),
                                       prm("rel_bias", 0, 31 * HEADS), ALU.subtract))
                link(dve.memset(wide[:, 24 * T:32 * T], 0.0))
                for hd in range(HEADS):
                    v = flat(wbias[:, hd])
                    ins = dve.tensor_scalar(v, v, A["delta"][:, hd:hd + 1], None, ALU.add)
                link(ins)

            thresholds = bucket_thresholds()
            steps = iter(range(1, N_BUCKETS))

            def bias_steps(n):
                for _ in range(n):
                    b = next(steps, None)
                    if b is None:
                        return
                    reached = scratch[:, 6 + b % 2, :]
                    link(dve.tensor_scalar(reached, flat(A["away"]), float(thresholds[b - 1]), None, ALU.is_ge))
                    for hd in range(HEADS):
                        v = flat(wbias[:, hd])
                        ins = dve.scalar_tensor_tensor(out=v, in0=reached, scalar=A["delta"][:, b * HEADS + hd:b * HEADS + hd + 1],
                                                       in1=v, op0=ALU.mult, op1=ALU.add)
                    link(ins)

            def rotate(bank, dst, kind, fill, *key):
                tmp = smax[:, 2, 0:T]
                dve.tensor_tensor(dst, bank[:, 0:T], A["cos"], ALU.mult)
                link(dve.tensor_tensor(tmp, bank[:, T:2 * T], A["sin"], ALU.mult))
                n = S.give(dve.tensor_tensor(dst, dst, tmp, ALU.add), kind, *key)
                read(kind, n, *fill)
                dve.wait_ge(S.sem(kind), n)

            conv_at = {}

            def conv_taps(l, n):
                i = conv_at.setdefault(l, 0)
                for i in range(i, min(i + n, TAPS * CT)):
                    tap, j = i // CT, i % CT
                    acc = A["conv"][:, j, :]
                    src = A["u"][:, j, tap:tap + T]
                    w = A["halfw"][:, j * TAPS + tap:j * TAPS + tap + 1]
                    if tap == 0:
                        ins = dve.tensor_scalar(acc, src, w, prm("b_dw", l * CT + j), ALU.mult, ALU.add)
                    else:
                        dve.wait_ge(S.sem("conv_tap"), S.count["conv_tap"] - 3)
                        ins = dve.scalar_tensor_tensor(out=acc, in0=src, scalar=w, in1=acc, op0=ALU.mult, op1=ALU.add)
                    S.give(ins, "conv_tap")
                    conv_at[l] = i + 1
                if conv_at[l] == TAPS * CT and n:
                    conv_at[l] = TAPS * CT
                    S.note(("conv_done", l), "conv_tap", S.count["conv_tap"])

            def scores(l, u):
                bank = take(dve, "s", l, u)
                if u >= 4:
                    S.wait(dve, "filled", "t", l, u - 4)
                st = 48 + u % 4 * 8
                s = smax[:, u % 4, :]
                if u < HEADS:
                    scale = float(NOPE + ROPE) ** -0.5
                    dve.scalar_tensor_tensor(out=s[:, 0:P], in0=bank[:, 0:P], scalar=scale, in1=cst("mask_cur"),
                                             op0=ALU.mult, op1=ALU.add)
                    dve.tensor_scalar(s[:, P:T], bank[:, P:T], scale, None, ALU.mult)
                    ins = dve.scalar_tensor_tensor(out=s[:, T:3 * P], in0=bank[:, T:3 * P], scalar=scale,
                                                   in1=cst("mask_cur"), op0=ALU.mult, op1=ALU.add)
                    n = S.give(ins, "dve_read")
                    read("dve_read", n, "s", l, u)
                    dve.wait_ge(S.sem("dve_read"), n)
                else:
                    hd = sink_of(u)
                    scale = float(HD) ** -0.5
                    dve.scalar_tensor_tensor(out=s[:, 0:P], in0=bank[:, 0:P], scalar=scale, in1=wbias[:, hd, 0, :],
                                             op0=ALU.mult, op1=ALU.add)
                    dve.scalar_tensor_tensor(out=s[:, P:T], in0=bank[:, P:T], scalar=scale, in1=wbias[:, hd, 1, :],
                                             op0=ALU.mult, op1=ALU.add)
                    ins = dve.scalar_tensor_tensor(out=s[:, T:3 * P], in0=bank[:, T:3 * P], scalar=scale,
                                                   in1=wbias[:, hd, 1, :], op0=ALU.mult, op1=ALU.add)
                    n = S.give(ins, "dve_read")
                    read("dve_read", n, "s", l, u)
                    dve.wait_ge(S.sem("dve_read"), n)
                    dve.tensor_tensor(s[:, 0:P], s[:, 0:P], cst("mask_cur"), ALU.add)
                    dve.tensor_tensor(s[:, P:T], s[:, P:T], cst("mask_prev"), ALU.add)
                    link(dve.tensor_tensor(s[:, T:3 * P], s[:, T:3 * P], cst("mask_cur"), ALU.add))
                dve.tensor_reduce(small[:, st:st + 1], s[:, 0:P], AX.X, ALU.max)
                link(dve.tensor_reduce(small[:, st + 1:st + 2], s[:, P:3 * P], AX.X, ALU.max))
                if u < HEADS:
                    ins = dve.tensor_scalar(small[:, st:st + 2], small[:, st:st + 2], -1.0, None, ALU.mult)
                else:
                    ins = dve.tensor_scalar(small[:, st:st + 2], small[:, st:st + 2], prm("sinks", l * HEADS + sink_of(u)),
                                            -1.0, ALU.max, ALU.mult)
                S.give(ins, "row_max", l, u)

            def normalise(l, u):
                st = 48 + u % 4 * 8
                S.wait(dve, "exps", l, u)
                if l != "na" and u >= HEADS:
                    link(dve.tensor_tensor(small[:, st + 2:st + 4], small[:, st + 2:st + 4], small[:, st + 4:st + 6], ALU.add))
                n = 1 if l == "na" else 2
                link(dve.reciprocal(small[:, st + 2:st + 2 + n], small[:, st + 2:st + 2 + n]))
                p = smax[:, u % 4, :]
                if l == "na":
                    ins = dve.tensor_scalar(p, p, small[:, st + 2:st + 3], None, ALU.mult)
                else:
                    dve.tensor_scalar(p[:, 0:P], p[:, 0:P], small[:, st + 2:st + 3], None, ALU.mult)
                    ins = dve.tensor_scalar(p[:, P:3 * P], p[:, P:3 * P], small[:, st + 3:st + 4], None, ALU.mult)
                S.give(ins, "probs", l, u)

            def mix_in(l, n, first, last):
                for i in range(4):
                    bank = take(dve, "branch", l, n, i)
                    S.wait(dve, "gates_ready", l, 21)
                    g = flat(gates[:, 8 * n + 2 * i:8 * n + 2 * i + 2, :])
                    dst = flat(h[:, 2 * i:2 * i + 2, :])
                    if first:
                        done(dve.scalar_tensor_tensor(out=dst, in0=g, scalar=1.0, in1=bank[:, :], op0=ALU.add, op1=ALU.mult),
                             "branch", l, n, i)
                    else:
                        tmp = smax[:, 2 * (i % 2), :]
                        m = S.give(dve.scalar_tensor_tensor(out=tmp, in0=g, scalar=1.0, in1=bank[:, :], op0=ALU.add,
                                                            op1=ALU.mult), "dve_read")
                        read("dve_read", m, "branch", l, n, i)
                        dve.wait_ge(S.sem("dve_read"), m)
                        ins = dve.tensor_tensor(dst, dst, tmp, ALU.add)
                        if last and i == 3:
                            S.give(ins, "mixed", l)

            def centre(tag, src, tiles, n, fill):
                bank = take(dve, *fill)
                for k in range(tiles):
                    ins = dve.scalar_tensor_tensor(out=src[:, k, :], in0=bank[:, 0:T], scalar=-1.0 / n, in1=src[:, k, :],
                                                   op0=ALU.mult, op1=ALU.add)
                m = S.give(ins, "dve_read")
                read("dve_read", m, *fill)
                dve.wait_ge(S.sem("dve_read"), m)
                squares(src, tag, tiles)

            def keep_mod(l, c):
                S.wait(dve, "mod_turned", l, c)
                b = prm("b_mod", 48 * l + 4 * c, 4).unsqueeze(2).to_broadcast([P, 4, 2])
                v = sums[2][:, 0:8].rearrange("p (t c) -> p t c", c=2)
                S.give(dve.tensor_tensor(mod[l][:, 4 * c:4 * c + 4, :], v, b, ALU.add), "mod_kept", l, c)

            def block_1(l):
                rms(("mix", l), lambda k: ("g_mix", l * KT + k), h, "h_ready")
                if l == 0:
                    dve.wait_ge(S.sem("consts_landed"), 16)
                    first_steps()
                link(dve.tensor_scalar(A["halfw"], prm("w_dw", l * CT * TAPS, CT * TAPS), 0.5, None, ALU.mult))
                if l == 0:
                    bias_steps(8)
                rotate(take(dve, "in", l, 5), A["kp"], "key_rotated", ("in", l, 5), l)
                if l == 0:
                    S.wait(dve, "pad_zeroed", "conv")
                for j in range(CT):
                    bank = take(dve, "in", l, 6 + j)
                    S.wait(dve, "glu_tanh", l, j)
                    ins = dve.scalar_tensor_tensor(out=A["u"][:, j, 30:], in0=smax[:, 0, (j % 2) * T:(j % 2 + 1) * T],
                                                   scalar=1.0, in1=bank[:, 0:T], op0=ALU.add, op1=ALU.mult)
                    read("glu", S.give(ins, "glu", l, j), "in", l, 6 + j)
                    if l == 0 and j < CT - 1:
                        bias_steps(2)
                S.wait(dve, "glu", l, 3)
                bank = take(dve, "sum", "latent", l)
                dve.tensor_scalar(stat[:, 0, 0:T], bank[:, 0:T], 1.0 / QR, EPS, ALU.mult, ALU.add)
                ins = dve.tensor_scalar(stat[:, 0, T:2 * T], bank[:, T:2 * T], 1.0 / KVR, EPS, ALU.mult, ALU.add)
                read("variance", S.give(ins, "variance", "latent", l), "sum", "latent", l)
                inverse_root(("latent", l), 512)
                for k in range(2):
                    dve.scalar_tensor_tensor(out=A["cq"][:, k, :], in0=A["cq"][:, k, :], scalar=prm("g_q", 2 * l + k),
                                             in1=stat[:, 1, 0:T], op0=ALU.mult, op1=ALU.mult)
                ins = dve.scalar_tensor_tensor(out=A["ckv"], in0=A["ckv"], scalar=prm("g_kv", l),
                                               in1=stat[:, 1, T:2 * T], op0=ALU.mult, op1=ALU.mult)
                S.give(ins, "latent_normed", l)
                if l == 0:
                    bias_steps(4)
                for i in range(2):
                    rotate(take(dve, "qp", l, i), A["qp"][:, i, :],
                           "latent_rotated", ("qp", l, i), *((l,) if i else (l, "first")))
                for u in range(2 * HEADS + 1):
                    if u < 2 * HEADS:
                        if l == 0 and u == HEADS:
                            bias_steps(N_BUCKETS)
                        scores(l, u)
                    if u >= 1:
                        normalise(l, u - 1)
                    if u in MOD_UNITS and u > 1:
                        keep_mod(l, MOD_UNITS[u] - 1)
                    if l == 0 and u < HEADS:
                        bias_steps(2)
                    conv_taps(l, 4 if l == 0 and u < HEADS else 12)
                conv_taps(l, TAPS * CT)
                keep_mod(l, 8)
                mix_in(l, 0, True, False)
                centre(("conv", l), A["conv"], CT, 512, ("sum", "conv", l))
                keep_mod(l, 9)
                mix_in(l, 2, False, False)
                variance(("conv", l), 512, EPS, ("sum2", "conv", l))
                inverse_root(("conv", l))
                for j in range(CT):
                    ins = dve.tensor_tensor(scratch[:, j, :], A["conv"][:, j, :], stat[:, 1, 0:T], ALU.mult)
                    S.give(ins, "conv_normed", l, j)
                keep_mod(l, 10)
                mix_in(l, 1, False, True)
                for i in range(4):
                    bank = take(dve, "out", l, i)
                    dst = flat(x[:, 2 * i:2 * i + 2, :])
                    ins = dve.scalar_tensor_tensor(out=dst, in0=bank[:, :], scalar=0.5, in1=dst, op0=ALU.mult, op1=ALU.add)
                    n = S.give(ins, "x_added", l, "out", i)
                    read("x_added", n, "out", l, i)
                keep_mod(l, 11)
                dve.wait_ge(S.sem("x_added"), n)
                tag = ("mlp", l)
                squares(x, tag)
                variance(tag, D, EPS, ("sum", *tag))
                inverse_root(tag)
                for k in range(KT):
                    ins = dve.scalar_tensor_tensor(out=scratch[:, k, :], in0=x[:, k, :], scalar=prm("g_mlp", l * KT + k),
                                                   in1=stat[:, 1, 0:T], op0=ALU.mult, op1=ALU.mult)
                    if k % 2 == 1:
                        S.give(ins, "h_whole", l, k // 2)
                for i in range(4):
                    S.wait(dve, "h_high", l, i)
                    v = flat(scratch[:, 2 * i:2 * i + 2, :])
                    ins = dve.tensor_tensor(flat(split["scratch"][:, 2 * i:2 * i + 2, :]), v,
                                            flat(split["h"][:, 2 * i:2 * i + 2, :]).bitcast(F32), ALU.subtract)
                S.give(ins, "h_ready", *tag)
                n0 = chunk_mlp(l)
                rb, hb = S.of("relued_base", l)[1], S.base("mlp_hidden")
                wb, lb = S.of("mlp_high_base", l)[1], S.base("mlp_low")
                S.note(("mlp_hidden_base", l), "mlp_hidden", hb)
                S.note(("mlp_low_base", l), "mlp_low", lb)
                square_base = S.base("mlp_square")

                def low(i, j, part):
                    slot = (n0 + j) % RING
                    dve.wait_ge(S.sem("mlp_high"), i * 8 + (wb + 2 * j + part + 1))
                    v = ring[:, slot, 2048 * part:2048 * part + 2048]
                    dve.tensor_tensor(split["ring"][:, slot, 2048 * part:2048 * part + 2048], v,
                                      HI[("up", "down")[part]][:, j % 2, :].bitcast(F32), ALU.subtract)\
                       .then_inc(S.sem("mlp_low"), 1)

                def step(i, last=False):
                    for j in range(4):
                        final = last and j == 3
                        if not final:
                            low(i, j + 1, 0)
                        v, hi = hid[:, j % 2, :], split["smax"][:, 2 + j % 2, :]
                        dve.wait_ge(S.sem("relued"), i * 4 + (rb + j + 1))
                        dve.tensor_tensor(v, v, v, ALU.mult).then_inc(S.sem("mlp_square"), 1)
                        dve.wait_ge(S.sem("mlp_square"), i * 8 + (square_base + 2 * j + 1))
                        dve.tensor_copy(hi, v).then_inc(S.sem("mlp_square"), 1)
                        dve.wait_ge(S.sem("mlp_square"), i * 8 + (square_base + 2 * j + 2))
                        dve.tensor_tensor(split["smax"][:, 4 + j % 2, :], v, hi.bitcast(F32), ALU.subtract).then_inc(S.sem("mlp_hidden"), 1)
                        if not final:
                            low(i, j + 1, 1)

                low(0, 0, 0)
                low(0, 0, 1)
                with dve.Fori(0, MLP_CHUNKS // 4 - 1) as i:
                    step(i)
                step(MLP_CHUNKS // 4 - 1, last=True)
                S.base("mlp_low", lb + 2 * MLP_CHUNKS)
                S.base("mlp_square", square_base + 2 * MLP_CHUNKS)
                S.base("mlp_hidden", hb + MLP_CHUNKS)
                S.wait(dve, "mlp_summed", l)
                for b in range(4):
                    dst = flat(x[:, 2 * b:2 * b + 2, :])
                    ins = dve.tensor_tensor(dst, dst, sums[b][:, :], ALU.add)
                give_link(ins, "x_added", l, "mlp")

            for l in range(LAYERS):
                block_1(l)

            def modv(i, j, k, c=0):
                return mod[i][:, 8 * j + k, c:c + 1]

            def modulate(dst, src, i, shift, scale, c=0):
                for k in range(KT):
                    ins = dve.tensor_scalar(dst[:, k, :], src[:, k, :], modv(i, scale, k, c), modv(i, shift, k, c),
                                            ALU.mult, ALU.add)
                return ins

            for i in range(2):
                for j in (1, 4):
                    ins = dve.tensor_scalar(mod[i][:, 8 * j:8 * j + 8, :], mod[i][:, 8 * j:8 * j + 8, :], 1.0, None, ALU.add)
            link(ins)
            rms(("final",), lambda k: ("g_final", k), x, "x_normed")
            S.wait(dve, "x_normed", "final")
            S.give(modulate(h, x, 0, 0, 1), "h_ready", "mod", 0, 0)
            dve.wait_ge(S.sem("ctx_landed"), 16)
            S.give(modulate(scratch, scratch, 0, 0, 1, 1), "ctx_modulated", 0)
            dve.wait_ge(S.sem("consts2_landed"), 16)
            for hd in range(RET):
                link(dve.tensor_scalar(W2["decay"][:, hd, :], cst2("dist_f"), loggam[:, hd:hd + 1], None, ALU.mult))
                S.give(dve.scalar_tensor_tensor(out=W2["decay"][:, hd, :], in0=cst2("dist_b"),
                                                scalar=loggam[:, 4 + hd:5 + hd], in1=W2["decay"][:, hd, :],
                                                op0=ALU.mult, op1=ALU.add), "exponent", hd)
            for hd in range(RET):
                S.wait(dve, "decay_exps", hd)
                ins = dve.tensor_tensor(W2["decay"][:, hd, :], W2["decay"][:, hd, :], cst2("diag"), ALU.mult)
            link(ins)
            dve.wait_ge(S.sem("na_bias_landed"), 16)
            nb = W2["nbias"].rearrange("p h (e c) -> p (h e) c", c=GRID)
            m = cst("na_mask").unsqueeze(1).to_broadcast([P, 48, GRID])
            link(dve.tensor_tensor(nb, nb, m, ALU.add))
            for which in ("rk", "rq"):
                for i in range(2):
                    bank = take(dve, "swap", which, i)
                    src = B[which][:, 2 * i:2 * i + 2, :]
                    cos = cst2("axial_cos").unsqueeze(1).to_broadcast([P, 2, T])
                    sin = cst2("axial_sin").unsqueeze(1).to_broadcast([P, 2, T])
                    tmp = smax[:, 5, :].rearrange("p (a b) -> p a b", a=2)
                    m = S.give(dve.tensor_tensor(tmp, bank[:, :].rearrange("p (a b) -> p a b", a=2), sin, ALU.mult), "dve_read")
                    read("dve_read", m, "swap", which, i)
                    ins = dve.tensor_tensor(src, src, cos, ALU.mult)
                    link(ins)
                    give_link(dve.tensor_tensor(src, src, tmp, ALU.add), "rotated", which, i)
            S.wait(dve, "key_decays", 0)
            for d in range(2):
                for hd in range(RET):
                    S.wait(dve, "projected", "rvc", 1)
                    u = 4 * d + hd
                    if u >= 6:
                        S.wait(dve, "state_done", 0, u - 6)
                    kd = smax[:, u % 6, 0:2 * P].rearrange("p (t c) -> p t c", t=2)
                    for t in range(2):
                        ins = dve.tensor_scalar(kd[:, t, :], B["rkc"][:, t, hd * P:(hd + 1) * P],
                                                small[:, 96 + 2 * u + t:97 + 2 * u + t], None, ALU.mult)
                    S.give(ins, "keys_decayed", d, hd)
            S.wait(dve, "query_decays", 0)
            for d in range(2):
                for hd in range(RET):
                    v = W2["qd"][:, 4 * d + hd, :]
                    ins = dve.tensor_tensor(v, v, B["rq"][:, hd, :], ALU.mult)
            S.give(ins, "queries_decayed", 0)
            S.wait(dve, "filled", "state", 1)
            for hd in range(RET):
                bank = take(dve, "att", hd)
                at = smax[:, 2 + hd, :]
                dve.tensor_tensor(at[:, 0:T], bank[:, 0:T], W2["decay"][:, hd, P:3 * P], ALU.mult)
                ins = dve.tensor_tensor(at[:, T:2 * T], bank[:, T:2 * T], W2["decay"][:, hd, 0:T], ALU.mult)
                read("att_decayed", S.give(ins, "att_decayed", hd), "att", hd)
            o = B["rkc"].rearrange("p a (b t) -> p (a b) t", b=2)
            for i in range(2):
                bank = take(dve, "sum", "head", i)
                v = flat(o[:, 2 * i:2 * i + 2, :])
                ins = dve.scalar_tensor_tensor(out=v, in0=bank[:, :], scalar=-1.0 / P, in1=v, op0=ALU.mult, op1=ALU.add)
                m = S.give(ins, "dve_read")
                read("dve_read", m, "sum", "head", i)
                dve.wait_ge(S.sem("dve_read"), m)
                S.give(dve.tensor_tensor(flat(scratch[:, 2 * i:2 * i + 2, :]), v, v, ALU.mult), "squares", "head", i)
            for i in range(2):
                bank = take(dve, "sum2", "head", i)
                ins = dve.tensor_scalar(smax[:, 2 + i, :], bank[:, :], 1.0 / P, LN_EPS, ALU.mult, ALU.add)
                read("variance", S.give(ins, "variance", "head", i), "sum2", "head", i)
            for i in range(2):
                S.wait(dve, "root", "head", i)
                v, r = flat(o[:, 2 * i:2 * i + 2, :]), smax[:, 2 + i, :]
                link(dve.reciprocal(r, r))
                link(dve.tensor_tensor(v, v, r, ALU.mult))
                S.wait(dve, "projected", "rg", i)
                g = flat(B["rg"][:, 2 * i:2 * i + 2, :])
                ins = dve.tensor_tensor(g, g, v, ALU.mult)
            S.give(ins, "ret_ready", 0)
            for u in range(16 + 1):
                if u < 16:
                    hd, t = u // 2, u % 2
                    bank = take(dve, "s", "na", u)
                    if u >= 4:
                        S.wait(dve, "filled", "t", "na", u - 4)
                    st = 48 + u % 4 * 8
                    s = smax[:, u % 4, :]
                    e0 = 2 - 2 * t
                    dve.scalar_tensor_tensor(out=s[:, 0:T], in0=bank[:, 0:T], scalar=float(HD) ** -0.5,
                                             in1=W2["nbias"][:, hd, e0 * GRID:(e0 + 4) * GRID], op0=ALU.mult, op1=ALU.add)
                    ins = dve.tensor_scalar(s[:, T:2 * T], bank[:, T:2 * T], float(HD) ** -0.5, None, ALU.mult)
                    m = S.give(ins, "dve_read")
                    read("dve_read", m, "s", "na", u)
                    dve.wait_ge(S.sem("dve_read"), m)
                    link(dve.tensor_reduce(small[:, st:st + 1], s, AX.X, ALU.max))
                    S.give(dve.tensor_scalar(small[:, st:st + 1], small[:, st:st + 1], -1.0, None, ALU.mult), "row_max", "na", u)
                if u >= 1:
                    normalise("na", u - 1)

            def post_norm(i, s):
                tag = ("post", i, s)
                centre(tag, x, KT, D, ("sum", *tag))
                variance(tag, D, LN_EPS, ("sum2", *tag))
                inverse_root(tag)
                for k in range(KT):
                    ins = dve.scalar_tensor_tensor(out=x[:, k, :], in0=x[:, k, :], scalar=prm("ln_g", (2 * i + s) * KT + k),
                                                   in1=stat[:, 1, 0:T], op0=ALU.mult, op1=ALU.mult)
                link(ins)
                for k in range(KT):
                    ins = dve.tensor_scalar(x[:, k, :], x[:, k, :], prm("ln_b", (2 * i + s) * KT + k), None, ALU.add)
                give_link(ins, "x_normed", *tag)

            def scale_x():
                v = flat(x[:, :, :])
                link(dve.tensor_scalar(v, v, float(ALPHA), None, ALU.mult))

            def residual(i, s, j, bank_for, kind, gate=None):
                for b in range(4):
                    bank, fill = bank_for(b)
                    for q in range(2):
                        k = 2 * b + q
                        g = gate(k) if gate else modv(i, j, k)
                        ins = dve.scalar_tensor_tensor(out=x[:, k, :], in0=bank[:, q * T:(q + 1) * T], scalar=g,
                                                       in1=x[:, k, :], op0=ALU.mult, op1=ALU.add)
                    if b == 3:
                        n = S.give(ins, "added", i, s)
                        kind = "added"
                    else:
                        n = S.give(ins, "dve_read")
                        kind = "dve_read"
                    if fill:
                        read(kind, n, *fill)
                dve.wait_ge(S.sem("added"), S.count["added"])

            scale_x()

            def ab_bank(b):
                fill = ("ab_out", b)
                return take(dve, *fill), fill

            residual(0, 0, 2, ab_bank, None)
            post_norm(0, 0)

            def one_hot(dst, vals, top, rank, tmp, tmp1, n):
                link(dve.tensor_reduce(top, vals, AX.X, ALU.max))
                link(dve.tensor_tensor(tmp, vals, top.unsqueeze(2).to_broadcast([P, 2, n]), ALU.is_ge))
                link(dve.tensor_tensor(tmp, tmp, rank, ALU.mult))
                link(dve.tensor_reduce(tmp1, tmp, AX.X, ALU.max))
                link(dve.tensor_tensor(dst, tmp, tmp1.unsqueeze(2).to_broadcast([P, 2, n]), ALU.is_equal))

            def route(i):
                r = smax[:, 2, :]

                def piece(a, *dims):
                    v = r[:, a:a + int(np.prod(dims))]
                    return v.rearrange("p (a b) -> p a b", a=dims[0]) if len(dims) == 2 else v

                lg, tmp4, oh4 = piece(0, 2, 36), piece(72, 2, 4), piece(80, 2, 4)
                m4, c4, gate = piece(88, 2), piece(90, 2), piece(92, 2)
                le, tmp8, oh1, oh2 = piece(96, 2, 8), piece(112, 2, 8), piece(128, 2, 8), piece(144, 2, 8)
                m1, m2, c1, w1, w2 = piece(160, 2), piece(162, 2), piece(164, 2), piece(166, 2), piece(168, 2)
                prod = r[:, 192:256].rearrange("p (t g e) -> p t g e", t=2, g=4)
                bank = take(dve, "router", i)
                for t in range(2):
                    ins = dve.tensor_tensor(lg[:, t, :], bank[:, t * 64:t * 64 + 36], prm("b_router", 36 * i, 36), ALU.add)
                m = S.give(ins, "dve_read")
                read("dve_read", m, "router", i)
                dve.wait_ge(S.sem("dve_read"), m)
                g = lg[:, :, 0:4]
                one_hot(oh4, g, m4, cst("rank4").rearrange("p (a b) -> p a b", a=2), tmp4, c4, GROUPS)
                S.give(dve.tensor_tensor(small[:, 0:8].rearrange("p (a b) -> p a b", a=2), g,
                                         m4.unsqueeze(2).to_broadcast([P, 2, 4]), ALU.subtract), "router_shifted", i)
                for t in range(2):
                    ins = dve.tensor_tensor(prod[:, t], lg[:, t, 4:36].rearrange("p (g e) -> p g e", g=4),
                                            oh4[:, t].unsqueeze(2).to_broadcast([P, 4, 8]), ALU.mult)
                link(ins)
                link(dve.tensor_reduce(le, prod.rearrange("p t g e -> p t e g"), AX.X, ALU.add))
                rank8 = cst("rank8").rearrange("p (a b) -> p a b", a=2)
                one_hot(oh1, le, m1, rank8, tmp8, c1, PER_GROUP)
                link(dve.scalar_tensor_tensor(out=le, in0=oh1, scalar=-3e38, in1=le, op0=ALU.mult, op1=ALU.add))
                one_hot(oh2, le, m2, rank8, tmp8, c1, PER_GROUP)
                S.give(dve.tensor_tensor(small[:, 8:10], m2, m1, ALU.subtract), "top_shifted", i)
                link(dve.tensor_tensor(tmp8, oh1, oh2, ALU.add))
                by_group = "p (g e) -> p g e"
                for t in range(2):
                    ins = dve.tensor_tensor(member[:, t, :].rearrange(by_group, g=4),
                                            tmp8[:, t].unsqueeze(1).to_broadcast([P, 4, 8]),
                                            oh4[:, t].unsqueeze(2).to_broadcast([P, 4, 8]), ALU.mult)
                give_link(ins, "members", i)
                S.wait(dve, "router_exps", i)
                link(dve.tensor_reduce(gate, small[:, 0:8].rearrange("p (a b) -> p a b", a=2), AX.X, ALU.add))
                S.wait(dve, "top_exps", i)
                link(dve.tensor_scalar(w1, small[:, 8:10], 1.0, None, ALU.add))
                link(dve.tensor_tensor(w1, w1, gate, ALU.mult))
                link(dve.reciprocal(w1, w1))
                link(dve.tensor_tensor(w2, w1, small[:, 8:10], ALU.mult))
                link(dve.tensor_tensor(oh1, oh1, w1.unsqueeze(2).to_broadcast([P, 2, 8]), ALU.mult))
                link(dve.tensor_tensor(oh2, oh2, w2.unsqueeze(2).to_broadcast([P, 2, 8]), ALU.mult))
                link(dve.tensor_tensor(oh1, oh1, oh2, ALU.add))
                for t in range(2):
                    ins = dve.tensor_tensor(weight_of[:, t, :].rearrange(by_group, g=4),
                                            oh1[:, t].unsqueeze(1).to_broadcast([P, 4, 8]),
                                            oh4[:, t].unsqueeze(2).to_broadcast([P, 4, 8]), ALU.mult)
                link(ins)
                bank = take(dve, "rank", i)
                dve.scalar_tensor_tensor(out=flat2(rank), in0=bank[:, 0:64], scalar=1.0, in1=flat2(member),
                                         op0=ALU.add, op1=ALU.mult)
                fullest, more = small[:, 10:11], small[:, 12:14]
                n = S.give(dve.tensor_reduce(fullest, bank[:, 64:96], AX.X, ALU.max), "dve_read")
                read("dve_read", n, "rank", i)
                dve.wait_ge(S.sem("dve_read"), n)
                link(dve.tensor_scalar(flat2(rank), flat2(rank), -1.0, None, ALU.add))
                link(dve.tensor_scalar(small[:, 16:16 + MAX_ROUNDS], cst("full"), fullest, None, ALU.is_lt))
                link(dve.tensor_reduce(more[:, 0:1], small[:, 16:16 + MAX_ROUNDS], AX.X, ALU.add))
                link(dve.tensor_scalar(more[:, 0:1], more[:, 0:1], 1.0, None, ALU.max))
                link(dve.tensor_scalar(more[:, 1:2], more[:, 0:1], -1.0, None, ALU.add))
                give_link(dve.tensor_copy(rounds_i[:, :], more), "rounds", i)

            def moe(i):
                give_link(modulate(h, x, i, 3, 4), "h_ready", "mod", i, 1)
                scale_x()
                route(i)
                with dve.Fori(0, rounds_of(dve, i)) as rnd:
                    with dve.Fori(0, TURNS) as g:
                        it = rnd * TURNS + g
                        four = [P, GROUP_OF, SLOTS]
                        for t in range(2):
                            ranks = rank[:, t, bass.ds(g * 4, 4)].unsqueeze(2).to_broadcast(four)
                            ins = dve.tensor_tensor(M["place"][:, t, :].rearrange("p (e s) -> p e s", e=GROUP_OF),
                                                    cst("slot_no").unsqueeze(1).to_broadcast(four), ranks, ALU.is_equal)
                        ins.then_inc(S.sem(f"moe{i}_placed"), 1)
                        dve.wait_ge(S.sem(f"moe{i}_placed"), it + 1)
                        twice = [P, GROUP_OF, 2, SLOTS]
                        for t in range(2):
                            w = weight_of[:, t, bass.ds(g * 4, 4)].unsqueeze(2).unsqueeze(3).to_broadcast(twice)
                            place = M["place"][:, t, :].rearrange("p (e s) -> p e s", e=GROUP_OF).unsqueeze(2)
                            dve.tensor_tensor(M["weighted"][:, t, :].rearrange("p (e a s) -> p e a s", e=GROUP_OF, a=2),
                                              place.to_broadcast(twice), w, ALU.mult)
                        for e in range(GROUP_OF):
                            dve.wait_ge(S.sem(f"moe{i}_silued"), it * 4 + (e + 1))
                            dve.tensor_tensor(M["hidden"], banks[0][:, T:2 * T], M["silu"], ALU.mult)\
                               .then_inc(S.sem(f"moe{i}_hidden"), 1)
                            dve.wait_ge(S.sem(f"moe{i}_down_done"), it * 4 + (e + 3))
                            dve.tensor_copy(M["y"], banks[2][:, :]).then_inc(S.sem(f"moe{i}_y_kept"), 1)
                    dve.tensor_scalar(flat2(rank), flat2(rank), -float(SLOTS), None, ALU.add)\
                       .then_inc(S.sem(f"moe{i}_ranks_left"), 1)
                    dve.wait_ge(S.sem(f"moe{i}_ranks_left"), rnd + 1)
                S.wait(dve, "moe_summed", i)
                residual(i, 1, 5, lambda b: (sums[b], None), None)
                post_norm(i, 1)

            moe(0)
            give_link(modulate(h, x, 1, 0, 1), "h_ready", "mod", 1, 0)
            S.wait(dve, "pad_zeroed", "pool")
            dve.wait_ge(S.sem("counts_landed"), 16)
            pad = PL["pad"][:, 0, :]
            for k in range(KT):
                g = k // 2
                link(dve.tensor_copy(pad[:, 8:8 + T], h[:, k, :]))
                cur, at, left, right = pad, 8, 1, 0
                lo, hi = 0, T + 16
                for level in range(g + 1):
                    half = POOL_SIZES[level] // 2
                    left, right = (1, 0) if level == 0 else (half // 2, half // 2)
                    nxt = PL["lvl"][:, level % 2, :]
                    lo, hi = lo + left, hi - right
                    link(dve.tensor_tensor(nxt[:, lo:hi], cur[:, lo - left:hi - left], cur[:, lo + right:hi + right], ALU.add))
                    cur = nxt
                link(dve.tensor_tensor(cur[:, 8:8 + T], cur[:, 8:8 + T], PL["counts"][:, g, :], ALU.mult))
                ins = dve.tensor_tensor(PL["z"][:, k, :], cur[:, 8:8 + T], h[:, k, :], ALU.subtract)
                if k % 2 == 1:
                    S.give(ins, "pooled", g)
            for k in range(KT):
                ins = dve.tensor_tensor(small[:, 8 + k:9 + k], prm("pool_scale", k), modv(1, 2, k), ALU.mult)
            link(ins)

            scale_x()

            def pool_bank(b):
                fill = ("pool", b)
                return take(dve, *fill), fill

            residual(1, 0, 2, pool_bank, None, gate=lambda k: small[:, 8 + k:9 + k])
            post_norm(1, 0)
            moe(1)
    return S


def sink_of(u):
    j = u - HEADS
    return j // 2 + 4 * (j % 2)


def by_partition(w):
    return w.reshape(w.shape[0] // P, P, w.shape[1]).transpose(1, 0, 2)


def pack_weights(a):
    out = np.zeros((N_CHUNKS, P, CW), np.float32)

    def put(n, v, at=0):
        v = v.reshape(P, -1)
        out[n, :, at:at + v.shape[1]] = v

    r = np.arange
    for l in range(LAYERS):
        w = by_partition(a["w_in"][l])
        pe = 2176 + r(32)
        tiles = []
        for j in range(4):
            tiles.append(np.concatenate([j * 64 + r(64), (j + 4) * 64 + r(64)]))
        tiles += [512 + r(128), 640 + r(128), 1792 + r(128), 1920 + r(128), 2048 + r(128), None,
                  np.tile(pe, 4), np.tile(np.concatenate([pe[16:], pe[:16]]), 4)]
        for j in range(4):
            tiles += [768 + 128 * j + r(128), 1280 + 128 * j + r(128)]
        tiles += [2208 + 128 * j + r(128) for j in range(24)]
        for i, cols in enumerate(tiles):
            if cols is not None:
                v = out[chunk_in(l, i // 2)].reshape(P, KT, 512)
                v[:, :, (i % 4) * P:(i % 4 + 1) * P] = w[:, :, cols]
        q = by_partition(a["w_q_up"][l]).reshape(P, 2, HEADS, NOPE + ROPE)
        qr = q[:, :, (0, 2, 1, 3, 4, 6, 5, 7), NOPE:]
        q = np.concatenate([q[..., :NOPE].reshape(P, 2, 512), qr.reshape(P, 2, 256),
                            np.concatenate([qr[..., 16:], qr[..., :16]], -1).reshape(P, 2, 256)], axis=2)
        kv = a["w_kv_up"][l].reshape(P, HEADS, 128)
        put(chunk_of(l, "latent"), q)
        put(chunk_of(l, "latent"), kv[..., :64], 2048)
        put(chunk_of(l, "latent"), kv[..., 64:], 2560)
        for n in range(3):
            w = a["w_branch"][l, n]
            if n == 0:
                w = w[np.concatenate(tiles[:4])]
            put(chunk_of(l, "branch", BRANCH_ORDER.index(n)), by_partition(w))
        w = by_partition(a["w_out"][l])
        for half in range(2):
            put(chunk_of(l, "out", half), w[:, :, 512 * half:512 * half + 512])
        up, down = by_partition(a["w_up"][l]), by_partition(a["w_down"][l])
        for c in range(MLP_CHUNKS):
            put(chunk_mlp(l) + c, up[:, :, 256 * c:256 * c + 256])
            put(chunk_mlp(l) + c, down[:, 2 * c:2 * c + 2, :], 2048)
    for i in range(2):
        w = by_partition(a["w_mod_2"][i])
        for c in range(MOD_CHUNKS):
            put(chunk_of(i, "mod", c), w[:, :, 512 * c:512 * c + 512])
    w = by_partition(a["ab_w_in_2"][0])
    order = [0, 512, 1024, 1536, 2048, 2560, 3072]
    for c, at in enumerate(order):
        put(C_AB + c, w[:, :, at:at + 512])
    w = by_partition(a["ab_w_out_2"][0])
    for half in range(2):
        put(C_ABOUT + half, w[:, :, 512 * half:512 * half + 512])
    put(C_POOL, a["pool_w_2"][0].reshape(4, 2, P, 256).transpose(2, 0, 1, 3))
    return out


def pack_experts(a):
    out = np.empty((2, EXPERTS, EXPERT_CHUNKS, P, CW), np.float32)
    up = out[:, :, 0:2].reshape(2, EXPERTS, 2, P, 4, 2, 2, 256)
    for j, name in enumerate(("moe_w_gate_2", "moe_w_up_2")):
        w = a[name].reshape(2, EXPERTS, 2, 4, P, 2, 256)
        up[:, :, :, :, :, :, j, :] = w.transpose(0, 1, 2, 4, 3, 5, 6)
    out[:, :, 0:2] = up.reshape(2, EXPERTS, 2, P, CW)
    out[:, :, 2] = a["moe_w_down_2"].reshape(2, EXPERTS, 4, P, D).transpose(0, 1, 3, 2, 4).reshape(2, EXPERTS, P, CW)
    return out.reshape(2 * EXPERTS * EXPERT_CHUNKS, P, CW)


def pack_params(a):
    out = np.zeros((P, N_PARAM), np.float32)

    def put(name, v):
        i, j = PARAM[name]
        out[:, i:j] = v

    def cols(v):
        return v.reshape(-1, P).T

    for name, key in (("g_final", "g_final"), ("g_mix", "g_mix"), ("g_mlp", "g_mlp"), ("g_q", "g_q_norm"),
                      ("g_kv", "g_kv_norm"), ("b_dw", "b_dw"), ("g_conv", "g_conv_ln"), ("b_conv", "b_conv_ln"),
                      ("b_mod", "b_mod_2"), ("ln_g", "ln_g_2"), ("ln_b", "ln_b_2"), ("pool_scale", "pool_scale_2")):
        put(name, cols(a[key]))
    put("w_dw", a["w_dw"][:, :, 0, :].reshape(2, TAPS, CT, P).transpose(3, 0, 2, 1).reshape(P, -1))
    cond = np.stack([cols(a["c_2"][0]), cols(a["c_ctx_2"])], axis=2)
    put("cond", cond.reshape(P, -1))
    for name, key in (("sinks", "swa_sinks"), ("rel_bias", "rel_bias"), ("log_decay", "ab_log_decay_2")):
        put(name, a[key].reshape(1, -1))
    put("b_router", np.concatenate([a["moe_b_r1_2"], a["moe_b_r2_2"].reshape(2, 32)], axis=1).reshape(1, -1))
    w = np.concatenate([a["moe_w_r1_2"], a["moe_w_r2_2"].transpose(0, 2, 1, 3).reshape(2, D, 32)], axis=2)
    put("w_router", w.reshape(2, KT, P, 36).transpose(2, 0, 1, 3).reshape(P, -1))
    return out


def pack_neighbour_bias(rpb):
    out = np.zeros((P, HEADS, 6, GRID), np.float32)
    for p in range(P):
        half, qc = p // GRID, p % GRID
        lo, hi = max(0, qc - 15), min(GRID, qc + 16)
        out[p, :, :, lo:hi] = rpb[:, 5 - half:11 - half, lo - qc + 15:hi - qc + 15]
    return out.reshape(P, HEADS, 6 * GRID)


def layout(inputs):
    a = {k: np.asarray(v) for k, v in inputs.items()}
    pos = a["positions"].reshape(T)
    positions = np.concatenate([np.tile(pos[None, :], (P, 1)), pos.reshape(2, P).T], axis=1)
    c, c2, counts = shape_constants()
    return {
        "stream": pack_weights(a),
        "experts": pack_experts(a),
        "tokens": by_partition(a["x"][0].T),
        "ctx_tokens": by_partition(a["ctx_2"][0].T),
        "params": pack_params(a),
        "consts": c,
        "consts2": c2,
        "pool_counts": counts,
        "positions": positions,
        "na_bias": pack_neighbour_bias(a["ab_rpb_2"][0]),
    }


def program(nc, shapes):
    ins = {}
    for name, (shape, dtype) in shapes.items():
        ins[name] = nc.dram_tensor(f"in_{name}", shape, mybir.dt.from_np(dtype), kind="ExternalInput").ap()
    out = nc.dram_tensor("out_x", [P, KT, T], F32, kind="ExternalOutput").ap()
    return ins, out


def kernel(**inputs):
    import concourse.bacc as bacc
    from concourse.bass_utils import run_bass_kernel_spmd

    arrays = {k: np.ascontiguousarray(v) for k, v in layout(inputs).items()}
    shapes = {k: (v.shape, v.dtype) for k, v in arrays.items()}
    counted = {}
    for _ in range(2):
        nc = bacc.Bacc("TRN2", target_bir_lowering=False, num_devices=1)
        ins, out = program(nc, shapes)
        counted = two_blocks_kernel(nc, **ins, out=out, counted=counted).at
    r = run_bass_kernel_spmd(nc, [{f"in_{k}": v for k, v in arrays.items()}], core_ids=[0])
    y = r.results[0]["out_x"]
    return y.transpose(2, 1, 0).reshape(1, T, D)
```
